# Optimizing a Trainium2 kernel written in Bass

```python
import math
import jax
import jax.numpy as jnp
from jax import lax
import numpy as np

D_MODEL = 1024
BATCH = 1
SEQ = 256
DEPTH = 2

HEAD_DIM = 64
MIX_WIDTH = D_MODEL
GROUP_WIDTH = MIX_WIDTH // 2
EPS = 1e-6
NEG = -1e30
ROPE_THETA = 10000.0

HY_CHANNELS = GROUP_WIDTH
HY_ORDER = 2
HY_IN = (HY_ORDER + 1) * HY_CHANNELS
HY_SHORT = 3
HY_EMB = 33
HY_BANDS = (HY_EMB - 1) // 2
HY_FILTER_HIDDEN = 64
HY_FAST_DECAY = 0.3
HY_SLOW_DECAY = 1.5
HY_DECAY_TARGET = 1e-2
HY_MAX_DECAY = math.log(HY_DECAY_TARGET) / HY_FAST_DECAY
HY_MIN_DECAY = math.log(HY_DECAY_TARGET) / HY_SLOW_DECAY
HY_MOD_SHIFT = 0.05

RET_HEADS = GROUP_WIDTH // HEAD_DIM
RET_CHUNK = 128
EVEN_IN = HY_IN + 4 * GROUP_WIDTH

GRID_W = 64
NA_HEADS = GROUP_WIDTH // HEAD_DIM
NA_ROWS = 8
NA_COLS = 16

DIL_HEADS = GROUP_WIDTH // HEAD_DIM
DIL_BRANCHES = ((128, 1), (512, 4), (2048, 16))
ODD_IN = 3 * NA_HEADS * HEAD_DIM + 3 * DIL_HEADS * HEAD_DIM

PEER_HEADS = 8
PEER_KEYS = 128
PEER_EXPERTS = PEER_KEYS * PEER_KEYS
PEER_DK = 128
PEER_TOPK = 16
PEER_BLOCK = 128

N_EVEN = (DEPTH + 1) // 2
N_ODD = DEPTH // 2

kernel_name = 'hybrid_hyena_retnet_natten_dilated_peer'

F32 = jnp.float32

def _rms_norm(x, gain):
    xf = x.astype(F32)
    y = xf * lax.rsqrt(jnp.mean(xf * xf, axis=-1, keepdims=True) + EPS)
    return (y * gain.astype(F32)).astype(x.dtype)

def _head_rms(t, gain):
    t = t.astype(F32)
    return t * lax.rsqrt(jnp.mean(t * t, axis=-1, keepdims=True) + EPS) * gain.astype(F32)

def _rope(t):
    S, hd = t.shape[1], t.shape[-1]
    inv = ROPE_THETA ** (-jnp.arange(0, hd, 2, dtype=F32) / hd)
    ang = jnp.arange(S, dtype=F32)[:, None] * inv[None, :]
    cos = jnp.cos(ang)[None, :, None, :]
    sin = jnp.sin(ang)[None, :, None, :]
    t1, t2 = jnp.split(t.astype(F32), 2, axis=-1)
    return jnp.concatenate([t1 * cos - t2 * sin, t2 * cos + t1 * sin], axis=-1)

def _hyena_filters(L, fw1, fb1, fw2, fb2, fw3, fb3, fw_out, freq):
    t_norm = jnp.linspace(0.0, 1.0, L, dtype=F32)[:, None]
    w = 2.0 * math.pi * jnp.arange(L, dtype=F32)[:, None] / L
    f = jnp.linspace(1e-4, HY_BANDS - 1, HY_BANDS, dtype=F32)[None, :]
    emb = jnp.concatenate([t_norm, jnp.cos(f * w), -jnp.sin(f * w)], axis=-1)
    fr = freq.astype(F32)
    hdn = jnp.sin(fr * (emb @ fw1.astype(F32) + fb1.astype(F32)))
    hdn = jnp.sin(fr * (hdn @ fw2.astype(F32) + fb2.astype(F32)))
    hdn = jnp.sin(fr * (hdn @ fw3.astype(F32) + fb3.astype(F32)))
    filt = (hdn @ fw_out.astype(F32)).reshape(L, HY_ORDER, 2, HY_CHANNELS)
    deltas = jnp.abs(jnp.linspace(HY_MIN_DECAY, HY_MAX_DECAY, HY_CHANNELS, dtype=F32))
    window = jnp.exp(-t_norm * deltas[None, :]) + HY_MOD_SHIFT
    filt = filt * window[:, None, None, :]
    fwd = filt[:, :, 0]
    bwd = filt[:, :, 1]
    circ = jnp.concatenate([fwd, jnp.zeros_like(fwd[:1]), bwd[:0:-1]], axis=0)
    return jnp.fft.rfft(circ, axis=0)

def _fft_long_conv(z, filt_f, skip):
    L = z.shape[1]
    zf = jnp.fft.rfft(z, n=2 * L, axis=1)
    y = jnp.fft.irfft(zf * filt_f[None], n=2 * L, axis=1)[:, :L]
    return y + z * skip.astype(F32)

def _hyena(u, conv_w, conv_b, fw1, fb1, fw2, fb2, fw3, fb3, fw_out, freq, skip):
    L = u.shape[1]
    up = jnp.pad(u, ((0, 0), (1, 1), (0, 0)))
    cw = conv_w.astype(F32)
    uc = up[:, :-2] * cw[0] + up[:, 1:-1] * cw[1] + up[:, 2:] * cw[2] + conv_b.astype(F32)
    v, x1, x2 = jnp.split(uc, 3, axis=-1)
    filt_f = _hyena_filters(L, fw1, fb1, fw2, fb2, fw3, fb3, fw_out, freq)
    z = x1 * _fft_long_conv(v, filt_f[:, 0], skip[0])
    return x2 * _fft_long_conv(z, filt_f[:, 1], skip[1])

def _retention_scan(q, k, v, log_g, strict):
    B, H, S, dk = q.shape
    dv = v.shape[-1]
    C = RET_CHUNK
    n = S // C
    qc = q.reshape(B, H, n, C, dk)
    kc = k.reshape(B, H, n, C, dk)
    vc = v.reshape(B, H, n, C, dv)
    pos = jnp.arange(C, dtype=F32)
    lg = log_g[:, None]
    diff = pos[:, None] - pos[None, :]
    keep = (diff > 0) if strict else (diff >= 0)
    dmat = jnp.where(keep[None], jnp.exp(lg[:, :, None] * jnp.maximum(diff, 0.0)[None]), 0.0)
    scores = jnp.einsum('bhncd,bhnkd->bhnck', qc, kc) * dmat[None, :, None]
    y_intra = jnp.einsum('bhnck,bhnke->bhnce', scores, vc)
    k_dec = jnp.exp(lg * (C - 1 - pos))
    q_dec = jnp.exp(lg * (pos + 1))
    kv = jnp.einsum('bhncd,bhnce->nbhde', kc * k_dec[None, :, None, :, None], vc)
    chunk_decay = jnp.exp(lg[:, 0] * C)[None, :, None, None]

    def step(state, kv_i):
        return state * chunk_decay + kv_i, state

    _, prev = lax.scan(step, jnp.zeros((B, H, dk, dv), F32), kv)
    y_cross = jnp.einsum('bhncd,nbhde->bhnce', qc * q_dec[None, :, None, :, None], prev)
    return (y_intra + y_cross).reshape(B, H, S, dv)

def _retention(r_in, log_decay_param, gn_gain):
    B, S, _ = r_in.shape
    rq, rk, rv, rg = jnp.split(r_in, 4, axis=-1)
    shp = (B, S, RET_HEADS, HEAD_DIM)
    q = _rope(rq.reshape(shp)).transpose(0, 2, 1, 3)
    k = (_rope(rk.reshape(shp)) * HEAD_DIM ** -0.5).transpose(0, 2, 1, 3)
    v = rv.reshape(shp).transpose(0, 2, 1, 3)
    log_g = -jnp.exp(log_decay_param.astype(F32))
    y_fwd = _retention_scan(q, k, v, log_g[0], False)
    rev = lambda t: t[:, :, ::-1]
    y_bwd = rev(_retention_scan(rev(q), rev(k), rev(v), log_g[1], True))
    y = (y_fwd + y_bwd).transpose(0, 2, 1, 3)
    y = y * lax.rsqrt(jnp.mean(y * y, axis=-1, keepdims=True) + EPS)
    y = y.reshape(B, S, GROUP_WIDTH) * gn_gain.astype(F32)
    return jax.nn.silu(rg) * y

def _neighbourhood_attention(q, k, v, rpb):
    B, S, H, hd = q.shape
    rows = S // GRID_W
    kh = min(NA_ROWS, rows)
    r = jnp.arange(rows)
    row_idx = jnp.clip(r - kh // 2, 0, rows - kh)[:, None] + jnp.arange(kh)[None, :]
    c = jnp.arange(GRID_W)
    c0 = jnp.clip(c - NA_COLS // 2, 0, GRID_W - NA_COLS)
    col_valid = (c[None, :] >= c0[:, None]) & (c[None, :] < c0[:, None] + NA_COLS)
    col_off = jnp.clip(c[None, :] - c[:, None] + NA_COLS - 1, 0, 2 * NA_COLS - 2)
    row_off = row_idx - r[:, None] + NA_ROWS - 1
    qg = q.reshape(B, rows, GRID_W, H, hd)
    kb = k.reshape(B, rows, GRID_W, H, hd)[:, row_idx]
    vb = v.reshape(B, rows, GRID_W, H, hd)[:, row_idx]
    s = jnp.einsum('brqhd,brkchd->bhrqkc', qg, kb)
    bias = rpb.astype(F32)[:, row_off[:, None, :, None], col_off[None, :, None, :]]
    s = jnp.where(col_valid[:, None, :], s + bias[None], NEG)
    p = jax.nn.softmax(s, axis=(-2, -1))
    o = jnp.einsum('bhrqkc,brkchd->brqhd', p, vb)
    return o.reshape(B, S, H, hd)

def _band_attention(q, k, v, radius):
    N, L, hd = q.shape
    blk = radius
    nb = -(-L // blk)
    pad = nb * blk - L
    qb = jnp.pad(q, ((0, 0), (0, pad), (0, 0))).reshape(N, nb, blk, hd)
    kp = jnp.pad(k, ((0, 0), (blk, blk + pad), (0, 0))).reshape(N, nb + 2, blk, hd)
    vp = jnp.pad(v, ((0, 0), (blk, blk + pad), (0, 0))).reshape(N, nb + 2, blk, hd)
    kb = jnp.concatenate([kp[:, :-2], kp[:, 1:-1], kp[:, 2:]], axis=2)
    vb = jnp.concatenate([vp[:, :-2], vp[:, 1:-1], vp[:, 2:]], axis=2)
    qi = (jnp.arange(nb)[:, None] * blk + jnp.arange(blk)[None, :])[:, :, None]
    kj = (jnp.arange(nb)[:, None] * blk - blk + jnp.arange(3 * blk)[None, :])[:, None, :]
    valid = (jnp.abs(kj - qi) <= radius) & (kj >= 0) & (kj < L)
    s = jnp.where(valid[None], jnp.einsum('nbqd,nbkd->nbqk', qb, kb), NEG)
    m = jnp.max(s, axis=-1, keepdims=True)
    p = jnp.exp(s - m)
    den = jnp.sum(p, axis=-1, keepdims=True)
    o = jnp.einsum('nbqk,nbkd->nbqd', p, vb) / den
    lse = (m + jnp.log(den))[..., 0]
    return o.reshape(N, nb * blk, hd)[:, :L], lse.reshape(N, nb * blk)[:, :L]

def _dilated_attention(q, k, v):
    B, S, H, hd = q.shape
    outs, lses = [], []
    for window, dil in DIL_BRANCHES:
        Ls = S // dil

        def to_sub(t, Ls=Ls, dil=dil):
            return t.reshape(B, Ls, dil, H, hd).transpose(0, 2, 3, 1, 4).reshape(B * dil * H, Ls, hd)

        o, lse = _band_attention(to_sub(q), to_sub(k), to_sub(v), window // (2 * dil))
        outs.append(o.reshape(B, dil, H, Ls, hd).transpose(0, 3, 1, 2, 4).reshape(B, S, H, hd))
        lses.append(lse.reshape(B, dil, H, Ls).transpose(0, 3, 1, 2).reshape(B, S, H))
    wts = jax.nn.softmax(jnp.stack(lses), axis=0)
    return jnp.sum(wts[..., None] * jnp.stack(outs), axis=0)

def _peer(xn, w_q, sub_keys, u, v):
    B, S, D = xn.shape
    T = B * S
    xt = xn.reshape(T, D)
    q = (xt @ w_q).astype(F32).reshape(T, PEER_HEADS, 2, PEER_DK // 2)
    sc = jnp.einsum('thpd,hpkd->thpk', q, sub_keys.astype(F32))
    s_top, i_top = lax.top_k(sc, PEER_TOPK)
    cand_s = (s_top[:, :, 0, :, None] + s_top[:, :, 1, None, :]).reshape(T, PEER_HEADS, PEER_TOPK * PEER_TOPK)
    cand_i = (i_top[:, :, 0, :, None] * PEER_KEYS + i_top[:, :, 1, None, :]).reshape(T, PEER_HEADS, PEER_TOPK * PEER_TOPK)
    g_s, pick = lax.top_k(cand_s, PEER_TOPK)
    experts = jnp.take_along_axis(cand_i, pick, axis=-1).reshape(T, PEER_HEADS * PEER_TOPK)
    gates = jax.nn.softmax(g_s, axis=-1).reshape(T, PEER_HEADS * PEER_TOPK)
    nblk = T // PEER_BLOCK

    def block(args):
        xb, eb, gb = args
        ub = jnp.take(u, eb, axis=0)
        act = jax.nn.gelu(jnp.einsum('td,tkd->tk', xb, ub).astype(F32)) * gb
        vb = jnp.take(v, eb, axis=0)
        return jnp.einsum('tk,tkd->td', act, vb.astype(F32))

    out = lax.map(block, (xt.reshape(nblk, PEER_BLOCK, D),
                          experts.reshape(nblk, PEER_BLOCK, -1),
                          gates.reshape(nblk, PEER_BLOCK, -1)))
    return out.reshape(B, S, D)

def setup_inputs(seed: int = 0) -> dict:
    key = jax.random.key(seed)
    ks = iter(jax.random.split(key, 32))

    def nrm(shape, std):
        return std * jax.random.normal(next(ks), shape, F32)

    Hf = HY_FILTER_HIDDEN
    ret_init = jnp.log(-jnp.log1p(-jnp.power(2.0, -5.0 - jnp.arange(RET_HEADS, dtype=F32))))
    return {
        'x': nrm((BATCH, SEQ, D_MODEL), 1.0),
        'mix_norm_gain': 1.0 + nrm((DEPTH, D_MODEL), 0.02),
        'ffn_norm_gain': 1.0 + nrm((DEPTH, D_MODEL), 0.02),
        'ev_w_in': nrm((N_EVEN, D_MODEL, EVEN_IN), D_MODEL ** -0.5),
        'ev_w_out': nrm((N_EVEN, MIX_WIDTH, D_MODEL), MIX_WIDTH ** -0.5),
        'hy_conv_w': nrm((N_EVEN, HY_SHORT, HY_IN), HY_SHORT ** -0.5),
        'hy_conv_b': nrm((N_EVEN, HY_IN), 0.02),
        'hy_fw1': nrm((N_EVEN, HY_EMB, Hf), HY_EMB ** -0.5),
        'hy_fb1': nrm((N_EVEN, Hf), 0.1),
        'hy_fw2': nrm((N_EVEN, Hf, Hf), Hf ** -0.5),
        'hy_fb2': nrm((N_EVEN, Hf), 0.1),
        'hy_fw3': nrm((N_EVEN, Hf, Hf), Hf ** -0.5),
        'hy_fb3': nrm((N_EVEN, Hf), 0.1),
        'hy_fw_out': nrm((N_EVEN, Hf, HY_ORDER * 2 * HY_CHANNELS), 0.01),
        'hy_freq': 1.0 + nrm((N_EVEN, Hf), 0.05),
        'hy_skip': nrm((N_EVEN, HY_ORDER, HY_CHANNELS), 1.0),
        'ret_log_decay': ret_init[None, None, :] + nrm((N_EVEN, 2, RET_HEADS), 0.05),
        'ret_gn_gain': 1.0 + nrm((N_EVEN, GROUP_WIDTH), 0.02),
        'od_w_in': nrm((N_ODD, D_MODEL, ODD_IN), D_MODEL ** -0.5),
        'od_w_out': nrm((N_ODD, MIX_WIDTH, D_MODEL), MIX_WIDTH ** -0.5),
        'na_qk_gain': 1.0 + nrm((N_ODD, 2, HEAD_DIM), 0.02),
        'na_rpb': nrm((N_ODD, NA_HEADS, 2 * NA_ROWS - 1, 2 * NA_COLS - 1), 0.05),
        'dil_qk_gain': 1.0 + nrm((N_ODD, 2, HEAD_DIM), 0.02),
        'peer_w_q': nrm((DEPTH, D_MODEL, PEER_HEADS * PEER_DK), D_MODEL ** -0.5),
        'peer_sub_keys': nrm((DEPTH, PEER_HEADS, 2, PEER_KEYS, PEER_DK // 2), (PEER_DK // 2) ** -0.5),
        'peer_u': nrm((DEPTH, PEER_EXPERTS, D_MODEL), D_MODEL ** -0.5),
        'peer_v': nrm((DEPTH, PEER_EXPERTS, D_MODEL), PEER_HEADS ** -0.5),
    }

def reference(x, mix_norm_gain, ffn_norm_gain, ev_w_in, ev_w_out, hy_conv_w, hy_conv_b,
              hy_fw1, hy_fb1, hy_fw2, hy_fb2, hy_fw3, hy_fb3, hy_fw_out, hy_freq, hy_skip,
              ret_log_decay, ret_gn_gain, od_w_in, od_w_out, na_qk_gain, na_rpb, dil_qk_gain,
              peer_w_q, peer_sub_keys, peer_u, peer_v):
    B, S, _ = x.shape
    scale = HEAD_DIM ** -0.5
    for layer in range(DEPTH):
        h = _rms_norm(x, mix_norm_gain[layer])
        if layer % 2 == 0:
            e = layer // 2
            proj = (h @ ev_w_in[e]).astype(F32)
            a_out = _hyena(proj[..., :HY_IN], hy_conv_w[e], hy_conv_b[e], hy_fw1[e], hy_fb1[e],
                           hy_fw2[e], hy_fb2[e], hy_fw3[e], hy_fb3[e], hy_fw_out[e], hy_freq[e], hy_skip[e])
            b_out = _retention(proj[..., HY_IN:], ret_log_decay[e], ret_gn_gain[e])
            mixed = jnp.concatenate([a_out, b_out], axis=-1).astype(x.dtype) @ ev_w_out[e]
        else:
            o = layer // 2
            proj = (h @ od_w_in[o]).astype(F32)
            na_q, na_k, na_v, dl_q, dl_k, dl_v = jnp.split(proj, 6, axis=-1)
            shp = (B, S, NA_HEADS, HEAD_DIM)
            nq = _head_rms(na_q.reshape(shp), na_qk_gain[o, 0]) * scale
            nk = _head_rms(na_k.reshape(shp), na_qk_gain[o, 1])
            c_out = _neighbourhood_attention(nq, nk, na_v.reshape(shp), na_rpb[o])
            dshp = (B, S, DIL_HEADS, HEAD_DIM)
            dq = _rope(_head_rms(dl_q.reshape(dshp), dil_qk_gain[o, 0])) * scale
            dk = _rope(_head_rms(dl_k.reshape(dshp), dil_qk_gain[o, 1]))
            d_out = _dilated_attention(dq, dk, dl_v.reshape(dshp))
            mixed = jnp.concatenate([c_out.reshape(B, S, -1), d_out.reshape(B, S, -1)],
                                    axis=-1).astype(x.dtype) @ od_w_out[o]
        x = x + mixed.astype(x.dtype)
        x = x + _peer(_rms_norm(x, ffn_norm_gain[layer]), peer_w_q[layer], peer_sub_keys[layer],
                      peer_u[layer], peer_v[layer]).astype(x.dtype)
    return x


_drawn_inputs = setup_inputs


def setup_inputs(seed=0):
    import zlib

    import numpy as np

    out = dict(_drawn_inputs(seed))
    spreads = {}
    factors = {'na_qk_gain': 6.28, 'na_rpb': 14.491, 'dil_qk_gain': 8.0}
    for name, (base, spread) in spreads.items():
        noise = np.random.default_rng([zlib.crc32(name.encode()), seed]).standard_normal(out[name].shape)
        drawn = base * np.exp(spread * noise) if base else spread * noise
        out[name] = jnp.asarray(drawn.astype(out[name].dtype))
    for name, factor in factors.items():
        out[name] = (out[name] * factor).astype(out[name].dtype)
    return out
```

```python
from contextlib import ExitStack

import concourse.bass as bass
from concourse import mybir
from concourse.alu_op_type import AluOpType as ALU

F32 = mybir.dt.float32
U32 = mybir.dt.uint32
ACT = mybir.ActivationFunctionType
AX = mybir.AxisListType

P = 128
D = 1024
DC = D // P
T = 256
TT = T // P
GW = 512
GC = GW // P
HD = 64
H = 8
EPS = 1e-6
NEG = -1e30
RING = 4
BLK = 2048
KEYS = 128
RUN = 64
EARLY = 40
ABT = 4
GB = 4

EV_IN, EV_OUT, OD_IN, OD_OUT, WQ = 14, 4, 12, 4, 4
HY_FILTERS = 64
EMB = 33

PAR = {}


def par_columns():
    at = 0
    for name, n in (("mix_gain", 2 * DC), ("ffn_gain", 2 * DC), ("conv_w", 3 * 12), ("conv_b", 12), ("skip", 8),
                    ("gn", GC), ("na_gain", 2), ("dil_gain", 2), ("fb", 3), ("freq", 1), ("decay", 16),
                    ("fw1", 64), ("fw2", 64), ("fw3", 64)):
        PAR[name] = at
        at += n
    return at


NPAR = par_columns()


class Jobs:

    def __init__(self):
        self.number, self.who, self.rank, self.total = {}, [], [], {"act": 0, "dve": 0}

    def add(self, name, who):
        self.number[name] = len(self.who)
        self.who.append(who)
        self.total[who] += 1
        self.rank.append(self.total[who])

    def bank(self, name):
        return self.number[name] % 8

    def drained(self, name):
        n = self.number[name]
        return self.who[n], self.rank[n]


def plan():
    jobs = Jobs()
    add = jobs.add
    add(("ms_mix", 0), "act")
    for n in range(3):
        add(("hidden", n), "dve")
        for it in (2 * n, 2 * n + 1):
            add(("in0", it), "dve")
    for o in range(2):
        for tt in range(TT):
            add(("filt", o, tt, 0), "dve")
            add(("filt", o, tt, 1), "dve")
        for it in (6 + 4 * o, 7 + 4 * o):
            add(("in0", it), "act")
        for kt in range(2):
            for ri in range(2):
                add(("hf", o, kt, ri), "act")
        for it in (8 + 4 * o, 9 + 4 * o):
            add(("in0", it), "act")
    for o in range(2):
        for tt in range(TT):
            add(("zt", o, tt), "act")
        if o == 0:
            for n in range(4):
                add(("rot0", n), "dve")
        for kt in range(2):
            for ri in range(2):
                add(("zf", o, kt, ri), "dve")
        for h in range(4 * o, 4 * o + 4):
            add(("ret_s", h), "dve")
        for n in range(2):
            add(("conv", o, n), "dve")
        for n in (2 * o, 2 * o + 1):
            add(("ret_y", n), "act")
    for n in range(2):
        add(("ms_gn", n), "act")
    for n in range(EV_OUT):
        add(("out0", n), "dve")
    for l in range(2):
        if l == 1:
            add(("ms_mix", 1), "act")
            for it in range(OD_IN):
                add(("in1", it), "act")
            for n in range(8):
                add(("ms_head", n), "act")
            for n in range(4):
                add(("rot1", n), "dve")
            for u in range(16 + 2):
                if u < 16:
                    add(("att_s", u), "dve")
                if u >= 1 and u <= 16:
                    add(("att_t", u - 1), "act")
                if u >= 2 and (u - 2) % 2 == 1:
                    add(("att_o", (u - 2) // 2), "act")
            for n in range(OD_OUT):
                add(("out1", n), "dve")
        add(("ms_ffn", l), "act")
        for n in range(WQ):
            add(("q", l, n), "act")
        for n in range(8):
            add(("sc", l, n), "act" if n % 2 else "dve")
        for n in range(3):
            add(("gt", l, n), "dve")
    return jobs


class Chain:

    def __init__(self, eng, sem):
        self.eng, self.sem, self.n, self.turn, self.per, self.k = eng, sem, 0, None, 0, 0

    def link(self, ins):
        ins.then_inc(self.sem, 1)
        if self.turn is None:
            self.n += 1
            self.eng.wait_ge(self.sem, self.n)
        else:
            self.k += 1
            self.eng.wait_ge(self.sem, self.turn * self.per + (self.n + self.k))

    def drain_after(self, ins):
        self.eng.drain()

    def wait(self):
        self.eng.wait_ge(self.sem, self.n)

    def enter(self, turn, per):
        self.turn, self.per, self.k = turn, per, 0

    def leave(self, turns):
        assert self.k == self.per, (self.k, self.per)
        self.n += turns * self.per
        self.turn = None


def hybrid_trunk(nc, xT, par, consts, con0, con1, subk, w_ev_in, w_ev_out, w_od_in, w_od_out, w_q, fw_out,
                 na_bias, u_t, v_t, out, dbg=None):
    jobs = plan()
    ctx = ExitStack()
    with ctx:
        def sb(name, shape, dt=F32):
            return ctx.enter_context(nc.sbuf_tensor(name, shape, dt))

        def sem(name):
            return ctx.enter_context(nc.semaphore(name))

        x = sb("x", [P, DC, T])
        h = sb("h", [P, DC, T])
        ring = sb("ring", [P, RING, BLK])
        big = sb("big", [P, KEYS * T])
        coef = big[:, :].rearrange("p (j t) -> p j t", t=T)
        pa = sb("pa", [P, NPAR])
        cst = sb("cst", [P, 5 * P + 2 * T])
        ident, rot_m, ones_d, ones_h, iota = (cst[:, k * P:(k + 1) * P] for k in range(5))
        cos_t = cst[:, 5 * P:5 * P + T]
        sin_t = cst[:, 5 * P + T:5 * P + 2 * T]
        ab = sb("ab", [P, 2, 2, ABT, P])
        gij = sb("gij", [P, 3, T])
        gtmp = sb("gtmp", [P, 2, T])
        rs = sb("rs", [P, 2 * T])
        eps = sb("eps", [P, 2])
        lgn = sb("lgn", [P, 16])

        at = [0]

        def carve(n, start=None):
            if start is not None:
                at[0] = start
            ap = big[:, at[0]:at[0] + n]
            at[0] += n
            assert at[0] <= KEYS * T, at[0]
            return ap

        uc = carve(12 * T, 0).rearrange("p (m t) -> p m t", t=T)
        qk = carve(8 * T).rearrange("p (m t) -> p m t", t=T)
        v0 = carve(TT * GW).rearrange("p (a c) -> p a c", a=TT)
        rg = carve(GC * T).rearrange("p (m t) -> p m t", t=T)
        hid = carve(T)
        harg = carve(2 * T).rearrange("p (a t) -> p a t", a=2)
        fpm = carve(4 * GW).rearrange("p (s a c) -> p s a c", s=2, a=TT)
        hf = carve(8 * GW).rearrange("p (o k r c) -> p o k r c", o=2, k=2, r=2)
        fwo = carve(4 * GW)
        zt = carve(TT * GW).rearrange("p (a c) -> p a c", a=TT)
        yf = carve(4 * GW).rearrange("p (k r c) -> p k r c", k=2, r=2)
        tmp = carve(2 * GW).rearrange("p (a c) -> p a c", a=2)
        cat = carve(DC * T).rearrange("p (m t) -> p m t", t=T)
        dec = carve(2 * GW).rearrange("p (a c) -> p a c", a=2)
        prob = carve(4 * GW).rearrange("p (b a t) -> p b a t", b=4, a=2)
        sig = carve(GC * T).rearrange("p (m t) -> p m t", t=T)
        con0_s = carve(256 + 1024 + 1024 + 2048 + 1024)
        emb = con0_s[:, 0:256]
        dft = con0_s[:, 256:1280].rearrange("p (a k) -> p a k", a=TT)
        idft = con0_s[:, 1280:2304].rearrange("p (r t) -> p r t", t=T)
        win = con0_s[:, 2304:4352].rearrange("p (a d c) -> p a d c", a=TT, d=2)
        dist = con0_s[:, 4352:5376].rearrange("p (d a t) -> p d a t", d=2, a=2)
        yr = hf[:, 0, :, :, :].rearrange("p k r c -> p (k r c)")[:, 0:GC * T].rearrange("p (m t) -> p m t", t=T)
        ysq = hf[:, 0, :, :, :].rearrange("p k r c -> p (k r c)")[:, GC * T:2 * GC * T].rearrange("p (m t) -> p m t", t=T)
        zc = uc[:, 0:4, :]

        def gn_root(n):
            return ysq[:, 2 * n:2 * n + 2, :].rearrange("p a t -> p (a t)")

        hq = carve(16 * T, 0).rearrange("p (m t) -> p m t", t=T)
        hsq = carve(16 * T).rearrange("p (m t) -> p m t", t=T)
        v1 = carve(2 * TT * GW).rearrange("p (g a c) -> p g a c", g=2, a=TT)
        bias = carve(9 * 2 * T).rearrange("p (h a t) -> p h a t", h=9, a=2)
        s_att = carve(2 * 2 * T).rearrange("p (b a t) -> p b a t", b=2, a=2)
        p_att = carve(2 * 2 * T).rearrange("p (b a t) -> p b a t", b=2, a=2)
        pt_att = carve(2 * 2 * T).rearrange("p (b a t) -> p b a t", b=2, a=2)
        cat1 = carve(DC * T).rearrange("p (m t) -> p m t", t=T)
        st_att = carve(64).rearrange("p (b s a) -> p b s a", b=8, s=4)

        qT = carve(8 * T, RUN * T).rearrange("p (m t) -> p m t", t=T)
        sc = carve(2 * 16 * KEYS).rearrange("p (s c) -> p s c", s=2)
        cur = carve(2 * KEYS).rearrange("p (s c) -> p s c", s=2)
        cut = carve(2 * KEYS).rearrange("p (s c) -> p s c", s=2)
        top_s = carve(32).rearrange("p (s c) -> p s c", s=2)
        top_i = carve(32).rearrange("p (s c) -> p s c", s=2).bitcast(U32)
        top_f = carve(32).rearrange("p (s c) -> p s c", s=2)
        cand = carve(256)
        cand2 = carve(256)
        g16 = carve(16)
        pick = carve(16).bitcast(U32)
        pab = carve(32).rearrange("p (s c) -> p s c", s=2).bitcast(U32)
        pabf = carve(32).rearrange("p (s c) -> p s c", s=2)
        look = carve(512).rearrange("p (s k a) -> p s k a", s=2, k=16)
        gs = carve(256)
        ijs = carve(512).rearrange("p (s c) -> p s c", s=2)
        ge = carve(256)
        gsum = carve(16)
        assert at[0] <= KEYS * T - 1024
        sk = big[:, KEYS * T - 1024:KEYS * T].rearrange("p (h k) -> p h k", h=8)

        ps = ctx.enter_context(nc.psum_tensor("ps", [P, 8, 512], F32))

        def bank(name):
            return ps[:, jobs.bank(name), :]

        x_in = sem("x_in")
        par_in = sem("par_in")
        cst_in = sem("cst_in")
        con0_in = sem("con0_in")
        fwo_in = sem("fwo_in")
        sk_in = sem("sk_in")
        bias_in = sem("bias_in")
        out_done = sem("out_done")
        full = [sem(f"block_in{s}") for s in range(RING)]
        psum_full = sem("psum_full")
        drained = {"act": sem("drained_by_act"), "dve": sem("drained_by_dve")}
        dve_own = sem("dve_own")
        consts_set = sem("consts_set")
        squared = sem("squared")
        normed = sem("normed")
        hid_arg = sem("hid_arg")
        hid_done = sem("hid_done")
        conv_mid = sem("conv_mid")
        filt_pm = sem("filt_pm")
        yf_done = sem("yf_done")
        roped = sem("roped")
        dec_arg = sem("dec_arg")
        dec_exp = sem("dec_exp")
        lg_done = sem("lg_done")
        ysq_done = sem("ysq_done")
        silu_e = sem("silu_e")
        cat_done = sem("cat_done")
        head_done = sem("head_done")
        s_biased = sem("s_biased")
        s_exp = sem("s_exp")
        p_normed = sem("p_normed")
        gate_arg = sem("gate_arg")
        gate_exp = sem("gate_exp")
        gates_done = sem("gates_done")
        u_full = sem("u_full")
        v_used = sem("v_used")
        gelu_done = sem("gelu_done")

        onehots = sem("onehots")
        onehots_used = sem("onehots_used")
        gate_full = sem("gate_full")
        gate_mult = sem("gate_mult")
        gate_free = sem("gate_free")
        coef_done = sem("coef_done")
        acc_read = sem("acc_read")

        block = ctx.enter_context(nc.Block())

        def par_col(name, k=0, rows=P):
            return pa[0:rows, PAR[name] + k:PAR[name] + k + 1]

        starts = {}
        n_blocks = 0
        for name, n in (("ev_in", EV_IN), ("ev_out", EV_OUT), ("wq0", WQ), ("experts0", KEYS),
                        ("od_in", OD_IN), ("od_out", OD_OUT), ("wq1", WQ), ("experts1", KEYS)):
            starts[name] = n_blocks
            n_blocks += n

        half = RUN // 2
        assert 2 * RUN == KEYS
        used = {}

        def note(name, jobs_of):
            for k, job in enumerate(jobs_of):
                used[starts[name] + k] = (psum_full, jobs.number[job] + 1)

        note("ev_in", [("in0", k) for k in range(EV_IN)])
        note("ev_out", [("out0", k) for k in range(EV_OUT)])
        note("od_in", [("in1", k) for k in range(OD_IN)])
        note("od_out", [("out1", k) for k in range(OD_OUT)])
        for l in range(2):
            note(f"wq{l}", [("q", l, k) for k in range(WQ)])

        def u_used(l, pair):
            return u_full, KEYS * l + 2 * pair + 2

        def v_used_by(l, pair):
            return v_used, (KEYS // 2) * l + pair + 1

        @block.sync
        def _(sp):
            def load(n, src):
                if n >= RING:
                    sp.wait_ge(*used[n - RING])
                sp.dma_start(ring[:, n % RING, :], src).then_inc(full[n % RING], 16)

            def load_part(name, w):
                for k in range(w.shape[0]):
                    load(starts[name] + k, w[k])

            sp.dma_start(x[:, :, :], xT).then_inc(x_in, 16)
            load_part("ev_in", w_ev_in)
            load_part("ev_out", w_ev_out)
            for l in range(2):
                if l == 1:
                    load_part("od_in", w_od_in)
                    load_part("od_out", w_od_out)
                load_part(f"wq{l}", w_q[l])

                def experts(first, turns, order):
                    for k, (table, base, step, told) in enumerate(order):
                        load(first + k, table[l, base])
                        used[first + (turns - 1) * RING + k] = (told[0], told[1] + (turns - 1) * told[2])
                    with sp.Fori(1, turns) as i:
                        for k, (table, base, step, told) in enumerate(order):
                            sp.wait_ge(told[0], i * told[2] + (told[1] - told[2]))
                            src = table[l, bass.ds(i * step + base, 1), :, :].rearrange("a p n -> p (a n)")
                            sp.dma_start(ring[:, (first + k) % RING, :], src).then_inc(full[(first + k) % RING], 16)

                n0 = starts[f"experts{l}"]
                experts(n0, half // RING, [(u_t, k, RING, (*u_used(l, k), 2 * RING)) for k in range(RING)])
                experts(n0 + half, half // 2,
                        [(u_t, half, 2, (*u_used(l, half), 4)), (v_t, 0, 2, (*v_used_by(l, 0), 2)),
                         (u_t, half + 1, 2, (*u_used(l, half + 1), 4)), (v_t, 1, 2, (*v_used_by(l, 1), 2))])
                experts(n0 + 3 * half, half // RING,
                        [(v_t, half + k, RING, (*v_used_by(l, half + k), RING)) for k in range(RING)])
            sp.wait_ge(acc_read, 2)
            sp.dma_start(out, x[:, :, :]).then_inc(out_done, 16)
            sp.wait_ge(out_done, 16)

        @block.gpsimd
        def _(pool):
            pool.dma_start(pa[:, :], par).then_inc(par_in, 16)
            pool.dma_start(cst[:, :], consts).then_inc(cst_in, 16)
            pool.dma_start(con0_s[:, :], con0).then_inc(con0_in, 16)
            pool.dma_start(fwo[0:HY_FILTERS, :], fw_out).then_inc(fwo_in, 16)
            pool.dma_start(sk[:, :, :], subk[0]).then_inc(sk_in, 16)
            pool.wait_ge(v_used, KEYS // 2)
            pool.dma_start(bias[:, 0:8, :, :], na_bias).then_inc(bias_in, 16)
            pool.dma_start(bias[:, 8, :, :], con1).then_inc(bias_in, 16)
            pool.dma_start(sk[:, :, :], subk[1]).then_inc(sk_in, 16)

        @block.tensor
        def _(pe):
            def begin(name):
                n = jobs.number[name]
                if n >= 8:
                    pe.wait_ge(drained[jobs.who[n - 8]], jobs.rank[n - 8])

            def wait_drained(*name):
                who, count = jobs.drained(name)
                pe.wait_ge(drained[who], count)

            def mm(o, a, b, start, stop, **kw):
                return nc.tensor.matmul(o, a, b, start=start, stop=stop, **kw)

            def mean_square(name, count):
                begin(name)
                pe.wait_ge(squared, count)
                for c in range(DC):
                    last = mm(bank(name)[:, 0:T], ones_d, h[:, c, :], c == 0, c == DC - 1)
                last.then_inc(psum_full, 1)

            def project(name, n, rhs, transposed=True):
                begin(name)
                pe.wait_ge(full[n % RING], 16 * (n // RING + 1))
                w = ring[:, n % RING, :].rearrange("p (c m) -> p c m", c=DC)
                for m in range(2):
                    for c in range(DC):
                        if transposed:
                            last = mm(bank(name)[:, m * T:(m + 1) * T], w[:, c, m * P:(m + 1) * P], rhs[:, c, :],
                                      c == 0, c == DC - 1)
                        else:
                            last = mm(bank(name)[:, m * T:(m + 1) * T], rhs[:, c, m * P:(m + 1) * P], w[:, c, :],
                                      c == 0, c == DC - 1)
                last.then_inc(psum_full, 1)

            def one(name, *mms):
                begin(name)
                for o, a, b, s, e in mms:
                    last = mm(o, a, b, s, e)
                last.then_inc(psum_full, 1)

            pe.wait_ge(cst_in, 16)
            mean_square(("ms_mix", 0), 1)
            pe.wait_ge(par_in, 16)
            pe.wait_ge(con0_in, 16)
            for n in range(3):
                if n:
                    pe.wait_ge(hid_done, n)
                name = ("hidden", n)
                w = pa[0:EMB if n == 0 else HY_FILTERS, PAR["fw1"] + 64 * n:PAR["fw1"] + 64 * n + 64]
                one(name, (bank(name)[0:HY_FILTERS, 0:T], w, emb[0:EMB, :] if n == 0 else hid[0:HY_FILTERS, :],
                           True, True))
                if n == 0:
                    pe.wait_ge(normed, 1)
                for it in (2 * n, 2 * n + 1):
                    project(("in0", it), starts["ev_in"] + it, h)
            pe.wait_ge(hid_done, 3)
            pe.wait_ge(fwo_in, 16)
            for o in range(2):
                for tt in range(TT):
                    for d in range(2):
                        name = ("filt", o, tt, d)
                        one(name, (bank(name), hid[0:HY_FILTERS, tt * P:(tt + 1) * P],
                                   fwo[0:HY_FILTERS, (o * 2 + d) * GW:(o * 2 + d + 1) * GW], True, True))
                for it in (6 + 4 * o, 7 + 4 * o):
                    project(("in0", it), starts["ev_in"] + it, h)
                pe.wait_ge(filt_pm, 2 * (o + 1))
                for kt in range(2):
                    for ri in range(2):
                        name = ("hf", o, kt, ri)
                        one(name, *((bank(name), dft[:, tt, ri * T + kt * P:ri * T + (kt + 1) * P],
                                     fpm[:, ri, tt, :], tt == 0, tt == TT - 1) for tt in range(TT)))
                for it in (8 + 4 * o, 9 + 4 * o):
                    project(("in0", it), starts["ev_in"] + it, h, transposed=(o == 1))

            def retention_scores(hh):
                name = ("ret_s", hh)
                o64 = 64 * (hh % 2)
                one(name, *((bank(name)[:, a * T:(a + 1) * T], qk[o64:o64 + 64, 4 + hh // 2, a * P:(a + 1) * P],
                             qk[o64:o64 + 64, hh // 2, :], True, True) for a in range(2)))

            def retention_values(n):
                name = ("ret_y", n)
                begin(name)
                for b in range(2):
                    hh = 2 * n + b
                    wait_drained("ret_s", hh)
                    for a in range(2):
                        last = mm(bank(name)[64 * b:64 * b + 64, 0:T], v0[:, a, hh * HD:(hh + 1) * HD],
                                  prob[:, hh % 4, a, :], a == 0, a == 1)
                    last.then_inc(psum_full, 1) if b == 1 else None

            for o in range(2):
                if o == 0:
                    wait_drained("in0", 1)
                else:
                    wait_drained("conv", 0, 1)
                for tt in range(TT):
                    name = ("zt", o, tt)
                    begin(name)
                    for c in range(GC):
                        last = nc.tensor.transpose(bank(name)[:, c * P:(c + 1) * P], zc[:, c, tt * P:(tt + 1) * P],
                                                   ident)
                    last.then_inc(psum_full, 1)
                if o == 0:
                    wait_drained("in0", 11)
                    for n in range(4):
                        name = ("rot0", n)
                        one(name, (bank(name), rot_m, qk[:, 2 * n:2 * n + 2, :].rearrange("p a t -> p (a t)"),
                                   True, True))
                wait_drained("zt", o, 1)
                for kt in range(2):
                    for ri in range(2):
                        name = ("zf", o, kt, ri)
                        one(name, *((bank(name), dft[:, tt, ri * T + kt * P:ri * T + (kt + 1) * P], zt[:, tt, :],
                                     tt == 0, tt == TT - 1) for tt in range(TT)))
                pe.wait_ge(roped, 4)
                for hh in range(4 * o, 4 * o + 4):
                    retention_scores(hh)
                pe.wait_ge(yf_done, 2 * (o + 1))
                for n in range(2):
                    name = ("conv", o, n)
                    begin(name)
                    for b in range(2):
                        c = 2 * n + b
                        for r in range(4):
                            last = mm(bank(name)[:, b * T:(b + 1) * T], yf[:, r // 2, r % 2, c * P:(c + 1) * P],
                                      idft[:, r, :], r == 0, r == 3)
                    last.then_inc(psum_full, 1)
                wait_drained("in0", 9)
                for n in (2 * o, 2 * o + 1):
                    retention_values(n)
            pe.wait_ge(ysq_done, 1)
            for n in range(2):
                name = ("ms_gn", n)
                one(name, (bank(name), ones_h, ysq[:, 2 * n:2 * n + 2, :].rearrange("p a t -> p (a t)"), True, True))
            wait_drained("conv", 1, 1)
            pe.wait_ge(cat_done, 2)
            for n in range(EV_OUT):
                project(("out0", n), starts["ev_out"] + n, cat)

            def attention_scores(u):
                g, hh = divmod(u, H)
                name = ("att_s", u)
                o64 = 64 * (hh % 2)
                one(name, *((bank(name)[:, a * T:(a + 1) * T], hq[o64:o64 + 64, 8 * g + hh // 2, a * P:(a + 1) * P],
                             hq[o64:o64 + 64, 8 * g + 4 + hh // 2, :], True, True) for a in range(2)))

            def attention_turn(u):
                name = ("att_t", u)
                begin(name)
                pe.wait_ge(p_normed, u + 1)
                for kt in range(2):
                    for a in range(2):
                        last = nc.tensor.transpose(bank(name)[:, kt * T + a * P:kt * T + (a + 1) * P],
                                                   p_att[:, u % 2, a, kt * P:(kt + 1) * P], ident)
                last.then_inc(psum_full, 1)

            def attention_values(n):
                name = ("att_o", n)
                begin(name)
                for b in range(2):
                    u = 2 * n + b
                    g, hh = divmod(u, H)
                    wait_drained("att_t", u)
                    for kt in range(2):
                        last = mm(bank(name)[64 * b:64 * b + 64, 0:T], v1[:, g, kt, hh * HD:(hh + 1) * HD],
                                  pt_att[:, u % 2, kt, :], kt == 0, kt == 1)
                    last.then_inc(psum_full, 1) if b == 1 else None

            for l in range(2):
                if l == 1:
                    mean_square(("ms_mix", 1), 3)
                    pe.wait_ge(normed, 3)
                    for it in range(OD_IN):
                        project(("in1", it), starts["od_in"] + it, h, transposed=it not in (4, 5, 10, 11))
                    for n in range(8):
                        name = ("ms_head", n)
                        wait_drained("in1", n + 2 * (n // 4))
                        one(name, (bank(name), ones_h, hsq[:, 2 * n:2 * n + 2, :].rearrange("p a t -> p (a t)"),
                                   True, True))
                    for n in range(4):
                        name = ("rot1", n)
                        pe.wait_ge(head_done, 8)
                        one(name, (bank(name), rot_m, hq[:, 8 + 2 * n:10 + 2 * n, :].rearrange("p a t -> p (a t)"),
                                   True, True))
                    for u in range(16 + 2):
                        if u < 16:
                            if u == H:
                                pe.wait_ge(roped, 8)
                            attention_scores(u)
                        if 1 <= u <= 16:
                            attention_turn(u - 1)
                        if u >= 2 and (u - 2) % 2 == 1:
                            attention_values((u - 2) // 2)
                    wait_drained("att_o", 7)
                    for n in range(OD_OUT):
                        project(("out1", n), starts["od_out"] + n, cat1)

                mean_square(("ms_ffn", l), 2 + 2 * l)
                pe.wait_ge(normed, 2 + 2 * l)
                for n in range(WQ):
                    project(("q", l, n), starts[f"wq{l}"] + n, h)
                wait_drained("q", l, WQ - 1)
                pe.wait_ge(sk_in, 16 * (l + 1))
                for n in range(8):
                    tt, quad, s = n // 4, n // 2 % 2, n % 2
                    name = ("sc", l, n)
                    one(name, *((bank(name)[:, k * KEYS:(k + 1) * KEYS],
                                 qT[64 * s:64 * s + 64, 4 * quad + k, tt * P:(tt + 1) * P],
                                 sk[64 * s:64 * s + 64, 4 * quad + k, :], True, True) for k in range(4)))

                def up(slot, i, k, per, j0):
                    w = ring[:, slot, :].rearrange("p (b c m) -> p b c m", b=2, c=DC)
                    for b in range(2):
                        pe.wait_ge(gelu_done, i * per + (KEYS * l + j0 + 2 * k + b + 1))
                        for c in range(DC):
                            last = mm(ps[:, 4 + b, 0:T], w[:, b, c, :], h[:, c, :], c == 0, c == DC - 1)
                        last.then_inc(u_full, 1)

                def down(slot, j):
                    w = ring[:, slot, :].rearrange("p (b c m) -> p b c m", b=2, c=DC)
                    for b in range(2):
                        for c in range(DC):
                            last = mm(ps[:, c // 2, (c % 2) * T:(c % 2 + 1) * T], w[:, b, c, :],
                                      coef[:, bass.ds(j + b, 1), :].rearrange("p a t -> p (a t)"), False, False,
                                      skip_group_check=True)
                    return last

                n0 = starts[f"experts{l}"]

                def up_loop(lo, hi):
                    with pe.Fori(lo, hi) as i:
                        for k in range(RING):
                            n = n0 + k
                            pe.wait_ge(full[n % RING], i * 16 + 16 * (n // RING + 1))
                            up(n % RING, i, k, 2 * RING, 0)

                wait_drained("sc", l, 6)
                wait_drained("sc", l, 7)
                up_loop(0, EARLY // (2 * RING))
                pe.wait_ge(gates_done, l + 1)
                for n in range(3):
                    name = ("gt", l, n)
                    src = gs if n == 0 else ijs[:, n - 1, :]
                    for tt in range(TT):
                        last = nc.tensor.transpose(ps[:, (6 + n) % 8, tt * P:(tt + 1) * P],
                                                   src[:, tt * P:(tt + 1) * P], ident)
                    last.then_inc(psum_full, 1)
                up_loop(EARLY // (2 * RING), RUN // (2 * RING))
                wait_drained("gt", l, 2)
                turns = T // (GB * ABT)
                with pe.Fori(0, turns) as i:
                    for q in range(GB):
                        pe.wait_ge(onehots, i * GB + (l * (turns * GB + 1) + q + 1))
                        pe.wait_ge(gate_free, i * GB + (l * turns * GB + q + 1))
                        for k in range(ABT):
                            last = mm(ps[:, q, k * P:(k + 1) * P], ab[:, q % 2, 0, k, :], ab[:, q % 2, 1, k, :],
                                      True, True)
                        last.then_inc(gate_full, 1)
                pe.wait_ge(gate_free, (l + 1) * turns * GB + GB)
                pe.wait_ge(onehots, (l + 1) * turns * GB + l + 1)
                for b in range(4):
                    last = mm(ps[:, b, :], ab[:, 0, 0, 0, :], gij[:, 0:2, :].rearrange("p a t -> p (a t)"),
                              True, True, skip_group_check=True)
                with pe.Fori(0, half // 2) as i:
                    for k in range(2):
                        n = n0 + half + 2 * k
                        pe.wait_ge(full[n % RING], i * 16 + 16 * (n // RING + 1))
                        up(n % RING, i, k, 4, RUN)
                        n += 1
                        pe.wait_ge(full[n % RING], i * 16 + 16 * (n // RING + 1))
                        down(n % RING, i * 4 + 2 * k).then_inc(v_used, 1)
                n1 = n0 + 3 * half
                with pe.Fori(0, half // RING) as i:
                    for k in range(RING):
                        n = n1 + k
                        pe.wait_ge(full[n % RING], i * 16 + 16 * (n // RING + 1))
                        pe.wait_ge(coef_done, i * (2 * RING) + (2 + l * (KEYS - RUN) + 2 * k + 2))
                        down(n % RING, i * (2 * RING) + (RUN + 2 * k)).then_inc(v_used, 1)

        @block.scalar
        def _(act):
            A = nc.scalar.activation

            def take(name):
                act.wait_ge(psum_full, jobs.number[name] + 1)

            def wait_drained(*name):
                who, count = jobs.drained(name)
                act.wait_ge(drained[who], count)

            def norm(name):
                A(h[:, :, :], x[:, :, :], ACT.Square).then_inc(squared, 1)
                take(name)
                A(rs[:, 0:T], bank(name)[:, 0:T], ACT.Sqrt, bias=eps[:, 0:1]).then_inc(drained["act"], 1)

            def copy(o, i, scale=1.0):
                A(o, i, ACT.Copy, scale=scale).then_inc(drained["act"], 1)

            act.sem_inc(gelu_done, 2)
            act.sem_inc(gate_free, GB)
            act.wait_ge(x_in, 16)
            act.wait_ge(consts_set, 1)
            norm(("ms_mix", 0))
            act.wait_ge(par_in, 16)
            A(lgn[:, :], pa[:, PAR["decay"]:PAR["decay"] + 16], ACT.Exp).then_inc(lg_done, 1)
            for n in range(3):
                act.wait_ge(hid_arg, n + 1)
                A(hid[0:HY_FILTERS, :], harg[0:HY_FILTERS, 0, :], ACT.Sin).then_inc(hid_done, 1)
                for it in (2 * n, 2 * n + 1):
                    take(("in0", it))
                    for m in range(2):
                        t = 2 * it + m
                        last = A(uc[:, t, :], bank(("in0", it))[:, m * T:(m + 1) * T], ACT.Identity,
                                 bias=par_col("conv_b", t), scale=par_col("conv_w", 12 + t))
                    last.then_inc(conv_mid, 1)
            for o in range(2):
                for it in (6 + 4 * o, 7 + 4 * o):
                    take(("in0", it))
                    t = 4 * o + 2 * (it % 2)
                    copy(qk[:, t:t + 2, :].rearrange("p a t -> p (a t)"), bank(("in0", it)),
                         scale=1.0 if o == 0 else HD ** -0.5)
                for kt in range(2):
                    for ri in range(2):
                        take(("hf", o, kt, ri))
                        copy(hf[:, o, kt, ri, :], bank(("hf", o, kt, ri)))
                for it in (8 + 4 * o, 9 + 4 * o):
                    take(("in0", it))
                    if o == 0:
                        c0 = T * (it % 2)
                        copy(v0[:, :, c0:c0 + T], bank(("in0", it)).rearrange("p (a c) -> p a c", a=2))
                    else:
                        t = 2 * (it % 2)
                        copy(rg[:, t:t + 2, :].rearrange("p a t -> p (a t)"), bank(("in0", it)))
            wait_drained("in0", 13)
            A(sig[:, :, :], rg[:, :, :], ACT.Exp, scale=-1.0).then_inc(silu_e, 1)
            for o in range(2):
                for tt in range(TT):
                    take(("zt", o, tt))
                    copy(zt[:, tt, :], bank(("zt", o, tt)))
                for hh in range(4 * o, 4 * o + 4):
                    act.wait_ge(dec_arg, hh + 1)
                    A(dec[:, hh % 2, :], dec[:, hh % 2, :], ACT.Exp, scale=-1.0).then_inc(dec_exp, 1)
                for n in (2 * o, 2 * o + 1):
                    take(("ret_y", n))
                    copy(yr[:, n, :], bank(("ret_y", n))[:, 0:T])
            wait_drained("ret_y", 3)
            A(ysq[:, :, :], yr[:, :, :], ACT.Square).then_inc(ysq_done, 1)
            for n in range(2):
                take(("ms_gn", n))
                A(gn_root(n), bank(("ms_gn", n)), ACT.Sqrt, bias=eps[:, 0:1]).then_inc(drained["act"], 1)

            for l in range(2):
                if l == 1:
                    act.wait_ge(acc_read, 1)
                    norm(("ms_mix", 1))
                    for it in range(OD_IN):
                        take(("in1", it))
                        g, k = divmod(it, 6)
                        if k < 4:
                            t = 8 * g + 2 * k
                            A(hq[:, t:t + 2, :].rearrange("p a t -> p (a t)"), bank(("in1", it)), ACT.Copy)
                            A(hsq[:, t:t + 2, :].rearrange("p a t -> p (a t)"), bank(("in1", it)),
                              ACT.Square).then_inc(drained["act"], 1)
                        else:
                            c0 = T * (k - 4)
                            copy(v1[:, g, :, c0:c0 + T], bank(("in1", it)).rearrange("p (a c) -> p a c", a=2))
                    for n in range(8):
                        take(("ms_head", n))
                        q = n % 4 < 2
                        A(hsq[:, 2 * n:2 * n + 2, :].rearrange("p a t -> p (a t)"), bank(("ms_head", n)), ACT.Sqrt,
                          scale=float(HD) if q else 1.0,
                          bias=eps[:, 1:2] if q else eps[:, 0:1]).then_inc(drained["act"], 1)
                    for u in range(16 + 2):
                        if u < 16:
                            act.wait_ge(s_biased, u + 1)
                            for a in range(2):
                                last = A(p_att[:, u % 2, a, :], s_att[:, u % 2, a, :], ACT.Exp,
                                         bias=st_att[:, u % 8, 0, a:a + 1], accum_out=st_att[:, u % 8, 1, a:a + 1])
                            last.then_inc(s_exp, 1)
                        if 1 <= u <= 16:
                            take(("att_t", u - 1))
                            if u - 1 >= 2:
                                act.wait_ge(psum_full, jobs.number[("att_o", (u - 3) // 2)] + 1)
                            copy(pt_att[:, (u - 1) % 2, :, :].rearrange("p a t -> p (a t)"), bank(("att_t", u - 1)))
                        if u >= 2 and (u - 2) % 2 == 1:
                            n = (u - 2) // 2
                            take(("att_o", n))
                            copy(cat1[:, n, :], bank(("att_o", n))[:, 0:T])

                wait_drained(f"out{l}", 3)
                norm(("ms_ffn", l))
                for n in range(WQ):
                    take(("q", l, n))
                    copy(qT[:, 2 * n:2 * n + 2, :].rearrange("p a t -> p (a t)"), bank(("q", l, n)))
                for n in range(1, 8, 2):
                    take(("sc", l, n))
                    tt, quad, s = n // 4, n // 2 % 2, n % 2
                    q0 = (tt * 8 + 4 * quad) * KEYS
                    copy(sc[:, s, q0:q0 + 4 * KEYS], bank(("sc", l, n)))

                def gelus(lo, hi):
                    with act.Fori(lo, hi) as j:
                        for b in range(2):
                            act.wait_ge(u_full, j * 2 + (l * KEYS + b + 1))
                            A(coef[:, bass.ds(2 * j + b, 1), :].rearrange("p a t -> p (a t)"), ps[:, 4 + b, 0:T],
                              ACT.Gelu_apprx_tanh).then_inc(gelu_done, 1)

                gelus(0, EARLY // 2)
                act.wait_ge(gate_arg, l + 1)
                A(ge[:, :], ge[:, :], ACT.Exp).then_inc(gate_exp, 1)
                gelus(EARLY // 2, RUN // 2)
                turns = T // (GB * ABT)
                with act.Fori(0, turns) as i:
                    for q in range(GB):
                        act.wait_ge(gate_mult, i * GB + (l * turns * GB + q + 1))
                        A(coef[:, RUN:KEYS, bass.ds(i * (GB * ABT) + q * ABT, ABT)],
                          ps[:, q, :].rearrange("p (t j) -> p j t", t=ABT)[:, RUN:KEYS, :],
                          ACT.Copy).then_inc(gate_free, 1)
                with act.Fori(0, (KEYS - RUN) // 2) as j:
                    for b in range(2):
                        act.wait_ge(u_full, j * 2 + (l * KEYS + RUN + b + 1))
                        act.wait_ge(coef_done, j * 2 + (l * (KEYS - RUN) + b + 1))
                        A(gtmp[:, b, :], ps[:, 4 + b, 0:T], ACT.Gelu_apprx_tanh).then_inc(gelu_done, 1)

        @block.vector
        def _(dve):
            own = Chain(dve, dve_own)
            V = nc.vector

            def take(name):
                dve.wait_ge(psum_full, jobs.number[name] + 1)

            def wait_drained(*name):
                who, count = jobs.drained(name)
                dve.wait_ge(drained[who], count)

            def drain(name, ins):
                ins.then_inc(drained["dve"], 1)
                wait_drained(*name)

            def norm(gain, l, *name):
                wait_drained(*name)
                own.link(V.reciprocal(rs[:, T:2 * T], rs[:, 0:T]))
                for c in range(DC):
                    last = V.scalar_tensor_tensor(out=h[:, c, :], in0=x[:, c, :], scalar=par_col(gain, l * DC + c),
                                                  in1=rs[:, T:2 * T], op0=ALU.mult, op1=ALU.mult)
                last.then_inc(normed, 1)

            V.memset(eps[:, 0:1], EPS)
            V.memset(eps[:, 1:2], EPS * HD).then_inc(consts_set, 1)
            dve.sem_inc(coef_done, 2)
            dve.wait_ge(par_in, 16)
            norm("mix_gain", 0, "ms_mix", 0)
            TWO_PI_HI, TWO_PI_LO, MAGIC = 6.28125, 0.0019353071795864769, 12582912.0
            F = HY_FILTERS
            for n in range(3):
                take(("hidden", n))
                if n:
                    dve.wait_ge(hid_done, n)
                a, r = harg[0:F, 0, :], harg[0:F, 1, :]
                drain(("hidden", n), V.tensor_scalar(a, bank(("hidden", n))[0:F, 0:T], par_col("fb", n, F), par_col("freq", 0, F),
                                      ALU.add, ALU.mult))
                own.link(V.tensor_scalar(r, a, 0.15915494309189535, MAGIC, ALU.mult, ALU.add))
                own.link(V.tensor_scalar(r, r, -MAGIC, None, ALU.add))
                own.link(V.scalar_tensor_tensor(out=a, in0=r, scalar=-TWO_PI_HI, in1=a, op0=ALU.mult, op1=ALU.add))
                own.link(V.scalar_tensor_tensor(out=a, in0=r, scalar=-TWO_PI_LO, in1=a, op0=ALU.mult, op1=ALU.add))
                V.tensor_scalar(a, a, 3.1415925, -3.1415925, ALU.min, ALU.max).then_inc(hid_arg, 1)
                for it in (2 * n, 2 * n + 1):
                    dve.wait_ge(conv_mid, it + 1)
                    for m in range(2):
                        t = 2 * it + m
                        b = bank(("in0", it))[:, m * T:(m + 1) * T]
                        own.link(V.scalar_tensor_tensor(out=uc[:, t, 1:T], in0=b[:, 0:T - 1],
                                                        scalar=par_col("conv_w", t), in1=uc[:, t, 1:T],
                                                        op0=ALU.mult, op1=ALU.add))
                        ins = V.scalar_tensor_tensor(out=uc[:, t, 0:T - 1], in0=b[:, 1:T],
                                                     scalar=par_col("conv_w", 24 + t), in1=uc[:, t, 0:T - 1],
                                                     op0=ALU.mult, op1=ALU.add)
                    ins.then_inc(drained["dve"], 1)
            dve.wait_ge(con0_in, 16)
            for o in range(2):
                for tt in range(TT):
                    if o == 1 and tt == 0:
                        wait_drained("hf", 0, 1, 1)
                    f, b = bank(("filt", o, tt, 0)), bank(("filt", o, tt, 1))
                    if o + tt:
                        dve.wait_ge(filt_pm, 2 * o + tt)
                    take(("filt", o, tt, 1))
                    drain(("filt", o, tt, 0), V.tensor_tensor(tmp[:, 0, :], f, win[:, tt, 0, :], ALU.mult))
                    drain(("filt", o, tt, 1), V.tensor_tensor(tmp[:, 1, :], b, win[:, tt, 1, :], ALU.mult))
                    V.tensor_tensor(fpm[:, 0, tt, :], tmp[:, 0, :], tmp[:, 1, :], ALU.add)
                    V.tensor_tensor(fpm[:, 1, tt, :], tmp[:, 0, :], tmp[:, 1, :], ALU.subtract).then_inc(filt_pm, 1)

            ropes = [0]

            def rope(name, tiles):
                take(name)
                dve.wait_ge(filt_pm, 4)
                own.wait()
                t3 = tmp[:, 0, :].rearrange("p (a t) -> p a t", a=2)
                sin2 = sin_t.unsqueeze(1).broadcast_to([P, 2, T])
                cos2 = cos_t.unsqueeze(1).broadcast_to([P, 2, T])
                drain(name, V.tensor_tensor(t3, bank(name).rearrange("p (a t) -> p a t", a=2), sin2, ALU.mult))
                own.link(V.tensor_tensor(tiles, tiles, cos2, ALU.mult))
                V.tensor_tensor(tiles, tiles, t3, ALU.add).then_inc(roped, 1)
                ropes[0] += 1
                dve.wait_ge(roped, ropes[0])

            def decay_arg(hh):
                d = dec[:, hh % 2, :]
                own.link(V.tensor_scalar(d, dist[:, 0, :, :].rearrange("p a t -> p (a t)"),
                                         lgn[:, hh:hh + 1], None, ALU.mult))
                V.scalar_tensor_tensor(out=d, in0=dist[:, 1, :, :].rearrange("p a t -> p (a t)"),
                                       scalar=lgn[:, 8 + hh:9 + hh], in1=d, op0=ALU.mult,
                                       op1=ALU.add).then_inc(dec_arg, 1)

            dve.wait_ge(lg_done, 1)
            for o in range(2):
                if o == 0:
                    for n in range(4):
                        rope(("rot0", n), qk[:, 2 * n:2 * n + 2, :])
                wait_drained("hf", o, 1, 1)
                for kt in range(2):
                    take(("zf", o, kt, 1))
                    zr, zi = bank(("zf", o, kt, 0)), bank(("zf", o, kt, 1))
                    hr, hi = hf[:, o, kt, 0, :], hf[:, o, kt, 1, :]
                    if o == 1 and kt == 0:
                        dve.wait_ge(psum_full, jobs.number[("conv", 0, 1)] + 1)
                    V.tensor_tensor(yf[:, kt, 0, :], zr, hr, ALU.mult)
                    own.link(V.tensor_tensor(tmp[:, 0, :], zi, hi, ALU.mult))
                    V.tensor_tensor(yf[:, kt, 0, :], yf[:, kt, 0, :], tmp[:, 0, :], ALU.subtract)
                    V.tensor_tensor(yf[:, kt, 1, :], zr, hi, ALU.mult)
                    own.link(V.tensor_tensor(tmp[:, 1, :], zi, hr, ALU.mult))
                    dve.sem_inc(drained["dve"], 2)
                    V.tensor_tensor(yf[:, kt, 1, :], yf[:, kt, 1, :], tmp[:, 1, :], ALU.add).then_inc(yf_done, 1)
                if o:
                    wait_drained("ret_s", 2)
                decay_arg(4 * o)
                for hh in range(4 * o, 4 * o + 4):
                    if hh % 4 < 3:
                        if hh:
                            wait_drained("ret_s", hh - 1)
                        decay_arg(hh + 1)
                    take(("ret_s", hh))
                    dve.wait_ge(dec_exp, hh + 1)
                    if o == 1:
                        dve.wait_ge(psum_full, jobs.number[("ret_y", hh // 2 - 2)] + 1)
                    V.tensor_tensor(prob[:, hh % 4, :, :].rearrange("p a t -> p (a t)"), bank(("ret_s", hh)),
                                    dec[:, hh % 2, :], ALU.mult).then_inc(drained["dve"], 1)
                for n in range(2):
                    take(("conv", o, n))
                    dve.wait_ge(yf_done, 2 * (o + 1)) if n == 0 else wait_drained("conv", o, 0)
                    for b in range(2):
                        c = 2 * n + b
                        z = zc[:, c, :]
                        own.link(V.scalar_tensor_tensor(out=tmp[:, b, 0:T], in0=z, scalar=par_col("skip", 4 * o + c),
                                                        in1=bank(("conv", o, n))[:, b * T:(b + 1) * T],
                                                        op0=ALU.mult, op1=ALU.add))
                        last = V.tensor_tensor(z if o == 0 else cat[:, c, :], tmp[:, b, 0:T], uc[:, 4 + 4 * o + c, :],
                                               ALU.mult)
                    last.then_inc(drained["dve"], 1)
            dve.wait_ge(silu_e, 1)
            own.link(V.tensor_scalar(sig[:, :, :], sig[:, :, :], 1.0, None, ALU.add))
            own.link(V.reciprocal(sig[:, :, :], sig[:, :, :]))
            own.link(V.tensor_tensor(sig[:, :, :], sig[:, :, :], rg[:, :, :], ALU.mult))
            for n in range(2):
                wait_drained("ms_gn", n)
                own.link(V.reciprocal(gn_root(n), gn_root(n)))
                own.link(V.tensor_tensor(yr[:, 2 * n:2 * n + 2, :], yr[:, 2 * n:2 * n + 2, :],
                                         gn_root(n).rearrange("p (a t) -> p a t", a=2), ALU.mult))
                for b in range(2):
                    c = 2 * n + b
                    last = V.scalar_tensor_tensor(out=cat[:, 4 + c, :], in0=yr[:, c, :], scalar=par_col("gn", c),
                                                  in1=sig[:, c, :], op0=ALU.mult, op1=ALU.mult)
                last.then_inc(cat_done, 1)

            def residual(name, n):
                take(name)
                drain(name, V.tensor_tensor(x[:, 2 * n:2 * n + 2, :], x[:, 2 * n:2 * n + 2, :],
                                      bank(name).rearrange("p (a t) -> p a t", a=2), ALU.add))

            for n in range(EV_OUT):
                residual(("out0", n), n)

            for l in range(2):
                if l == 1:
                    norm("mix_gain", 1, "ms_mix", 1)
                    for n in range(8):
                        wait_drained("ms_head", n)
                        inv = hsq[:, 2 * n:2 * n + 2, :]
                        own.link(V.reciprocal(inv, inv))
                        g = par_col("na_gain" if n < 4 else "dil_gain", n % 4 // 2)
                        tiles = hq[:, 2 * n:2 * n + 2, :]
                        V.scalar_tensor_tensor(out=tiles, in0=tiles, scalar=g, in1=inv, op0=ALU.mult,
                                               op1=ALU.mult).then_inc(head_done, 1)
                    for n in range(4):
                        rope(("rot1", n), hq[:, 8 + 2 * n:10 + 2 * n, :])
                    dve.wait_ge(bias_in, 32)
                    for u in range(16 + 1):
                        if u < 16:
                            g, hh = divmod(u, H)
                            take(("att_s", u))
                            b = bias[:, hh if g == 0 else 8, :, :]
                            drain(("att_s", u), V.tensor_tensor(s_att[:, u % 2, :, :],
                                                  bank(("att_s", u)).rearrange("p (a t) -> p a t", a=2), b, ALU.add))
                            V.tensor_reduce(st_att[:, u % 8, 0, :], s_att[:, u % 2, :, :], AX.X, ALU.max,
                                            negate=True).then_inc(s_biased, 1)
                        if u >= 1:
                            w = u - 1
                            dve.wait_ge(s_exp, w + 1)
                            own.link(V.reciprocal(st_att[:, w % 8, 2, :], st_att[:, w % 8, 1, :]))
                            for a in range(2):
                                last = V.tensor_scalar(p_att[:, w % 2, a, :], p_att[:, w % 2, a, :],
                                                       st_att[:, w % 8, 2, a:a + 1], None, ALU.mult)
                            last.then_inc(p_normed, 1)
                    for n in range(OD_OUT):
                        residual(("out1", n), n)

                norm("ffn_gain", l, "ms_ffn", l)
                for n in range(0, 8, 2):
                    take(("sc", l, n))
                    tt, quad = n // 4, n // 2 % 2
                    q0 = (tt * 8 + 4 * quad) * KEYS
                    drain(("sc", l, n), V.tensor_copy(sc[:, 0, q0:q0 + 4 * KEYS], bank(("sc", l, n))))
                wait_drained("sc", l, 7)

                with dve.Fori(0, 16) as q:
                    own.enter(q, 7)
                    own.drain_after(V.tensor_copy(cur[:, :, :], sc[:, :, bass.ds(q * KEYS, KEYS)]))

                    def top16(values, rest, best, index):
                        own.drain_after(V.max(best[:, 0:8], values))
                        V.max_index(index[:, 0:8], best[:, 0:8], values)
                        own.drain_after(V.match_replace(rest, best[:, 0:8], values, -3.0e38))
                        own.drain_after(V.max(best[:, 8:16], rest))
                        return V.max_index(index[:, 8:16], best[:, 8:16], rest)

                    for s in range(2):
                        ins = top16(cur[:, s, :], cut[:, s, :], top_s[:, s, :], top_i[:, s, :])
                    own.link(ins)
                    V.tensor_copy(top_f[:, :, :], top_i[:, :, :])
                    own.drain_after(V.tensor_tensor(cand.rearrange("p (a b) -> p a b", a=16),
                                             top_s[:, 0, :].unsqueeze(2).broadcast_to([P, 16, 16]),
                                             top_s[:, 1, :].unsqueeze(1).broadcast_to([P, 16, 16]), ALU.add))
                    own.link(top16(cand, cand2, g16, pick))
                    V.tensor_copy(gs[:, bass.ds(q * 16, 16)], g16)
                    V.tensor_scalar(pab[:, 0, :], pick, 4, None, ALU.logical_shift_right)
                    own.link(V.tensor_scalar(pab[:, 1, :], pick, 15, None, ALU.bitwise_and))
                    own.link(V.tensor_copy(pabf[:, :, :], pab[:, :, :]))
                    io = iota[:, 0:16].unsqueeze(1).broadcast_to([P, 16, 16])
                    for s in range(2):
                        last = V.tensor_tensor(look[:, s, :, :], io,
                                               pabf[:, s, :].unsqueeze(2).broadcast_to([P, 16, 16]), ALU.is_equal)
                    own.link(last)
                    for s in range(2):
                        last = V.tensor_tensor(look[:, s, :, :], look[:, s, :, :],
                                               top_f[:, s, :].unsqueeze(1).broadcast_to([P, 16, 16]), ALU.mult)
                    own.link(last)
                    own.link(V.tensor_reduce(ijs[:, :, bass.ds(q * 16, 16)], look[:, :, :, :], AX.X, ALU.add))
                own.leave(16)

                g3 = gs.rearrange("p (q k) -> p q k", k=16)
                e3 = ge.rearrange("p (q k) -> p q k", k=16)
                V.tensor_tensor(e3, g3, g3[:, :, 0:1].broadcast_to([P, 16, 16]), ALU.subtract).then_inc(gate_arg, 1)
                dve.wait_ge(gate_exp, l + 1)
                own.link(V.tensor_reduce(gsum, e3, AX.X, ALU.add))
                own.link(V.reciprocal(gsum, gsum))
                own.link(V.tensor_tensor(g3, e3, gsum.unsqueeze(2).broadcast_to([P, 16, 16]), ALU.mult))
                dve.sem_inc(gates_done, 1)
                for n in range(3):
                    take(("gt", l, n))
                    drain(("gt", l, n), V.tensor_copy(gij[:, n, :], ps[:, (6 + n) % 8, 0:T]))

                turns = T // (GB * ABT)

                def onehot_pair(q, t0):
                    for k in range(ABT):
                        t = t0 + k
                        V.tensor_scalar(ab[:, q % 2, 0, k, :], iota, gij[:, 1, bass.ds(t, 1)], gij[:, 0, bass.ds(t, 1)],
                                        ALU.is_equal, ALU.mult)
                        last = V.tensor_scalar(ab[:, q % 2, 1, k, :], iota, gij[:, 2, bass.ds(t, 1)], None,
                                               ALU.is_equal)
                    last.then_inc(onehots, 1)

                def gate_tiles(q, i):
                    dve.wait_ge(gate_full, i * GB + (l * turns * GB + q + 1))
                    c = coef[:, 0:RUN, bass.ds(i * (GB * ABT) + q * ABT, ABT)]
                    V.tensor_tensor(c, c, ps[:, q, :].rearrange("p (t j) -> p j t", t=ABT)[:, 0:RUN, :],
                                    ALU.mult).then_inc(gate_mult, 1)

                dve.wait_ge(gelu_done, 2 + l * KEYS + RUN)
                with dve.Fori(0, turns) as i:
                    for q in range(GB):
                        if q >= 2:
                            dve.wait_ge(gate_full, i * GB + (l * turns * GB + q - 1))
                        onehot_pair(q, i * (GB * ABT) + q * ABT)
                        if q >= 1:
                            gate_tiles(q - 1, i)
                    gate_tiles(GB - 1, i)
                dve.wait_ge(gate_free, (l + 1) * turns * GB + GB)
                V.memset(ab[:, 0, 0, 0, :], 0.0).then_inc(onehots, 1)

                with dve.Fori(0, (KEYS - RUN) // 2) as j:
                    for b in range(2):
                        dve.wait_ge(gelu_done, j * 2 + (2 + l * KEYS + RUN + b + 1))
                        c = coef[:, bass.ds(2 * j + (RUN + b), 1), :].rearrange("p a t -> p (a t)")
                        V.tensor_tensor(c, c, gtmp[:, b, :], ALU.mult).then_inc(coef_done, 1)
                dve.wait_ge(v_used, (l + 1) * (KEYS // 2))
                for b in range(4):
                    last = V.tensor_tensor(x[:, 2 * b:2 * b + 2, :], x[:, 2 * b:2 * b + 2, :],
                                           ps[:, b, :].rearrange("p (a t) -> p a t", a=2), ALU.add)
                own.link(last)
                dve.sem_inc(acc_read, 1)




def _constants():
    import numpy as np

    f = np.float32
    t = np.arange(T)
    inv = (10000.0 ** (-np.arange(0, HD, 2, dtype=f) / HD)).astype(f)
    ang = (t.astype(f)[:, None] * inv[None, :]).astype(f)
    cos = np.tile(np.cos(ang).T, (4, 1))
    sin = np.tile(np.sin(ang).T, (4, 1))
    rot = np.zeros((P, P))
    for b in (0, HD):
        for k in range(HD // 2):
            rot[b + HD // 2 + k, b + k] = -1.0
            rot[b + k, b + HD // 2 + k] = 1.0
    same_head = np.kron(np.eye(2), np.full((HD, HD), 1.0 / HD))
    consts = np.concatenate([np.eye(P), rot, np.full((P, P), 1.0 / D), same_head,
                             np.tile(np.arange(P), (P, 1)), cos, sin], axis=1)
    bands = (EMB - 1) // 2
    t_norm = np.linspace(0.0, 1.0, T, dtype=f)[:, None]
    w = (2.0 * np.pi * np.arange(T, dtype=f)[:, None] / T).astype(f)
    fb = np.linspace(1e-4, bands - 1, bands, dtype=f)[None, :]
    e = np.concatenate([t_norm, np.cos(fb * w), -np.sin(fb * w)], axis=-1)
    emb = np.zeros((P, T))
    emb[:EMB] = e.T
    lo, hi = np.log(1e-2) / 1.5, np.log(1e-2) / 0.3
    deltas = np.abs(np.linspace(lo, hi, GW, dtype=f))
    win = np.exp(-t_norm * deltas[None, :]) + 0.05
    win_b = win.copy()
    win_b[0] = 0.0
    ph = np.pi * np.outer(t, 2 * t + 1) / (2 * T)
    dft = np.concatenate([np.cos(ph), -np.sin(ph)], axis=1)
    idft = np.stack([np.cos(ph).T, -np.sin(ph).T]) / T
    dft_s = dft.reshape(TT, P, 2 * T).transpose(1, 0, 2).reshape(P, -1)
    idft_s = idft.reshape(2, 2, P, T).transpose(2, 1, 0, 3).reshape(P, -1)
    win_s = np.stack([win, win_b]).reshape(2, TT, P, GW).transpose(2, 1, 0, 3).reshape(P, -1)
    m = np.arange(T).reshape(TT, P)
    ahead = np.maximum(t[None, None, :] - m[:, :, None], 0)
    behind = np.maximum(m[:, :, None] - t[None, None, :], 0)
    dist = np.stack([ahead, behind]).transpose(2, 0, 1, 3).reshape(P, -1)
    con0 = np.concatenate([emb, dft_s, idft_s, win_s, dist], axis=1)
    q, k = t[:, None], t[None, :]
    seen = np.zeros((T, T))
    for window, dil in ((128, 1), (512, 4), (2048, 16)):
        seen += (q % dil == k % dil) & (np.abs(q // dil - k // dil) <= window // (2 * dil))
    merged = np.where(seen > 0, np.log(np.maximum(seen, 1)), NEG)
    con1 = merged.reshape(TT, P, T).transpose(1, 0, 2)
    return [np.ascontiguousarray(a, dtype=f) for a in (consts, con0, con1)]


def kernel(**inputs):
    import numpy as np
    import concourse.bacc as bacc
    from concourse.bass_utils import run_bass_kernel_spmd as run

    a = {k: np.asarray(v) for k, v in inputs.items()}

    def chunks(v):
        return np.ascontiguousarray(v.reshape(-1, P).T)

    def blocks(w):
        n = w.shape[1] // T
        return np.ascontiguousarray(w.reshape(DC, P, n, T).transpose(2, 1, 0, 3).reshape(n, P, BLK))

    def rows(v):
        out = np.zeros((P, v.shape[1]), v.dtype)
        out[:v.shape[0]] = v
        return out

    def twice(v):
        return np.concatenate([v.T, v.T], axis=0)

    par = np.concatenate([
        chunks(a["mix_norm_gain"]), chunks(a["ffn_norm_gain"]), chunks(a["hy_conv_w"][0]), chunks(a["hy_conv_b"][0]),
        chunks(a["hy_skip"][0]), chunks(a["ret_gn_gain"][0]), twice(a["na_qk_gain"][0]), twice(a["dil_qk_gain"][0]),
        rows(np.stack([a["hy_fb1"][0], a["hy_fb2"][0], a["hy_fb3"][0], a["hy_freq"][0]], axis=1)),
        np.tile(a["ret_log_decay"][0].reshape(1, 16), (P, 1)),
        rows(a["hy_fw1"][0]), rows(a["hy_fw2"][0]), rows(a["hy_fw3"][0])], axis=1)
    assert par.shape[1] == NPAR
    consts, con0, con1 = _constants()

    rows_, cols = T // 64, 64
    r, c = np.arange(rows_), np.arange(cols)
    c0 = np.clip(c - 8, 0, cols - 16)
    valid = (c[None, :] >= c0[:, None]) & (c[None, :] < c0[:, None] + 16)
    row_off = r[None, :] - r[:, None] + 7
    col_off = np.clip(c[None, :] - c[:, None] + 15, 0, 30)
    b = a["na_rpb"][0][:, row_off[:, None, :, None], col_off[None, :, None, :]]
    b = np.where(valid[None, None, :, None, :], b, np.float32(NEG)).reshape(8, TT, P, T)
    na_bias = np.ascontiguousarray(b.transpose(2, 0, 1, 3))

    w_in = a["ev_w_in"][0]
    ev = blocks(w_in)[[0, 1, 2, 3, 4, 5, 6, 7, 10, 11, 8, 9, 12, 13]]
    subk = np.ascontiguousarray(a["peer_sub_keys"].transpose(0, 2, 4, 1, 3).reshape(2, P, 8, KEYS))
    u_t = a["peer_u"].reshape(2, KEYS, KEYS // 2, 2, DC, P).transpose(0, 2, 5, 3, 4, 1).reshape(2, KEYS // 2, P, BLK)
    v_t = a["peer_v"].reshape(2, KEYS, KEYS // 2, 2, D).transpose(0, 2, 1, 3, 4).reshape(2, KEYS // 2, P, BLK)
    arrays = {
        "xT": a["x"][0].T.reshape(DC, P, T).transpose(1, 0, 2), "par": par, "consts": consts, "con0": con0,
        "con1": con1, "subk": subk, "w_ev_in": ev, "w_ev_out": blocks(a["ev_w_out"][0]),
        "w_od_in": blocks(a["od_w_in"][0]), "w_od_out": blocks(a["od_w_out"][0]),
        "w_q": np.stack([blocks(a["peer_w_q"][0]), blocks(a["peer_w_q"][1])]), "fw_out": a["hy_fw_out"][0],
        "na_bias": na_bias, "u_t": u_t, "v_t": v_t,
    }
    nc = bacc.Bacc("TRN2", target_bir_lowering=False, num_devices=1)
    args = {}
    for name, v in arrays.items():
        arrays[name] = np.ascontiguousarray(v)
        args[name] = nc.dram_tensor(name, v.shape, F32, kind="ExternalInput").ap()
    out = nc.dram_tensor("out", (P, DC, T), F32, kind="ExternalOutput").ap()
    hybrid_trunk(nc, out=out, **args)
    got = run(nc, [arrays], core_ids=[0]).results[0]["out"]
    return np.ascontiguousarray(got.transpose(1, 0, 2).reshape(D, T).T)[None]
```

```python
from contextlib import ExitStack

import concourse.bass as bass
from concourse import mybir
from concourse.alu_op_type import AluOpType as ALU

F32 = mybir.dt.float32
F32R = mybir.dt.float32r
U32 = mybir.dt.uint32
ACT = mybir.ActivationFunctionType
AX = mybir.AxisListType

P = 128
D = 1024
DC = D // P
T = 256
TT = T // P
GW = 512
GC = GW // P
HD = 64
H = 8
EPS = 1e-6
NEG = -1e30
RING = 4
TILE = 1024
PARTS = 4
HALF = TILE // 2
KEYS = 128
RUN = 64
EARLY = 60
ABT = 2
ABN = 4
GB = 4
BT = 2 * ABT
TURNS = T // (GB * BT)

EV_IN, EV_OUT, OD_IN, OD_OUT, WQ = 14, 4, 12, 4, 4
HY_FILTERS = 64
EMB = 33

PAR = {}


def par_columns():
    at = 0
    for name, n in (("mix_gain", 2 * DC), ("ffn_gain", 2 * DC), ("conv_w", 3 * 12), ("conv_b", 12), ("skip", 8),
                    ("gn", GC), ("na_gain", 2), ("dil_gain", 2), ("fb", 3), ("freq", 1), ("decay", 16),
                    ("fw1", 64), ("fw2", 64), ("fw3", 64)):
        PAR[name] = at
        at += n
    return at


NPAR = par_columns()


def stream():
    starts, n = {}, 0
    for name, tiles in (("in0", 2 * EV_IN), ("out0", 2 * EV_OUT), ("q0", 2 * WQ), ("experts0", 2 * KEYS),
                        ("in1", 2 * OD_IN), ("out1", 2 * OD_OUT), ("q1", 2 * WQ), ("experts1", 2 * KEYS)):
        starts[name] = n
        n += tiles
    return starts, n


STARTS, TILES = stream()


class Jobs:

    def __init__(self):
        self.number, self.who, self.rank, self.total = {}, [], [], {"act": 0, "dve": 0}
        self.whole, self.others = {}, 0

    def add(self, name, who, tile=None):
        self.number[name] = len(self.who)
        self.who.append(who)
        self.total[who] += 1
        self.rank.append(self.total[who])
        if tile is None:
            self.others += 1
            self.whole[name] = "psum_full", self.others
        else:
            self.whole[name] = "half_used", 2 * tile + 2

    def project(self, name, who):
        part, k = (f"q{name[1]}", name[2]) if name[0] == "q" else name
        self.add(name, who, STARTS[part] + 2 * k + 1)

    def bank(self, name):
        return self.number[name] % 8

    def drained(self, name):
        n = self.number[name]
        return self.who[n], self.rank[n]


def plan():
    jobs = Jobs()
    add = jobs.add
    add(("ms_mix", 0), "act")
    for n in range(3):
        add(("hidden", n), "dve")
        for it in (2 * n, 2 * n + 1):
            jobs.project(("in0", it), "dve")
    for o in range(2):
        for tt in range(TT):
            add(("filt", o, tt, 0), "dve")
            add(("filt", o, tt, 1), "dve")
        for it in (6 + 4 * o, 7 + 4 * o):
            jobs.project(("in0", it), "act")
        for kt in range(2):
            for ri in range(2):
                add(("hf", o, kt, ri), "act")
        for it in (8 + 4 * o, 9 + 4 * o):
            jobs.project(("in0", it), "act")
    for o in range(2):
        for tt in range(TT):
            add(("zt", o, tt), "act")
        if o == 0:
            for n in range(4):
                add(("rot0", n), "dve")
        for kt in range(2):
            for ri in range(2):
                add(("zf", o, kt, ri), "dve")
        for h in range(4 * o, 4 * o + 4):
            add(("ret_s", h), "dve")
        for n in range(2):
            add(("conv", o, n), "dve")
        for n in (2 * o, 2 * o + 1):
            add(("ret_y", n), "act")
    for n in range(2):
        add(("ms_gn", n), "act")
    for n in range(EV_OUT):
        jobs.project(("out0", n), "dve")
    for l in range(2):
        if l == 1:
            add(("ms_mix", 1), "act")
            for it in range(OD_IN):
                jobs.project(("in1", it), "act")
            for n in range(8):
                add(("ms_head", n), "act")
            for n in range(4):
                add(("rot1", n), "dve")
            for u in range(16 + 2):
                if u < 16:
                    add(("att_s", u), "dve")
                if u >= 1 and u <= 16:
                    add(("att_t", u - 1), "act")
                if u >= 2 and (u - 2) % 2 == 1:
                    add(("att_o", (u - 2) // 2), "act")
            for n in range(OD_OUT):
                jobs.project(("out1", n), "dve")
        add(("ms_ffn", l), "act")
        for n in range(WQ):
            jobs.project(("q", l, n), "act")
        for n in range(8):
            add(("sc", l, n), "act" if n % 2 else "dve")
        for n in range(3):
            add(("gt", l, n), "dve")
    return jobs


class Chain:

    def __init__(self, eng, sem):
        self.eng, self.sem, self.n, self.turn, self.per, self.k = eng, sem, 0, None, 0, 0

    def link(self, ins):
        ins.then_inc(self.sem, 1)
        if self.turn is None:
            self.n += 1
            self.eng.wait_ge(self.sem, self.n)
        else:
            self.k += 1
            self.eng.wait_ge(self.sem, self.turn * self.per + (self.n + self.k))

    def drain_after(self, ins):
        self.eng.drain()

    def wait(self):
        self.eng.wait_ge(self.sem, self.n)

    def enter(self, turn, per):
        self.turn, self.per, self.k = turn, per, 0

    def leave(self, turns):
        assert self.k == self.per, (self.k, self.per)
        self.n += turns * self.per
        self.turn = None


def hybrid_trunk(nc, xT, par, consts, con0, con1, subk, w_ev_in, w_ev_out, w_od_in, w_od_out, w_q, fw_out,
                 na_bias, u_t, v_t, out, dbg=None):
    jobs = plan()
    ctx = ExitStack()
    with ctx:
        def sb(name, shape, dt=F32):
            return ctx.enter_context(nc.sbuf_tensor(name, shape, dt))

        def sem(name):
            return ctx.enter_context(nc.semaphore(name))

        x = sb("x", [P, DC, T])
        rhs = sb("rhs", [P, 2, DC, T], F32R)
        ring = sb("ring", [P, RING, TILE])
        parts = sb("parts", [P, PARTS, 2, HALF], F32R)
        cparts = sb("cparts", [P, 2, 2, T], F32R)
        big = sb("big", [P, KEYS * T])
        coef = big[:, :].rearrange("p (j t) -> p j t", t=T)
        pa = sb("pa", [P, NPAR])
        cst = sb("cst", [P, 5 * P + 2 * T])
        ident, rot_m, ones_d, ones_h, iota = (cst[:, k * P:(k + 1) * P] for k in range(5))
        cos_t = cst[:, 5 * P:5 * P + T]
        sin_t = cst[:, 5 * P + T:5 * P + 2 * T]
        ab = sb("ab", [P, ABN, 2, ABT, P])
        gij = sb("gij", [P, 3, T])
        gtmp = sb("gtmp", [P, 2, T])
        rs = gtmp[:, :, :].rearrange("p a t -> p (a t)")
        eps = sb("eps", [P, 2])
        lgn = sb("lgn", [P, 16])

        at = [0]

        def carve(n, start=None):
            if start is not None:
                at[0] = start
            ap = big[:, at[0]:at[0] + n]
            at[0] += n
            assert at[0] <= KEYS * T, at[0]
            return ap

        h = carve(DC * T, 0).rearrange("p (c t) -> p c t", t=T)
        uc = carve(12 * T, 0).rearrange("p (m t) -> p m t", t=T)
        qk = carve(8 * T).rearrange("p (m t) -> p m t", t=T)
        v0 = carve(TT * GW).rearrange("p (a c) -> p a c", a=TT)
        rg = carve(GC * T).rearrange("p (m t) -> p m t", t=T)
        hid = carve(T)
        harg = carve(2 * T).rearrange("p (a t) -> p a t", a=2)
        fpm = carve(4 * GW).rearrange("p (s a c) -> p s a c", s=2, a=TT)
        hf = carve(8 * GW).rearrange("p (o k r c) -> p o k r c", o=2, k=2, r=2)
        fwo = carve(4 * GW)
        zt = carve(TT * GW).rearrange("p (a c) -> p a c", a=TT)
        yf = carve(4 * GW).rearrange("p (k r c) -> p k r c", k=2, r=2)
        tmp = carve(2 * GW).rearrange("p (a c) -> p a c", a=2)
        cat = carve(DC * T).rearrange("p (m t) -> p m t", t=T)
        dec = carve(2 * GW).rearrange("p (a c) -> p a c", a=2)
        prob = carve(4 * GW).rearrange("p (b a t) -> p b a t", b=4, a=2)
        sig = carve(GC * T).rearrange("p (m t) -> p m t", t=T)
        con0_s = carve(256 + 1024 + 1024 + 2048 + 1024)
        emb = con0_s[:, 0:256]
        dft = con0_s[:, 256:1280].rearrange("p (a k) -> p a k", a=TT)
        idft = con0_s[:, 1280:2304].rearrange("p (r t) -> p r t", t=T)
        win = con0_s[:, 2304:4352].rearrange("p (a d c) -> p a d c", a=TT, d=2)
        dist = con0_s[:, 4352:5376].rearrange("p (d a t) -> p d a t", d=2, a=2)
        yr = hf[:, 0, :, :, :].rearrange("p k r c -> p (k r c)")[:, 0:GC * T].rearrange("p (m t) -> p m t", t=T)
        ysq = hf[:, 0, :, :, :].rearrange("p k r c -> p (k r c)")[:, GC * T:2 * GC * T].rearrange("p (m t) -> p m t", t=T)
        zc = uc[:, 0:4, :]

        def gn_root(n):
            return ysq[:, 2 * n:2 * n + 2, :].rearrange("p a t -> p (a t)")

        hq = carve(16 * T, 0).rearrange("p (m t) -> p m t", t=T)
        hsq = carve(16 * T).rearrange("p (m t) -> p m t", t=T)
        v1 = carve(2 * TT * GW).rearrange("p (g a c) -> p g a c", g=2, a=TT)
        bias = carve(9 * 2 * T).rearrange("p (h a t) -> p h a t", h=9, a=2)
        s_att = carve(2 * 2 * T).rearrange("p (b a t) -> p b a t", b=2, a=2)
        p_att = carve(2 * 2 * T).rearrange("p (b a t) -> p b a t", b=2, a=2)
        pt_att = carve(2 * 2 * T).rearrange("p (b a t) -> p b a t", b=2, a=2)
        cat1 = carve(DC * T).rearrange("p (m t) -> p m t", t=T)
        st_att = carve(64).rearrange("p (b s a) -> p b s a", b=8, s=4)

        qT = carve(8 * T, RUN * T).rearrange("p (m t) -> p m t", t=T)
        sc = carve(2 * 16 * KEYS).rearrange("p (s c) -> p s c", s=2)
        cur = carve(4 * KEYS).rearrange("p (s e c) -> p s e c", s=2, e=2)
        cut = carve(4 * KEYS).rearrange("p (s e c) -> p s e c", s=2, e=2)
        top_s = carve(64).rearrange("p (s e c) -> p s e c", s=2, e=2)
        top_i = carve(64).bitcast(U32).rearrange("p (s e c) -> p s e c", s=2, e=2)
        top_f = carve(64).rearrange("p (s e c) -> p s e c", s=2, e=2)
        cand = carve(512).rearrange("p (e c) -> p e c", e=2)
        cand2 = carve(512).rearrange("p (e c) -> p e c", e=2)
        g16 = carve(32).rearrange("p (e c) -> p e c", e=2)
        pick = carve(32).bitcast(U32).rearrange("p (e c) -> p e c", e=2)
        pab = carve(64).bitcast(U32).rearrange("p (s c) -> p s c", s=2)
        pabf = carve(64).rearrange("p (s c) -> p s c", s=2)
        look = carve(1024).rearrange("p (s e k a) -> p s e k a", s=2, e=2, k=16)
        gs = carve(256)
        ijs = carve(512).rearrange("p (s c) -> p s c", s=2)
        ge = carve(256)
        gsum = carve(16)
        assert at[0] <= KEYS * T - 1024
        sk = big[:, KEYS * T - 1024:KEYS * T].rearrange("p (h k) -> p h k", h=8)

        ps = ctx.enter_context(nc.psum_tensor("ps", [P, 8, 512], F32))

        def bank(name):
            return ps[:, jobs.bank(name), :]

        x_in = sem("x_in")
        par_in = sem("par_in")
        cst_in = sem("cst_in")
        con0_in = sem("con0_in")
        fwo_in = sem("fwo_in")
        sk_in = sem("sk_in")
        bias_in = sem("bias_in")
        out_done = sem("out_done")
        full = [sem(f"tile_in{s}") for s in range(RING)]
        hi_done = sem("hi_done")
        lo_done = sem("lo_done")
        half_used = sem("half_used")
        rhs_hi = sem("rhs_hi")
        rhs_lo = sem("rhs_lo")
        chi_done = sem("chi_done")
        clo_done = sem("clo_done")
        psum_full = sem("psum_full")
        drained = {"act": sem("drained_by_act"), "dve": sem("drained_by_dve")}
        dve_own = sem("dve_own")
        consts_set = sem("consts_set")
        squared = sem("squared")
        normed = sem("normed")
        hid_arg = sem("hid_arg")
        hid_done = sem("hid_done")
        conv_mid = sem("conv_mid")
        filt_pm = sem("filt_pm")
        yf_done = sem("yf_done")
        roped = sem("roped")
        dec_arg = sem("dec_arg")
        dec_exp = sem("dec_exp")
        lg_done = sem("lg_done")
        ysq_done = sem("ysq_done")
        silu_e = sem("silu_e")
        cat_done = sem("cat_done")
        head_done = sem("head_done")
        s_biased = sem("s_biased")
        s_exp = sem("s_exp")
        p_normed = sem("p_normed")
        gate_arg = sem("gate_arg")
        gate_exp = sem("gate_exp")
        gates_done = sem("gates_done")
        gelu_done = sem("gelu_done")

        plain_i = sem("plain_i")
        weighted_i = sem("weighted_i")
        onehots = sem("onehots")
        onehots_used = sem("onehots_used")
        gate_full = sem("gate_full")
        gate_mult = sem("gate_mult")
        gate_free = sem("gate_free")
        coef_done = sem("coef_done")
        acc_read = sem("acc_read")

        block = ctx.enter_context(nc.Block())

        def par_col(name, k=0, rows=P):
            return pa[0:rows, PAR[name] + k:PAR[name] + k + 1]

        def whole(name):
            which, count = jobs.whole[name]
            return (psum_full if which == "psum_full" else half_used), count

        assert 2 * RUN == KEYS and RING == 4 and PARTS == 4

        def part_a(l):
            return STARTS[f"experts{l}"]

        def part_b(l):
            return part_a(l) + RUN

        def part_c(l):
            return part_b(l) + 2 * (KEYS - RUN)

        def at_half(i, per, n, half):
            return i * (2 * per) + (2 * n + half + 1)

        @block.sync
        def _(sp):
            def load(n, src):
                if n >= RING:
                    sp.wait_ge(lo_done, 2 * (n - RING) + 2)
                sp.dma_start(ring[:, n % RING, :], src).then_inc(full[n % RING], 16)

            def load_part(name, w, first=0):
                for k in range(first, w.shape[0]):
                    load(STARTS[name] + k, w[k])

            sp.dma_start(x[:, :, :], xT).then_inc(x_in, 16)
            load_part("in0", w_ev_in)
            load_part("out0", w_ev_out)
            for l in range(2):
                if l == 1:
                    for k in range(RING):
                        load(STARTS["in1"] + k, w_od_in[k])
                    sp.wait_ge(acc_read, 1)
                    sp.dma_start(bias[:, 0:8, :, :], na_bias).then_inc(bias_in, 16)
                    sp.dma_start(bias[:, 8, :, :], con1).then_inc(bias_in, 16)
                    sp.dma_start(sk[:, :, :], subk[1]).then_inc(bias_in, 16)
                    load_part("in1", w_od_in, RING)
                    load_part("out1", w_od_out)
                load_part(f"q{l}", w_q[l])

                def experts(first, turns, order):
                    with sp.Fori(0, turns) as i:
                        for k, (table, base, step) in enumerate(order):
                            sp.wait_ge(lo_done, at_half(i, RING, first + k - RING, 1))
                            src = table[l, bass.ds(i * step + base, 1), :, :].rearrange("a p n -> p (a n)")
                            sp.dma_start(ring[:, (first + k) % RING, :], src).then_inc(full[(first + k) % RING], 16)

                experts(part_a(l), RUN // RING, [(u_t, k, RING) for k in range(RING)])
                experts(part_b(l), (KEYS - RUN) // 2, [(u_t, RUN, 2), (v_t, 0, 2), (u_t, RUN + 1, 2), (v_t, 1, 2)])
                experts(part_c(l), RUN // RING, [(v_t, KEYS - RUN + k, RING) for k in range(RING)])
            sp.wait_ge(acc_read, 2)
            sp.dma_start(out, x[:, :, :]).then_inc(out_done, 16)
            sp.wait_ge(out_done, 16)

        @block.gpsimd
        def _(pool):
            pool.dma_start(pa[:, :], par).then_inc(par_in, 16)
            pool.dma_start(cst[:, :], consts).then_inc(cst_in, 16)
            pool.dma_start(con0_s[:, :], con0).then_inc(con0_in, 16)
            pool.dma_start(fwo[0:HY_FILTERS, :], fw_out).then_inc(fwo_in, 16)
            pool.dma_start(sk[:, :, :], subk[0]).then_inc(sk_in, 16)

            def low_part(i, n, half):
                pool.wait_ge(hi_done, at_half(i, RING, n, half))
                p = parts[:, (2 * n + half) % PARTS, :, :]
                pool.tensor_tensor(p[:, 1, :], ring[:, n % RING, half * HALF:(half + 1) * HALF],
                                   p[:, 0, :].bitcast(F32), ALU.subtract).then_inc(lo_done, 1)

            def low_parts(first, end):
                turns = (end - first) // RING
                with pool.Fori(0, turns) as i:
                    for k in range(RING):
                        for half in range(2):
                            low_part(i, first + k, half)
                for n in range(first + turns * RING, end):
                    for half in range(2):
                        low_part(0, n, half)

            first = 0
            for l in range(2):
                low_parts(first, part_b(l) + 2)
                first = part_b(l) + 2
                with pool.Fori(0, TURNS) as i:
                    for g in range(2 * GB):
                        pool.wait_ge(plain_i, i * (2 * GB) + (l * TURNS * 2 * GB + g + 1))
                        a = ab[:, g % ABN, 0, :, :]
                        gates = gij[:, 0, bass.ds(i * (GB * BT) + g * ABT, ABT)]
                        pool.tensor_tensor(a, a, gates.unsqueeze(2).broadcast_to([P, ABT, P]),
                                           ALU.mult).then_inc(weighted_i, 1)
            low_parts(first, TILES)

        @block.tensor
        def _(pe):
            def begin(name):
                n = jobs.number[name]
                if n >= 8:
                    pe.wait_ge(drained[jobs.who[n - 8]], jobs.rank[n - 8])

            def wait_drained(*name):
                who, count = jobs.drained(name)
                pe.wait_ge(drained[who], count)

            def mm(o, a, b, start, stop, **kw):
                return nc.tensor.matmul(o, a, b, start=start, stop=stop, **kw)

            def product(o, w, b, start, stop, **kw):
                mm(o, w[0], b[0], start, False, **kw)
                mm(o, w[0], b[1], False, False, **kw)
                return mm(o, w[1], b[0], False, stop, **kw)

            def mean_square(name, count):
                begin(name)
                pe.wait_ge(squared, count)
                for c in range(DC):
                    last = mm(bank(name)[:, 0:T], ones_d, h[:, c, :], c == 0, c == DC - 1)
                last.then_inc(psum_full, 1)

            def project(name, transposed=True):
                begin(name)
                n = (jobs.whole[name][1] - 2) // 2 - 1
                for m in range(2):
                    for half in range(2):
                        k = 2 * (n + m) + half
                        pe.wait_ge(lo_done, k + 1)
                        w = parts[:, k % PARTS, :, :].rearrange("p s (c m) -> p s c m", m=P)
                        for c in range(4):
                            d = 4 * half + c
                            first, end = d == 0, d == DC - 1
                            wc = (w[:, 0, c, :], w[:, 1, c, :])
                            if transposed:
                                last = product(bank(name)[:, m * T:(m + 1) * T], wc,
                                               (rhs[:, 0, d, :], rhs[:, 1, d, :]), first, end)
                            else:
                                for tt in range(TT):
                                    last = product(bank(name)[:, tt * T + m * P:tt * T + (m + 1) * P],
                                                   (rhs[:, 0, d, tt * P:(tt + 1) * P],
                                                    rhs[:, 1, d, tt * P:(tt + 1) * P]), wc,
                                                   first and m == 0 and tt == 0, end, skip_group_check=True)
                        last.then_inc(half_used, 1)

            def one(name, *mms):
                begin(name)
                for o, a, b, s, e in mms:
                    last = mm(o, a, b, s, e)
                last.then_inc(psum_full, 1)

            pe.wait_ge(cst_in, 16)
            mean_square(("ms_mix", 0), 1)
            pe.wait_ge(par_in, 16)
            pe.wait_ge(con0_in, 16)
            for n in range(3):
                if n:
                    pe.wait_ge(hid_done, n)
                name = ("hidden", n)
                w = pa[0:EMB if n == 0 else HY_FILTERS, PAR["fw1"] + 64 * n:PAR["fw1"] + 64 * n + 64]
                one(name, (bank(name)[0:HY_FILTERS, 0:T], w, emb[0:EMB, :] if n == 0 else hid[0:HY_FILTERS, :],
                           True, True))
                if n == 0:
                    pe.wait_ge(rhs_lo, 2)
                for it in (2 * n, 2 * n + 1):
                    project(("in0", it))
            pe.wait_ge(hid_done, 3)
            pe.wait_ge(fwo_in, 16)
            for o in range(2):
                for tt in range(TT):
                    for d in range(2):
                        name = ("filt", o, tt, d)
                        one(name, (bank(name), hid[0:HY_FILTERS, tt * P:(tt + 1) * P],
                                   fwo[0:HY_FILTERS, (o * 2 + d) * GW:(o * 2 + d + 1) * GW], True, True))
                for it in (6 + 4 * o, 7 + 4 * o):
                    project(("in0", it))
                pe.wait_ge(filt_pm, 2 * (o + 1))
                for kt in range(2):
                    for ri in range(2):
                        name = ("hf", o, kt, ri)
                        one(name, *((bank(name), dft[:, tt, ri * T + kt * P:ri * T + (kt + 1) * P],
                                     fpm[:, ri, tt, :], tt == 0, tt == TT - 1) for tt in range(TT)))
                for it in (8 + 4 * o, 9 + 4 * o):
                    project(("in0", it), transposed=(o == 1))

            def retention_scores(hh):
                name = ("ret_s", hh)
                o64 = 64 * (hh % 2)
                one(name, *((bank(name)[:, a * T:(a + 1) * T], qk[o64:o64 + 64, 4 + hh // 2, a * P:(a + 1) * P],
                             qk[o64:o64 + 64, hh // 2, :], True, True) for a in range(2)))

            def retention_values(n):
                name = ("ret_y", n)
                begin(name)
                for b in range(2):
                    hh = 2 * n + b
                    wait_drained("ret_s", hh)
                    for a in range(2):
                        last = mm(bank(name)[64 * b:64 * b + 64, 0:T], v0[:, a, hh * HD:(hh + 1) * HD],
                                  prob[:, hh % 4, a, :], a == 0, a == 1)
                    last.then_inc(psum_full, 1) if b == 1 else None

            for o in range(2):
                if o == 0:
                    wait_drained("in0", 1)
                else:
                    wait_drained("conv", 0, 1)
                for tt in range(TT):
                    name = ("zt", o, tt)
                    begin(name)
                    for c in range(GC):
                        last = nc.tensor.transpose(bank(name)[:, c * P:(c + 1) * P], zc[:, c, tt * P:(tt + 1) * P],
                                                   ident)
                    last.then_inc(psum_full, 1)
                if o == 0:
                    wait_drained("in0", 11)
                    for n in range(4):
                        name = ("rot0", n)
                        one(name, (bank(name), rot_m, qk[:, 2 * n:2 * n + 2, :].rearrange("p a t -> p (a t)"),
                                   True, True))
                wait_drained("zt", o, 1)
                for kt in range(2):
                    for ri in range(2):
                        name = ("zf", o, kt, ri)
                        one(name, *((bank(name), dft[:, tt, ri * T + kt * P:ri * T + (kt + 1) * P], zt[:, tt, :],
                                     tt == 0, tt == TT - 1) for tt in range(TT)))
                pe.wait_ge(roped, 4)
                for hh in range(4 * o, 4 * o + 4):
                    retention_scores(hh)
                pe.wait_ge(yf_done, 2 * (o + 1))
                for n in range(2):
                    name = ("conv", o, n)
                    begin(name)
                    for b in range(2):
                        c = 2 * n + b
                        for r in range(4):
                            last = mm(bank(name)[:, b * T:(b + 1) * T], yf[:, r // 2, r % 2, c * P:(c + 1) * P],
                                      idft[:, r, :], r == 0, r == 3)
                    last.then_inc(psum_full, 1)
                wait_drained("in0", 9)
                for n in (2 * o, 2 * o + 1):
                    retention_values(n)
            pe.wait_ge(ysq_done, 1)
            for n in range(2):
                name = ("ms_gn", n)
                one(name, (bank(name), ones_h, ysq[:, 2 * n:2 * n + 2, :].rearrange("p a t -> p (a t)"), True, True))
            pe.wait_ge(rhs_lo, 4)
            for n in range(EV_OUT):
                project(("out0", n))

            def attention_scores(u):
                g, hh = divmod(u, H)
                name = ("att_s", u)
                o64 = 64 * (hh % 2)
                one(name, *((bank(name)[:, a * T:(a + 1) * T], hq[o64:o64 + 64, 8 * g + hh // 2, a * P:(a + 1) * P],
                             hq[o64:o64 + 64, 8 * g + 4 + hh // 2, :], True, True) for a in range(2)))

            def attention_turn(u):
                name = ("att_t", u)
                begin(name)
                pe.wait_ge(p_normed, u + 1)
                for kt in range(2):
                    for a in range(2):
                        last = nc.tensor.transpose(bank(name)[:, kt * T + a * P:kt * T + (a + 1) * P],
                                                   p_att[:, u % 2, a, kt * P:(kt + 1) * P], ident)
                last.then_inc(psum_full, 1)

            def attention_values(n):
                name = ("att_o", n)
                begin(name)
                for b in range(2):
                    u = 2 * n + b
                    g, hh = divmod(u, H)
                    wait_drained("att_t", u)
                    for kt in range(2):
                        last = mm(bank(name)[64 * b:64 * b + 64, 0:T], v1[:, g, kt, hh * HD:(hh + 1) * HD],
                                  pt_att[:, u % 2, kt, :], kt == 0, kt == 1)
                    last.then_inc(psum_full, 1) if b == 1 else None

            for l in range(2):
                if l == 1:
                    mean_square(("ms_mix", 1), 3)
                    pe.wait_ge(rhs_lo, 8)
                    for it in range(OD_IN):
                        project(("in1", it), transposed=it not in (4, 5, 10, 11))
                    for n in range(8):
                        name = ("ms_head", n)
                        wait_drained("in1", n + 2 * (n // 4))
                        one(name, (bank(name), ones_h, hsq[:, 2 * n:2 * n + 2, :].rearrange("p a t -> p (a t)"),
                                   True, True))
                    for n in range(4):
                        name = ("rot1", n)
                        pe.wait_ge(head_done, 8)
                        one(name, (bank(name), rot_m, hq[:, 8 + 2 * n:10 + 2 * n, :].rearrange("p a t -> p (a t)"),
                                   True, True))
                    for u in range(16 + 2):
                        if u < 16:
                            if u == H:
                                pe.wait_ge(roped, 8)
                            attention_scores(u)
                        if 1 <= u <= 16:
                            attention_turn(u - 1)
                        if u >= 2 and (u - 2) % 2 == 1:
                            attention_values((u - 2) // 2)
                    pe.wait_ge(rhs_lo, 10)
                    for n in range(OD_OUT):
                        project(("out1", n))

                mean_square(("ms_ffn", l), 2 + 2 * l)
                pe.wait_ge(rhs_lo, 6 + 6 * l)
                for n in range(WQ):
                    project(("q", l, n))
                wait_drained("q", l, WQ - 1)
                pe.wait_ge(bias_in, 48) if l else pe.wait_ge(sk_in, 16)
                for n in range(8):
                    tt, quad, s = n // 4, n // 2 % 2, n % 2
                    name = ("sc", l, n)
                    one(name, *((bank(name)[:, k * KEYS:(k + 1) * KEYS],
                                 qT[64 * s:64 * s + 64, 4 * quad + k, tt * P:(tt + 1) * P],
                                 sk[64 * s:64 * s + 64, 4 * quad + k, :], True, True) for k in range(4)))

                def halves(i, per, n):
                    for half in range(2):
                        pe.wait_ge(lo_done, at_half(i, per, n, half))
                        w = parts[:, (2 * n + half) % PARTS, :, :].rearrange("p s (c m) -> p s c m", m=P)
                        yield half, [(w[:, 0, c, :], w[:, 1, c, :]) for c in range(4)]

                def up(i, per, n, j, step):
                    pe.wait_ge(gelu_done, i * step + (KEYS * l + j + 1))
                    for half, w in halves(i, per, n):
                        for c in range(4):
                            d = 4 * half + c
                            last = product(ps[:, 4 + j % 2, 0:T], w[c], (rhs[:, 0, d, :], rhs[:, 1, d, :]),
                                           d == 0, d == DC - 1)
                        last.then_inc(half_used, 1)

                def down(i, per, n, v, step):
                    pe.wait_ge(clo_done, i * step + (KEYS * l + v + 1))
                    c2 = (cparts[:, v % 2, 0, :], cparts[:, v % 2, 1, :])
                    for half, w in halves(i, per, n):
                        for c in range(4):
                            d = 4 * half + c
                            last = product(ps[:, d // 2, (d % 2) * T:(d % 2 + 1) * T], w[c], c2, False, False,
                                           skip_group_check=True)
                        last.then_inc(half_used, 1)

                def up_loop(lo, hi):
                    with pe.Fori(lo, hi) as i:
                        for k in range(RING):
                            up(i, RING, part_a(l) + k, k, RING)

                wait_drained("sc", l, 6)
                wait_drained("sc", l, 7)
                up_loop(0, EARLY // RING)
                pe.wait_ge(gates_done, l + 1)
                for n in range(3):
                    name = ("gt", l, n)
                    src = gs if n == 0 else ijs[:, n - 1, :]
                    for tt in range(TT):
                        last = nc.tensor.transpose(ps[:, (6 + n) % 8, tt * P:(tt + 1) * P],
                                                   src[:, tt * P:(tt + 1) * P], ident)
                    last.then_inc(psum_full, 1)
                up_loop(EARLY // RING, RUN // RING)
                wait_drained("gt", l, 2)
                with pe.Fori(0, TURNS) as i:
                    for q in range(GB):
                        pe.wait_ge(gate_free, i * GB + (l * TURNS * GB + q + 1))
                        for b in range(2):
                            g = 2 * q + b
                            pe.wait_ge(onehots, i * (2 * GB) + (l * (TURNS * 2 * GB + 1) + g + 1))
                            pe.wait_ge(weighted_i, i * (2 * GB) + (l * TURNS * 2 * GB + g + 1))
                            for k in range(ABT):
                                t = ABT * b + k
                                last = mm(ps[:, q, t * P:(t + 1) * P], ab[:, g % ABN, 0, k, :],
                                          ab[:, g % ABN, 1, k, :], True, True)
                        last.then_inc(gate_full, 1)
                pe.wait_ge(gate_free, (l + 1) * TURNS * GB + GB)
                pe.wait_ge(onehots, (l + 1) * (TURNS * 2 * GB + 1))
                for b in range(4):
                    last = mm(ps[:, b, :], ab[:, 0, 0, 0, :], gij[:, 0:2, :].rearrange("p a t -> p (a t)"),
                              True, True, skip_group_check=True)
                with pe.Fori(0, (KEYS - RUN) // 2) as i:
                    for k in range(2):
                        up(i, RING, part_b(l) + 2 * k, RUN + k, 2)
                        down(i, RING, part_b(l) + 2 * k + 1, k, 2)
                with pe.Fori(0, RUN // RING) as i:
                    for k in range(RING):
                        down(i, RING, part_c(l) + k, KEYS - RUN + k, RING)

        @block.scalar
        def _(act):
            A = nc.scalar.activation

            def take(name):
                act.wait_ge(*whole(name))

            def wait_drained(*name):
                who, count = jobs.drained(name)
                act.wait_ge(drained[who], count)

            def round_half(i, per, n, half):
                if n >= 2:
                    act.wait_ge(half_used, at_half(i, per, n - 2, half))
                if half == 0:
                    act.wait_ge(full[n % RING], i * (16 * per // RING) + 16 * (n // RING + 1))
                A(parts[:, (2 * n + half) % PARTS, 0, :], ring[:, n % RING, half * HALF:(half + 1) * HALF],
                  ACT.Copy).then_inc(hi_done, 1)

            def stream(n, i=0, per=0):
                for half in range(2):
                    round_half(i, per, n + 2, half)

            def stream_pair(part, k):
                stream(STARTS[part] + 2 * k)
                stream(STARTS[part] + 2 * k + 1)

            def round_rhs(src, half):
                A(rhs[:, 0, 4 * half:4 * half + 4, :], src[:, 4 * half:4 * half + 4, :], ACT.Copy).then_inc(rhs_hi, 1)

            def norm(name):
                A(h[:, :, :], x[:, :, :], ACT.Square).then_inc(squared, 1)
                take(name)
                A(rs[:, 0:T], bank(name)[:, 0:T], ACT.Sqrt, bias=eps[:, 0:1]).then_inc(drained["act"], 1)
                for half in range(2):
                    norms[0] += 1
                    act.wait_ge(normed, norms[0])
                    round_rhs(h, half)

            def copy(o, i, scale=1.0):
                A(o, i, ACT.Copy, scale=scale).then_inc(drained["act"], 1)

            norms = [0]
            act.sem_inc(gelu_done, 2)
            act.sem_inc(gate_free, GB)
            act.wait_ge(x_in, 16)
            act.wait_ge(consts_set, 1)
            for n in range(2):
                for half in range(2):
                    round_half(0, 0, n, half)
            norm(("ms_mix", 0))
            act.wait_ge(par_in, 16)
            A(lgn[:, :], pa[:, PAR["decay"]:PAR["decay"] + 16], ACT.Exp).then_inc(lg_done, 1)
            for n in range(3):
                act.wait_ge(hid_arg, n + 1)
                A(hid[0:HY_FILTERS, :], harg[0:HY_FILTERS, 0, :], ACT.Sin).then_inc(hid_done, 1)
                for it in (2 * n, 2 * n + 1):
                    stream_pair("in0", it)
                    take(("in0", it))
                    for m in range(2):
                        t = 2 * it + m
                        last = A(uc[:, t, :], bank(("in0", it))[:, m * T:(m + 1) * T], ACT.Identity,
                                 bias=par_col("conv_b", t), scale=par_col("conv_w", 12 + t))
                    last.then_inc(conv_mid, 1)
            for o in range(2):
                for it in (6 + 4 * o, 7 + 4 * o):
                    stream_pair("in0", it)
                    take(("in0", it))
                    t = 4 * o + 2 * (it % 2)
                    copy(qk[:, t:t + 2, :].rearrange("p a t -> p (a t)"), bank(("in0", it)),
                         scale=1.0 if o == 0 else HD ** -0.5)
                for kt in range(2):
                    for ri in range(2):
                        take(("hf", o, kt, ri))
                        copy(hf[:, o, kt, ri, :], bank(("hf", o, kt, ri)))
                for it in (8 + 4 * o, 9 + 4 * o):
                    stream_pair("in0", it)
                    take(("in0", it))
                    if o == 0:
                        c0 = T * (it % 2)
                        copy(v0[:, :, c0:c0 + T], bank(("in0", it)).rearrange("p (a c) -> p a c", a=2))
                    else:
                        t = 2 * (it % 2)
                        copy(rg[:, t:t + 2, :].rearrange("p a t -> p (a t)"), bank(("in0", it)))
            wait_drained("in0", 13)
            A(sig[:, :, :], rg[:, :, :], ACT.Exp, scale=-1.0).then_inc(silu_e, 1)
            for o in range(2):
                for tt in range(TT):
                    take(("zt", o, tt))
                    copy(zt[:, tt, :], bank(("zt", o, tt)))
                for hh in range(4 * o, 4 * o + 4):
                    act.wait_ge(dec_arg, hh + 1)
                    A(dec[:, hh % 2, :], dec[:, hh % 2, :], ACT.Exp, scale=-1.0).then_inc(dec_exp, 1)
                for n in (2 * o, 2 * o + 1):
                    take(("ret_y", n))
                    copy(yr[:, n, :], bank(("ret_y", n))[:, 0:T])
            wait_drained("conv", 1, 1)
            round_rhs(cat, 0)
            wait_drained("ret_y", 3)
            A(ysq[:, :, :], yr[:, :, :], ACT.Square).then_inc(ysq_done, 1)
            for n in range(2):
                take(("ms_gn", n))
                A(gn_root(n), bank(("ms_gn", n)), ACT.Sqrt, bias=eps[:, 0:1]).then_inc(drained["act"], 1)
            act.wait_ge(cat_done, 2)
            round_rhs(cat, 1)
            for n in range(EV_OUT):
                stream_pair("out0", n)

            for l in range(2):
                if l == 1:
                    act.wait_ge(acc_read, 1)
                    norm(("ms_mix", 1))
                    for it in range(OD_IN):
                        stream_pair("in1", it)
                        take(("in1", it))
                        g, k = divmod(it, 6)
                        if k < 4:
                            t = 8 * g + 2 * k
                            A(hq[:, t:t + 2, :].rearrange("p a t -> p (a t)"), bank(("in1", it)), ACT.Copy)
                            A(hsq[:, t:t + 2, :].rearrange("p a t -> p (a t)"), bank(("in1", it)),
                              ACT.Square).then_inc(drained["act"], 1)
                        else:
                            c0 = T * (k - 4)
                            copy(v1[:, g, :, c0:c0 + T], bank(("in1", it)).rearrange("p (a c) -> p a c", a=2))
                    for n in range(8):
                        take(("ms_head", n))
                        q = n % 4 < 2
                        A(hsq[:, 2 * n:2 * n + 2, :].rearrange("p a t -> p (a t)"), bank(("ms_head", n)), ACT.Sqrt,
                          scale=float(HD) if q else 1.0,
                          bias=eps[:, 1:2] if q else eps[:, 0:1]).then_inc(drained["act"], 1)
                    for u in range(16 + 2):
                        if u < 16:
                            act.wait_ge(s_biased, u + 1)
                            for a in range(2):
                                last = A(p_att[:, u % 2, a, :], s_att[:, u % 2, a, :], ACT.Exp,
                                         bias=st_att[:, u % 8, 0, a:a + 1], accum_out=st_att[:, u % 8, 1, a:a + 1])
                            last.then_inc(s_exp, 1)
                        if 1 <= u <= 16:
                            take(("att_t", u - 1))
                            if u - 1 >= 2:
                                act.wait_ge(*whole(("att_o", (u - 3) // 2)))
                            copy(pt_att[:, (u - 1) % 2, :, :].rearrange("p a t -> p (a t)"), bank(("att_t", u - 1)))
                        if u >= 2 and (u - 2) % 2 == 1:
                            n = (u - 2) // 2
                            take(("att_o", n))
                            copy(cat1[:, n, :], bank(("att_o", n))[:, 0:T])
                    for half in range(2):
                        wait_drained("att_o", 4 * half + 3)
                        round_rhs(cat1, half)
                    for n in range(OD_OUT):
                        stream_pair("out1", n)

                wait_drained(f"out{l}", 3)
                norm(("ms_ffn", l))
                for n in range(WQ):
                    stream_pair(f"q{l}", n)
                    take(("q", l, n))
                    copy(qT[:, 2 * n:2 * n + 2, :].rearrange("p a t -> p (a t)"), bank(("q", l, n)))
                for n in range(1, 8, 2):
                    take(("sc", l, n))
                    tt, quad, s = n // 4, n // 2 % 2, n % 2
                    q0 = (tt * 8 + 4 * quad) * KEYS
                    copy(sc[:, s, q0:q0 + 4 * KEYS], bank(("sc", l, n)))

                def gelus(lo, hi):
                    with act.Fori(lo, hi) as i:
                        for k in range(RING):
                            n = part_a(l) + k
                            stream(n, i, RING)
                            act.wait_ge(half_used, at_half(i, RING, n, 1))
                            A(coef[:, bass.ds(RING * i + k, 1), :].rearrange("p a t -> p (a t)"),
                              ps[:, 4 + k % 2, 0:T], ACT.Gelu_apprx_tanh).then_inc(gelu_done, 1)

                gelus(0, EARLY // RING)
                act.wait_ge(gate_arg, l + 1)
                A(ge[:, :], ge[:, :], ACT.Exp).then_inc(gate_exp, 1)
                gelus(EARLY // RING, RUN // RING)
                with act.Fori(0, TURNS) as i:
                    for q in range(GB):
                        act.wait_ge(gate_mult, i * GB + (l * TURNS * GB + q + 1))
                        A(coef[:, RUN:KEYS, bass.ds(i * (GB * BT) + q * BT, BT)],
                          ps[:, q, :].rearrange("p (t j) -> p j t", t=BT)[:, RUN:KEYS, :],
                          ACT.Copy).then_inc(gate_free, 1)

                def round_coef(i, step, v):
                    src = coef[:, i * step + v, :] if isinstance(i, int) else \
                        coef[:, bass.ds(i * step + v, 1), :].rearrange("p a t -> p (a t)")
                    A(cparts[:, v % 2, 0, :], src, ACT.Copy).then_inc(chi_done, 1)

                round_coef(0, 0, 0)
                with act.Fori(0, (KEYS - RUN) // 2) as i:
                    for k in range(2):
                        n = part_b(l) + 2 * k
                        stream(n, i, RING)
                        act.wait_ge(coef_done, i * 2 + (l * (KEYS - RUN) + k + 1))
                        A(gtmp[:, k, :], ps[:, 4 + k, 0:T], ACT.Gelu_apprx_tanh).then_inc(gelu_done, 1)
                        round_coef(i, 2, k + 1)
                        stream(n + 1, i, RING)
                act.wait_ge(coef_done, 2 + (l + 1) * (KEYS - RUN))

                def last_part(i, end=False):
                    for k in range(RING):
                        n = part_c(l) + k
                        if not (end and k == RING - 1):
                            act.wait_ge(half_used, at_half(i, RING, n - 1, 1))
                            round_coef(i, RING, KEYS - RUN + k + 1)
                        if not (end and k >= RING - 2 and l == 1):
                            stream(n, i, RING)

                turns = RUN // RING
                with act.Fori(0, turns - 1) as i:
                    last_part(i)
                last_part(turns - 1, end=True)

        @block.vector
        def _(dve):
            own = Chain(dve, dve_own)
            V = nc.vector

            def take(name):
                dve.wait_ge(*whole(name))

            def wait_drained(*name):
                who, count = jobs.drained(name)
                dve.wait_ge(drained[who], count)

            def drain(name, ins):
                ins.then_inc(drained["dve"], 1)
                wait_drained(*name)

            rests = [0]

            def rest_of_rhs(src, half):
                rests[0] += 1
                dve.wait_ge(rhs_hi, rests[0])
                c = slice(4 * half, 4 * half + 4)
                V.tensor_tensor(rhs[:, 1, c, :], src[:, c, :], rhs[:, 0, c, :].bitcast(F32),
                                ALU.subtract).then_inc(rhs_lo, 1)

            def norm(gain, l, *name):
                wait_drained(*name)
                own.link(V.reciprocal(rs[:, T:2 * T], rs[:, 0:T]))
                for c in range(DC):
                    last = V.scalar_tensor_tensor(out=h[:, c, :], in0=x[:, c, :], scalar=par_col(gain, l * DC + c),
                                                  in1=rs[:, T:2 * T], op0=ALU.mult, op1=ALU.mult)
                    if c % 4 == 3:
                        last.then_inc(normed, 1)
                for half in range(2):
                    rest_of_rhs(h, half)

            V.memset(eps[:, 0:1], EPS)
            V.memset(eps[:, 1:2], EPS * HD).then_inc(consts_set, 1)
            dve.sem_inc(coef_done, 2)
            dve.wait_ge(par_in, 16)
            norm("mix_gain", 0, "ms_mix", 0)
            TWO_PI_HI, TWO_PI_LO, MAGIC = 6.28125, 0.0019353071795864769, 12582912.0
            F = HY_FILTERS
            for n in range(3):
                take(("hidden", n))
                if n:
                    dve.wait_ge(hid_done, n)
                a, r = harg[0:F, 0, :], harg[0:F, 1, :]
                drain(("hidden", n), V.tensor_scalar(a, bank(("hidden", n))[0:F, 0:T], par_col("fb", n, F), par_col("freq", 0, F),
                                      ALU.add, ALU.mult))
                own.link(V.tensor_scalar(r, a, 0.15915494309189535, MAGIC, ALU.mult, ALU.add))
                own.link(V.tensor_scalar(r, r, -MAGIC, None, ALU.add))
                own.link(V.scalar_tensor_tensor(out=a, in0=r, scalar=-TWO_PI_HI, in1=a, op0=ALU.mult, op1=ALU.add))
                own.link(V.scalar_tensor_tensor(out=a, in0=r, scalar=-TWO_PI_LO, in1=a, op0=ALU.mult, op1=ALU.add))
                V.tensor_scalar(a, a, 3.1415925, -3.1415925, ALU.min, ALU.max).then_inc(hid_arg, 1)
                for it in (2 * n, 2 * n + 1):
                    dve.wait_ge(conv_mid, it + 1)
                    for m in range(2):
                        t = 2 * it + m
                        b = bank(("in0", it))[:, m * T:(m + 1) * T]
                        own.link(V.scalar_tensor_tensor(out=uc[:, t, 1:T], in0=b[:, 0:T - 1],
                                                        scalar=par_col("conv_w", t), in1=uc[:, t, 1:T],
                                                        op0=ALU.mult, op1=ALU.add))
                        ins = V.scalar_tensor_tensor(out=uc[:, t, 0:T - 1], in0=b[:, 1:T],
                                                     scalar=par_col("conv_w", 24 + t), in1=uc[:, t, 0:T - 1],
                                                     op0=ALU.mult, op1=ALU.add)
                    ins.then_inc(drained["dve"], 1)
            dve.wait_ge(con0_in, 16)
            for o in range(2):
                for tt in range(TT):
                    if o == 1 and tt == 0:
                        wait_drained("hf", 0, 1, 1)
                    f, b = bank(("filt", o, tt, 0)), bank(("filt", o, tt, 1))
                    if o + tt:
                        dve.wait_ge(filt_pm, 2 * o + tt)
                    take(("filt", o, tt, 1))
                    drain(("filt", o, tt, 0), V.tensor_tensor(tmp[:, 0, :], f, win[:, tt, 0, :], ALU.mult))
                    drain(("filt", o, tt, 1), V.tensor_tensor(tmp[:, 1, :], b, win[:, tt, 1, :], ALU.mult))
                    V.tensor_tensor(fpm[:, 0, tt, :], tmp[:, 0, :], tmp[:, 1, :], ALU.add)
                    V.tensor_tensor(fpm[:, 1, tt, :], tmp[:, 0, :], tmp[:, 1, :], ALU.subtract).then_inc(filt_pm, 1)

            ropes = [0]

            def rope(name, tiles):
                take(name)
                dve.wait_ge(filt_pm, 4)
                own.wait()
                t3 = tmp[:, 0, :].rearrange("p (a t) -> p a t", a=2)
                sin2 = sin_t.unsqueeze(1).broadcast_to([P, 2, T])
                cos2 = cos_t.unsqueeze(1).broadcast_to([P, 2, T])
                drain(name, V.tensor_tensor(t3, bank(name).rearrange("p (a t) -> p a t", a=2), sin2, ALU.mult))
                own.link(V.tensor_tensor(tiles, tiles, cos2, ALU.mult))
                V.tensor_tensor(tiles, tiles, t3, ALU.add).then_inc(roped, 1)
                ropes[0] += 1
                dve.wait_ge(roped, ropes[0])

            def decay_arg(hh):
                d = dec[:, hh % 2, :]
                own.link(V.tensor_scalar(d, dist[:, 0, :, :].rearrange("p a t -> p (a t)"),
                                         lgn[:, hh:hh + 1], None, ALU.mult))
                V.scalar_tensor_tensor(out=d, in0=dist[:, 1, :, :].rearrange("p a t -> p (a t)"),
                                       scalar=lgn[:, 8 + hh:9 + hh], in1=d, op0=ALU.mult,
                                       op1=ALU.add).then_inc(dec_arg, 1)

            dve.wait_ge(lg_done, 1)
            for o in range(2):
                if o == 0:
                    for n in range(4):
                        rope(("rot0", n), qk[:, 2 * n:2 * n + 2, :])
                wait_drained("hf", o, 1, 1)
                for kt in range(2):
                    take(("zf", o, kt, 1))
                    zr, zi = bank(("zf", o, kt, 0)), bank(("zf", o, kt, 1))
                    hr, hi = hf[:, o, kt, 0, :], hf[:, o, kt, 1, :]
                    if o == 1 and kt == 0:
                        dve.wait_ge(*whole(("conv", 0, 1)))
                    V.tensor_tensor(yf[:, kt, 0, :], zr, hr, ALU.mult)
                    own.link(V.tensor_tensor(tmp[:, 0, :], zi, hi, ALU.mult))
                    V.tensor_tensor(yf[:, kt, 0, :], yf[:, kt, 0, :], tmp[:, 0, :], ALU.subtract)
                    V.tensor_tensor(yf[:, kt, 1, :], zr, hi, ALU.mult)
                    own.link(V.tensor_tensor(tmp[:, 1, :], zi, hr, ALU.mult))
                    dve.sem_inc(drained["dve"], 2)
                    V.tensor_tensor(yf[:, kt, 1, :], yf[:, kt, 1, :], tmp[:, 1, :], ALU.add).then_inc(yf_done, 1)
                if o:
                    wait_drained("ret_s", 2)
                decay_arg(4 * o)
                for hh in range(4 * o, 4 * o + 4):
                    if hh % 4 < 3:
                        if hh:
                            wait_drained("ret_s", hh - 1)
                        decay_arg(hh + 1)
                    take(("ret_s", hh))
                    dve.wait_ge(dec_exp, hh + 1)
                    if o == 1:
                        dve.wait_ge(*whole(("ret_y", hh // 2 - 2)))
                    V.tensor_tensor(prob[:, hh % 4, :, :].rearrange("p a t -> p (a t)"), bank(("ret_s", hh)),
                                    dec[:, hh % 2, :], ALU.mult).then_inc(drained["dve"], 1)
                for n in range(2):
                    take(("conv", o, n))
                    dve.wait_ge(yf_done, 2 * (o + 1)) if n == 0 else wait_drained("conv", o, 0)
                    for b in range(2):
                        c = 2 * n + b
                        z = zc[:, c, :]
                        own.link(V.scalar_tensor_tensor(out=tmp[:, b, 0:T], in0=z, scalar=par_col("skip", 4 * o + c),
                                                        in1=bank(("conv", o, n))[:, b * T:(b + 1) * T],
                                                        op0=ALU.mult, op1=ALU.add))
                        last = V.tensor_tensor(z if o == 0 else cat[:, c, :], tmp[:, b, 0:T], uc[:, 4 + 4 * o + c, :],
                                               ALU.mult)
                    last.then_inc(drained["dve"], 1)
            rest_of_rhs(cat, 0)
            dve.wait_ge(silu_e, 1)
            own.link(V.tensor_scalar(sig[:, :, :], sig[:, :, :], 1.0, None, ALU.add))
            own.link(V.reciprocal(sig[:, :, :], sig[:, :, :]))
            own.link(V.tensor_tensor(sig[:, :, :], sig[:, :, :], rg[:, :, :], ALU.mult))
            for n in range(2):
                wait_drained("ms_gn", n)
                own.link(V.reciprocal(gn_root(n), gn_root(n)))
                own.link(V.tensor_tensor(yr[:, 2 * n:2 * n + 2, :], yr[:, 2 * n:2 * n + 2, :],
                                         gn_root(n).rearrange("p (a t) -> p a t", a=2), ALU.mult))
                for b in range(2):
                    c = 2 * n + b
                    last = V.scalar_tensor_tensor(out=cat[:, 4 + c, :], in0=yr[:, c, :], scalar=par_col("gn", c),
                                                  in1=sig[:, c, :], op0=ALU.mult, op1=ALU.mult)
                last.then_inc(cat_done, 1)
            rest_of_rhs(cat, 1)

            def residual(name, n):
                take(name)
                drain(name, V.tensor_tensor(x[:, 2 * n:2 * n + 2, :], x[:, 2 * n:2 * n + 2, :],
                                      bank(name).rearrange("p (a t) -> p a t", a=2), ALU.add))

            for n in range(EV_OUT):
                residual(("out0", n), n)

            for l in range(2):
                if l == 1:
                    norm("mix_gain", 1, "ms_mix", 1)
                    for n in range(8):
                        wait_drained("ms_head", n)
                        inv = hsq[:, 2 * n:2 * n + 2, :]
                        own.link(V.reciprocal(inv, inv))
                        g = par_col("na_gain" if n < 4 else "dil_gain", n % 4 // 2)
                        tiles = hq[:, 2 * n:2 * n + 2, :]
                        V.scalar_tensor_tensor(out=tiles, in0=tiles, scalar=g, in1=inv, op0=ALU.mult,
                                               op1=ALU.mult).then_inc(head_done, 1)
                    for n in range(4):
                        rope(("rot1", n), hq[:, 8 + 2 * n:10 + 2 * n, :])
                    dve.wait_ge(bias_in, 48)
                    for u in range(16 + 1):
                        if u < 16:
                            g, hh = divmod(u, H)
                            take(("att_s", u))
                            b = bias[:, hh if g == 0 else 8, :, :]
                            drain(("att_s", u), V.tensor_tensor(s_att[:, u % 2, :, :],
                                                  bank(("att_s", u)).rearrange("p (a t) -> p a t", a=2), b, ALU.add))
                            V.tensor_reduce(st_att[:, u % 8, 0, :], s_att[:, u % 2, :, :], AX.X, ALU.max,
                                            negate=True).then_inc(s_biased, 1)
                        if u >= 1:
                            w = u - 1
                            dve.wait_ge(s_exp, w + 1)
                            own.link(V.reciprocal(st_att[:, w % 8, 2, :], st_att[:, w % 8, 1, :]))
                            for a in range(2):
                                last = V.tensor_scalar(p_att[:, w % 2, a, :], p_att[:, w % 2, a, :],
                                                       st_att[:, w % 8, 2, a:a + 1], None, ALU.mult)
                            last.then_inc(p_normed, 1)
                    for half in range(2):
                        rest_of_rhs(cat1, half)
                    for n in range(OD_OUT):
                        residual(("out1", n), n)

                norm("ffn_gain", l, "ms_ffn", l)
                for n in range(0, 8, 2):
                    take(("sc", l, n))
                    tt, quad = n // 4, n // 2 % 2
                    q0 = (tt * 8 + 4 * quad) * KEYS
                    drain(("sc", l, n), V.tensor_copy(sc[:, 0, q0:q0 + 4 * KEYS], bank(("sc", l, n))))
                wait_drained("sc", l, 7)

                with dve.Fori(0, 8) as i:
                    own.enter(i, 6)
                    own.drain_after(V.tensor_copy(cur.rearrange("p s e c -> p s (e c)"),
                                                  sc[:, :, bass.ds(i * 2 * KEYS, 2 * KEYS)]))

                    def top16(lists):
                        for values, rest, best, index in lists:
                            V.max(best[:, 0:8], values)
                        dve.drain()
                        for values, rest, best, index in lists:
                            V.max_index(index[:, 0:8], best[:, 0:8], values)
                        for values, rest, best, index in lists:
                            V.match_replace(rest, best[:, 0:8], values, -3.0e38)
                        dve.drain()
                        for values, rest, best, index in lists:
                            V.max(best[:, 8:16], rest)
                        dve.drain()
                        for values, rest, best, index in lists:
                            last = V.max_index(index[:, 8:16], best[:, 8:16], rest)
                        return last

                    own.link(top16([(cur[:, s, e, :], cut[:, s, e, :], top_s[:, s, e, :], top_i[:, s, e, :])
                                    for s in range(2) for e in range(2)]))
                    V.tensor_copy(top_f.rearrange("p s e c -> p (s e c)"), top_i.rearrange("p s e c -> p (s e c)"))
                    for e in range(2):
                        V.tensor_tensor(cand[:, e, :].rearrange("p (a b) -> p a b", a=16),
                                        top_s[:, 0, e, :].unsqueeze(2).broadcast_to([P, 16, 16]),
                                        top_s[:, 1, e, :].unsqueeze(1).broadcast_to([P, 16, 16]), ALU.add)
                    dve.drain()
                    own.link(top16([(cand[:, e, :], cand2[:, e, :], g16[:, e, :], pick[:, e, :]) for e in range(2)]))
                    V.tensor_copy(gs[:, bass.ds(i * 32, 32)], g16.rearrange("p e c -> p (e c)"))
                    pick2 = pick.rearrange("p e c -> p (e c)")
                    V.tensor_scalar(pab[:, 0, :], pick2, 4, None, ALU.logical_shift_right)
                    own.link(V.tensor_scalar(pab[:, 1, :], pick2, 15, None, ALU.bitwise_and))
                    own.link(V.tensor_copy(pabf[:, :, :], pab[:, :, :]))
                    for s in range(2):
                        last = V.tensor_tensor(look[:, s, :, :, :].rearrange("p e k a -> p (e k) a"),
                                               iota[:, 0:16].unsqueeze(1).broadcast_to([P, 32, 16]),
                                               pabf[:, s, :].unsqueeze(2).broadcast_to([P, 32, 16]), ALU.is_equal)
                    own.link(last)
                    for s in range(2):
                        last = V.tensor_tensor(look[:, s, :, :, :], look[:, s, :, :, :],
                                               top_f[:, s, :, :].unsqueeze(2).broadcast_to([P, 2, 16, 16]), ALU.mult)
                    own.link(last)
                    V.tensor_reduce(ijs[:, :, bass.ds(i * 32, 32)],
                                    look.rearrange("p s e k a -> p s (e k) a"), AX.X, ALU.add)
                    dve.drain()
                own.leave(8)

                g3 = gs.rearrange("p (q k) -> p q k", k=16)
                e3 = ge.rearrange("p (q k) -> p q k", k=16)
                V.tensor_tensor(e3, g3, g3[:, :, 0:1].broadcast_to([P, 16, 16]), ALU.subtract).then_inc(gate_arg, 1)
                dve.wait_ge(gate_exp, l + 1)
                own.link(V.tensor_reduce(gsum, e3, AX.X, ALU.add))
                own.link(V.reciprocal(gsum, gsum))
                own.link(V.tensor_tensor(g3, e3, gsum.unsqueeze(2).broadcast_to([P, 16, 16]), ALU.mult))
                dve.sem_inc(gates_done, 1)
                for n in range(3):
                    take(("gt", l, n))
                    drain(("gt", l, n), V.tensor_copy(gij[:, n, :], ps[:, (6 + n) % 8, 0:T]))

                def onehot_rows(i, q):
                    grid = iota.unsqueeze(1).broadcast_to([P, ABT, P])
                    for g in (2 * q, 2 * q + 1):
                        for s, signal in ((0, plain_i), (1, onehots)):
                            t0 = i * (GB * BT) + g * ABT
                            pick_t = gij[:, 1 + s, t0:t0 + ABT] if isinstance(i, int) else \
                                gij[:, 1 + s, bass.ds(t0, ABT)]
                            V.tensor_tensor(ab[:, g % ABN, s, :, :], grid,
                                            pick_t.unsqueeze(2).broadcast_to([P, ABT, P]),
                                            ALU.is_equal).then_inc(signal, 1)

                def gate_tiles(i, q):
                    dve.wait_ge(gate_full, i * GB + (l * TURNS * GB + q + 1))
                    t0 = i * (GB * BT) + q * BT
                    c = coef[:, 0:RUN, t0:t0 + BT] if isinstance(i, int) else coef[:, 0:RUN, bass.ds(t0, BT)]
                    V.tensor_tensor(c, c, ps[:, q, :].rearrange("p (t j) -> p j t", t=BT)[:, 0:RUN, :],
                                    ALU.mult).then_inc(gate_mult, 1)

                dve.wait_ge(gelu_done, 2 + l * KEYS + RUN)
                for q in range(GB):
                    if q >= 2:
                        gate_tiles(0, q - 2)
                    onehot_rows(0, q)
                with dve.Fori(1, TURNS) as i:
                    for q in range(GB):
                        gate_tiles(i - 1, q + 2) if q < 2 else gate_tiles(i, q - 2)
                        onehot_rows(i, q)
                for q in (2, 3):
                    gate_tiles(TURNS - 1, q)
                dve.wait_ge(gate_free, (l + 1) * TURNS * GB + GB)
                V.memset(ab[:, 0, 0, 0, :], 0.0).then_inc(onehots, 1)

                def rest_of_coef(i, step, v):
                    src = coef[:, i * step + v, :] if isinstance(i, int) else \
                        coef[:, bass.ds(i * step + v, 1), :].rearrange("p a t -> p (a t)")
                    dve.wait_ge(chi_done, i * step + (KEYS * l + v + 1))
                    V.tensor_tensor(cparts[:, v % 2, 1, :], src, cparts[:, v % 2, 0, :].bitcast(F32),
                                    ALU.subtract).then_inc(clo_done, 1)

                rest_of_coef(0, 0, 0)
                with dve.Fori(0, (KEYS - RUN) // 2) as i:
                    for k in range(2):
                        dve.wait_ge(gelu_done, i * 2 + (2 + l * KEYS + RUN + k + 1))
                        c = coef[:, bass.ds(2 * i + (RUN + k), 1), :].rearrange("p a t -> p (a t)")
                        V.tensor_tensor(c, c, gtmp[:, k, :], ALU.mult).then_inc(coef_done, 1)
                        rest_of_coef(i, 2, k + 1)
                turns = RUN // RING
                with dve.Fori(0, turns - 1) as i:
                    for k in range(RING):
                        rest_of_coef(i, RING, KEYS - RUN + k + 1)
                for k in range(RING - 1):
                    rest_of_coef(turns - 1, RING, KEYS - RUN + k + 1)
                dve.wait_ge(half_used, 2 * (part_c(l) + RUN))
                for b in range(4):
                    last = V.tensor_tensor(x[:, 2 * b:2 * b + 2, :], x[:, 2 * b:2 * b + 2, :],
                                           ps[:, b, :].rearrange("p (a t) -> p a t", a=2), ALU.add)
                own.link(last)
                dve.sem_inc(acc_read, 1)




def _constants():
    import numpy as np

    f = np.float32
    t = np.arange(T)
    inv = (10000.0 ** (-np.arange(0, HD, 2, dtype=f) / HD)).astype(f)
    ang = (t.astype(f)[:, None] * inv[None, :]).astype(f)
    cos = np.tile(np.cos(ang).T, (4, 1))
    sin = np.tile(np.sin(ang).T, (4, 1))
    rot = np.zeros((P, P))
    for b in (0, HD):
        for k in range(HD // 2):
            rot[b + HD // 2 + k, b + k] = -1.0
            rot[b + k, b + HD // 2 + k] = 1.0
    same_head = np.kron(np.eye(2), np.full((HD, HD), 1.0 / HD))
    consts = np.concatenate([np.eye(P), rot, np.full((P, P), 1.0 / D), same_head,
                             np.tile(np.arange(P), (P, 1)), cos, sin], axis=1)
    bands = (EMB - 1) // 2
    t_norm = np.linspace(0.0, 1.0, T, dtype=f)[:, None]
    w = (2.0 * np.pi * np.arange(T, dtype=f)[:, None] / T).astype(f)
    fb = np.linspace(1e-4, bands - 1, bands, dtype=f)[None, :]
    e = np.concatenate([t_norm, np.cos(fb * w), -np.sin(fb * w)], axis=-1)
    emb = np.zeros((P, T))
    emb[:EMB] = e.T
    lo, hi = np.log(1e-2) / 1.5, np.log(1e-2) / 0.3
    deltas = np.abs(np.linspace(lo, hi, GW, dtype=f))
    win = np.exp(-t_norm * deltas[None, :]) + 0.05
    win_b = win.copy()
    win_b[0] = 0.0
    ph = np.pi * np.outer(t, 2 * t + 1) / (2 * T)
    dft = np.concatenate([np.cos(ph), -np.sin(ph)], axis=1)
    idft = np.stack([np.cos(ph).T, -np.sin(ph).T]) / T
    dft_s = dft.reshape(TT, P, 2 * T).transpose(1, 0, 2).reshape(P, -1)
    idft_s = idft.reshape(2, 2, P, T).transpose(2, 1, 0, 3).reshape(P, -1)
    win_s = np.stack([win, win_b]).reshape(2, TT, P, GW).transpose(2, 1, 0, 3).reshape(P, -1)
    m = np.arange(T).reshape(TT, P)
    ahead = np.maximum(t[None, None, :] - m[:, :, None], 0)
    behind = np.maximum(m[:, :, None] - t[None, None, :], 0)
    dist = np.stack([ahead, behind]).transpose(2, 0, 1, 3).reshape(P, -1)
    con0 = np.concatenate([emb, dft_s, idft_s, win_s, dist], axis=1)
    q, k = t[:, None], t[None, :]
    seen = np.zeros((T, T))
    for window, dil in ((128, 1), (512, 4), (2048, 16)):
        seen += (q % dil == k % dil) & (np.abs(q // dil - k // dil) <= window // (2 * dil))
    merged = np.where(seen > 0, np.log(np.maximum(seen, 1)), NEG)
    con1 = merged.reshape(TT, P, T).transpose(1, 0, 2)
    return [np.ascontiguousarray(a, dtype=f) for a in (consts, con0, con1)]


def kernel(**inputs):
    import numpy as np
    import concourse.bacc as bacc
    from concourse.bass_utils import run_bass_kernel_spmd as run

    a = {k: np.asarray(v) for k, v in inputs.items()}

    def chunks(v):
        return np.ascontiguousarray(v.reshape(-1, P).T)

    def tiles(w):
        n = w.shape[1] // P
        return np.ascontiguousarray(w.reshape(DC, P, n, P).transpose(2, 1, 0, 3).reshape(n, P, TILE))

    def rows(v):
        out = np.zeros((P, v.shape[1]), v.dtype)
        out[:v.shape[0]] = v
        return out

    def twice(v):
        return np.concatenate([v.T, v.T], axis=0)

    par = np.concatenate([
        chunks(a["mix_norm_gain"]), chunks(a["ffn_norm_gain"]), chunks(a["hy_conv_w"][0]), chunks(a["hy_conv_b"][0]),
        chunks(a["hy_skip"][0]), chunks(a["ret_gn_gain"][0]), twice(a["na_qk_gain"][0]), twice(a["dil_qk_gain"][0]),
        rows(np.stack([a["hy_fb1"][0], a["hy_fb2"][0], a["hy_fb3"][0], a["hy_freq"][0]], axis=1)),
        np.tile(a["ret_log_decay"][0].reshape(1, 16), (P, 1)),
        rows(a["hy_fw1"][0]), rows(a["hy_fw2"][0]), rows(a["hy_fw3"][0])], axis=1)
    assert par.shape[1] == NPAR
    consts, con0, con1 = _constants()

    rows_, cols = T // 64, 64
    r, c = np.arange(rows_), np.arange(cols)
    c0 = np.clip(c - 8, 0, cols - 16)
    valid = (c[None, :] >= c0[:, None]) & (c[None, :] < c0[:, None] + 16)
    row_off = r[None, :] - r[:, None] + 7
    col_off = np.clip(c[None, :] - c[:, None] + 15, 0, 30)
    b = a["na_rpb"][0][:, row_off[:, None, :, None], col_off[None, :, None, :]]
    b = np.where(valid[None, None, :, None, :], b, np.float32(NEG)).reshape(8, TT, P, T)
    na_bias = np.ascontiguousarray(b.transpose(2, 0, 1, 3))

    w_in = a["ev_w_in"][0]
    ev = tiles(w_in)[[*range(16), *range(20, 24), *range(16, 20), *range(24, 28)]]
    subk = np.ascontiguousarray(a["peer_sub_keys"].transpose(0, 2, 4, 1, 3).reshape(2, P, 8, KEYS))
    u_t = a["peer_u"].reshape(2, KEYS, KEYS, DC, P).transpose(0, 2, 4, 3, 1).reshape(2, KEYS, P, TILE)
    v_t = a["peer_v"].reshape(2, KEYS, KEYS, D).transpose(0, 2, 1, 3)
    arrays = {
        "xT": a["x"][0].T.reshape(DC, P, T).transpose(1, 0, 2), "par": par, "consts": consts, "con0": con0,
        "con1": con1, "subk": subk, "w_ev_in": ev, "w_ev_out": tiles(a["ev_w_out"][0]),
        "w_od_in": tiles(a["od_w_in"][0]), "w_od_out": tiles(a["od_w_out"][0]),
        "w_q": np.stack([tiles(a["peer_w_q"][0]), tiles(a["peer_w_q"][1])]), "fw_out": a["hy_fw_out"][0],
        "na_bias": na_bias, "u_t": u_t, "v_t": v_t,
    }
    nc = bacc.Bacc("TRN2", target_bir_lowering=False, num_devices=1)
    args = {}
    for name, v in arrays.items():
        arrays[name] = np.ascontiguousarray(v)
        args[name] = nc.dram_tensor(name, v.shape, F32, kind="ExternalInput").ap()
    out = nc.dram_tensor("out", (P, DC, T), F32, kind="ExternalOutput").ap()
    hybrid_trunk(nc, out=out, **args)
    got = run(nc, [arrays], core_ids=[0]).results[0]["out"]
    return np.ascontiguousarray(got.transpose(1, 0, 2).reshape(D, T).T)[None]
```

```python
from contextlib import ExitStack

import concourse.bass as bass
from concourse import mybir
from concourse.alu_op_type import AluOpType as ALU

F32 = mybir.dt.float32
F32R = mybir.dt.float32r
U32 = mybir.dt.uint32
ACT = mybir.ActivationFunctionType
AX = mybir.AxisListType

P = 128
D = 1024
DC = D // P
T = 256
TT = T // P
GW = 512
GC = GW // P
HD = 64
H = 8
EPS = 1e-6
NEG = -1e30
RING = 4
TILE = 1024
PARTS = 4
HALF = TILE // 2
KEYS = 128
RUN = 68
ABT = 4
ABN = 4
GB = 4
BT = 4
PLACES = BT // ABT
TURNS = T // (GB * BT)
BODY = RING * GB
ACT_PLACES = range(2, PLACES * BODY, 5)
POOL_PLACES = [g for g in range(PLACES * BODY) if g not in ACT_PLACES]
AHEAD = RUN - TURNS
EARLY = AHEAD - RING

EV_IN, EV_OUT, OD_IN, OD_OUT, WQ = 14, 4, 12, 4, 4
HY_FILTERS = 64
EMB = 33
UNITS = 16
LAG = 3

PAR = {}


def par_columns():
    at = 0
    for name, n in (("mix_gain", 2 * DC), ("ffn_gain", 2 * DC), ("conv_w", 3 * 12), ("conv_b", 12), ("skip", 8),
                    ("gn", GC), ("na_gain", 2), ("dil_gain", 2), ("fb", 3), ("freq", 1), ("decay", 16),
                    ("fw1", 64), ("fw2", 64), ("fw3", 64)):
        PAR[name] = at
        at += n
    return at


NPAR = par_columns()


def stream():
    starts, n = {}, 0
    for name, tiles in (("in0", 2 * EV_IN), ("out0", 2 * EV_OUT), ("q0", 2 * WQ), ("experts0", 2 * KEYS),
                        ("in1", 2 * OD_IN), ("out1", 2 * OD_OUT), ("q1", 2 * WQ), ("experts1", 2 * KEYS)):
        starts[name] = n
        n += tiles
    return starts, n


STARTS, TILES = stream()


def even_order():
    def both(step, *at):
        return [(step, *at, 0), (step, *at, 1)]

    return [("hidden", 0), ("in0", 0), ("hidden", 1), ("in0", 1), ("hidden", 2), ("in0", 2), *both("filt", 0),
            ("in0", 3), *both("zt", 0), *both("hf", 0), ("in0", 4), *both("zf", 0), ("in0", 5), *both("filt", 1),
            ("in0", 6), *both("conv", 0), ("in0", 7), *both("hf", 1), ("rot", 0), *both("zt", 1), ("in0", 8),
            ("rot", 1), ("in0", 9), ("rot", 2), ("rot", 3), *(("decay", n) for n in range(4)), ("in0", 10),
            *(("scores", n) for n in range(4)), *(("decay", n) for n in range(4, 8)), ("in0", 11),
            *(("scores", n) for n in range(4, 8)), ("in0", 12), ("silu", 0), ("values", 0), ("values", 1),
            *both("zf", 1), ("gn", 0), ("in0", 13), ("values", 2), ("values", 3), ("gn", 1), *both("conv", 1)]


def odd_order():
    def unit(u):
        steps = []
        if u < UNITS:
            steps.append(("scores", u))
        if 0 <= u - LAG < UNITS:
            steps.append(("turn", u - LAG))
        if u > LAG and (u - LAG) % 2 == 0:
            steps.append(("values", (u - LAG) // 2 - 1))
        return steps

    order = [("in1", 0)]
    for k in range(4):
        order += [("in1", k + 1), ("head", k)]
    order += [("in1", 5), ("in1", 6), *unit(0), ("in1", 7), *unit(1)]
    for k in range(4):
        order += [("head", 4 + k), ("in1", 8 + k), *unit(2 + k), ("rot", k)]
    for u in range(6, UNITS + LAG + 1):
        order += unit(u)
    return order


class Jobs:

    def __init__(self):
        self.number, self.who, self.rank, self.total = {}, [], [], {"act": 0, "dve": 0}
        self.whole, self.others = {}, 0

    def add(self, name, who, tile=None):
        self.number[name] = len(self.who)
        self.who.append(who)
        self.total[who] += 1
        self.rank.append(self.total[who])
        if tile is None:
            self.others += 1
            self.whole[name] = "psum_full", self.others
        else:
            self.whole[name] = "half_used", 2 * tile + 2

    def project(self, name, who):
        part, k = (f"q{name[1]}", name[2]) if name[0] == "q" else name
        self.add(name, who, STARTS[part] + 2 * k + 1)

    def bank(self, name):
        return self.number[name] % 8

    def drained(self, name):
        n = self.number[name]
        return self.who[n], self.rank[n]


def plan():
    jobs = Jobs()
    add = jobs.add
    add(("ms_mix", 0), "act")
    for step, *at in even_order():
        if step == "in0":
            jobs.project(("in0", at[0]), "dve" if at[0] < 6 else "act")
        elif step in ("filt", "hf", "zf"):
            for part in range(2):
                add((step, *at, part), "act" if step == "hf" else "dve")
        elif step not in ("decay", "silu"):
            name, who = {"hidden": ("hidden", "dve"), "zt": ("zt", "act"), "conv": ("conv", "dve"),
                         "rot": ("rot0", "dve"), "scores": ("ret_s", "dve"), "values": ("ret_y", "act"),
                         "gn": ("ms_gn", "act")}[step]
            add((name, *at), who)
    for n in range(EV_OUT):
        jobs.project(("out0", n), "dve")
    for l in range(2):
        if l == 1:
            add(("ms_mix", 1), "act")
            for step, k in odd_order():
                if step == "in1":
                    jobs.project(("in1", k), "act")
                else:
                    name, who = {"head": ("ms_head", "act"), "rot": ("rot1", "dve"), "scores": ("att_s", "dve"),
                                 "turn": ("att_t", "act"), "values": ("att_o", "act")}[step]
                    add((name, k), who)
            for n in range(OD_OUT):
                jobs.project(("out1", n), "dve")
        add(("ms_ffn", l), "act")
        for n in range(WQ):
            jobs.project(("q", l, n), "act")
        for n in range(8):
            add(("sc", l, n), "act" if n % 2 else "dve")
        for n in range(3):
            add(("gt", l, n), "dve")
    return jobs


class Chain:

    def __init__(self, eng, sem):
        self.eng, self.sem, self.n, self.turn, self.per, self.k = eng, sem, 0, None, 0, 0

    def link(self, ins):
        ins.then_inc(self.sem, 1)
        if self.turn is None:
            self.n += 1
            self.eng.wait_ge(self.sem, self.n)
        else:
            self.k += 1
            self.eng.wait_ge(self.sem, self.turn * self.per + (self.n + self.k))

    def enter(self, turn, per):
        self.turn, self.per, self.k = turn, per, 0

    def leave(self, turns):
        assert self.k == self.per, (self.k, self.per)
        self.n += turns * self.per
        self.turn = None


def hybrid_trunk(nc, xT, par, consts, con0, con1, subk, w_ev_in, w_ev_out, w_od_in, w_od_out, w_q, fw_out,
                 na_bias, u_t, v_t, out):
    jobs = plan()
    ctx = ExitStack()
    with ctx:
        def sb(name, shape, dt=F32):
            return ctx.enter_context(nc.sbuf_tensor(name, shape, dt))

        def sem(name):
            return ctx.enter_context(nc.semaphore(name))

        x = sb("x", [P, DC, T])
        rhs = sb("rhs", [P, 2, DC, T], F32R)
        ring = sb("ring", [P, RING, TILE])
        parts = sb("parts", [P, PARTS, 2, HALF], F32R)
        cparts = sb("cparts", [P, 2, 2, T], F32R)
        big = sb("big", [P, KEYS * T])
        coef = big[:, :].rearrange("p (j t) -> p j t", t=T)
        pa = sb("pa", [P, NPAR])
        cst = sb("cst", [P, 5 * P + 2 * T])
        ident, rot_m, ones_d, ones_h, iota = (cst[:, k * P:(k + 1) * P] for k in range(5))
        cos_t = cst[:, 5 * P:5 * P + T]
        sin_t = cst[:, 5 * P + T:5 * P + 2 * T]
        ab = sb("ab", [P, ABN // 2, 2, ABT, P])
        ab_x = x[:, :, :].rearrange("p c t -> p (c t)").rearrange("p (n s k e) -> p n s k e", n=ABN // 2, s=2, k=ABT)
        places = [ab[:, k, :, :, :] for k in range(ABN // 2)] + [ab_x[:, k, :, :, :] for k in range(ABN // 2)]
        gij = sb("gij", [P, 3, T])
        gtmp = sb("gtmp", [P, 2, T])
        rs = gtmp[:, :, :].rearrange("p a t -> p (a t)")
        eps = sb("eps", [P, 2])
        warm = sb("warm", [P, 1])
        lgn = sb("lgn", [P, 16])

        at = [0]

        def carve(n, start=None):
            if start is not None:
                at[0] = start
            ap = big[:, at[0]:at[0] + n]
            at[0] += n
            assert at[0] <= KEYS * T, at[0]
            return ap

        h = carve(DC * T, 0).rearrange("p (c t) -> p c t", t=T)
        uc = carve(12 * T, 0).rearrange("p (m t) -> p m t", t=T)
        qk = carve(8 * T).rearrange("p (m t) -> p m t", t=T)
        v0 = carve(TT * GW).rearrange("p (a c) -> p a c", a=TT)
        rg = carve(GC * T).rearrange("p (m t) -> p m t", t=T)
        hid = carve(T)
        harg = carve(2 * T).rearrange("p (a t) -> p a t", a=2)
        fpm = carve(4 * GW).rearrange("p (s a c) -> p s a c", s=2, a=TT)
        hf = carve(8 * GW).rearrange("p (o k r c) -> p o k r c", o=2, k=2, r=2)
        fwo = carve(4 * GW)
        zt = carve(TT * GW).rearrange("p (a c) -> p a c", a=TT)
        yf = carve(4 * GW).rearrange("p (k r c) -> p k r c", k=2, r=2)
        tmp = carve(2 * GW).rearrange("p (a c) -> p a c", a=2)
        cat = carve(DC * T).rearrange("p (m t) -> p m t", t=T)
        prob = carve(4 * GW).rearrange("p (b a t) -> p b a t", b=4, a=2)
        sig = carve(GC * T).rearrange("p (m t) -> p m t", t=T)
        con0_s = carve(256 + 1024 + 1024 + 2048 + 1024)
        emb = con0_s[:, 0:256]
        dft = con0_s[:, 256:1280].rearrange("p (a k) -> p a k", a=TT)
        idft = con0_s[:, 1280:2304].rearrange("p (r t) -> p r t", t=T)
        win = con0_s[:, 2304:4352].rearrange("p (a d c) -> p a d c", a=TT, d=2)
        dist = con0_s[:, 4352:5376].rearrange("p (d a t) -> p d a t", d=2, a=2)
        hf0 = hf[:, 0, :, :, :].rearrange("p k r c -> p (k r c)")
        yr = hf0[:, 0:GC * T].rearrange("p (m t) -> p m t", t=T)
        ysq = hf0[:, GC * T:2 * GC * T].rearrange("p (m t) -> p m t", t=T)
        zc = uc[:, 0:4, :]
        probs = [prob[:, k, :, :] for k in range(4)] + \
            [fpm[:, k // 2, k % 2, :].rearrange("p (a t) -> p a t", a=2) for k in range(4)]
        decs = [fwo[:, k * GW:(k + 1) * GW] for k in range(4)] + [win[:, k // 2, k % 2, :] for k in range(4)]

        def gn_root(n):
            return ysq[:, 2 * n:2 * n + 2, :].rearrange("p a t -> p (a t)")

        hq = carve(16 * T, 0).rearrange("p (m t) -> p m t", t=T)
        hsq = carve(16 * T).rearrange("p (m t) -> p m t", t=T)
        v1 = carve(2 * TT * GW).rearrange("p (g a c) -> p g a c", g=2, a=TT)
        bias = carve(9 * 2 * T).rearrange("p (h a t) -> p h a t", h=9, a=2)
        s_att = carve(4 * 2 * T).rearrange("p (b a t) -> p b a t", b=4, a=2)
        p_att = carve(4 * 2 * T).rearrange("p (b a t) -> p b a t", b=4, a=2)
        pt_att = carve(4 * 2 * T).rearrange("p (b a t) -> p b a t", b=4, a=2)
        cat1 = carve(DC * T).rearrange("p (m t) -> p m t", t=T)
        st_att = carve(64).rearrange("p (b s a) -> p b s a", b=8, s=4)
        turned = carve(2 * T)

        qT = carve(8 * T, RUN * T).rearrange("p (m t) -> p m t", t=T)
        sc = carve(2 * 16 * KEYS).rearrange("p (s c) -> p s c", s=2)
        cur = carve(4 * KEYS).rearrange("p (s e c) -> p s e c", s=2, e=2)
        cut = carve(4 * KEYS).rearrange("p (s e c) -> p s e c", s=2, e=2)
        top_s = carve(64).rearrange("p (s e c) -> p s e c", s=2, e=2)
        top_i = carve(64).bitcast(U32).rearrange("p (s e c) -> p s e c", s=2, e=2)
        top_f = carve(64).rearrange("p (s e c) -> p s e c", s=2, e=2)
        cand = carve(512).rearrange("p (e c) -> p e c", e=2)
        cand2 = carve(512).rearrange("p (e c) -> p e c", e=2)
        g16 = carve(32).rearrange("p (e c) -> p e c", e=2)
        pick = carve(32).bitcast(U32).rearrange("p (e c) -> p e c", e=2)
        pab = carve(64).bitcast(U32).rearrange("p (s c) -> p s c", s=2)
        pabf = carve(64).rearrange("p (s c) -> p s c", s=2)
        look = carve(1024).rearrange("p (s e k a) -> p s e k a", s=2, e=2, k=16)
        gs = carve(256)
        ijs = carve(512).rearrange("p (s c) -> p s c", s=2)
        ge = carve(256)
        gsum = carve(16)
        assert at[0] <= KEYS * T - 1024
        sk = big[:, KEYS * T - 1024:KEYS * T].rearrange("p (h k) -> p h k", h=8)

        ps = ctx.enter_context(nc.psum_tensor("ps", [P, 8, 512], F32))

        def bank(name):
            return ps[:, jobs.bank(name), :]

        x_in = [sem(f"x_in{n}") for n in range(4)]
        par_in = sem("par_in")
        cst_in = sem("cst_in")
        con0_in = sem("con0_in")
        fwo_in = sem("fwo_in")
        sk_in = sem("sk_in")
        bias_in = sem("bias_in")
        out_done = sem("out_done")
        x_saved = sem("x_saved")
        x_back = sem("x_back")
        full = [sem(f"tile_in{s}") for s in range(RING)]
        hi_done = sem("hi_done")
        lo_done = sem("lo_done")
        half_used = sem("half_used")
        rhs_hi = sem("rhs_hi")
        rhs_lo = sem("rhs_lo")
        chi_done = sem("chi_done")
        clo_done = sem("clo_done")
        psum_full = sem("psum_full")
        drained = {"act": sem("drained_by_act"), "dve": sem("drained_by_dve")}
        dve_own = sem("dve_own")
        consts_set = sem("consts_set")
        squared = sem("squared")
        normed = sem("normed")
        hid_arg = sem("hid_arg")
        hid_done = sem("hid_done")
        conv_mid = sem("conv_mid")
        filt_pm = sem("filt_pm")
        yf_done = sem("yf_done")
        roped = sem("roped")
        dec_arg = sem("dec_arg")
        dec_exp = sem("dec_exp")
        lg_done = sem("lg_done")
        silu_e = sem("silu_e")
        cat_done = sem("cat_done")
        head_done = sem("head_done")
        s_biased = sem("s_biased")
        s_exp = sem("s_exp")
        p_normed = sem("p_normed")
        gate_arg = sem("gate_arg")
        gate_exp = sem("gate_exp")
        gates_done = sem("gates_done")
        gelu_done = sem("gelu_done")
        onehots = sem("onehots")
        pool_weighted = sem("pool_weighted")
        act_weighted = sem("act_weighted")
        gate_full = sem("gate_full")
        gate_mult = sem("gate_mult")
        gate_free = sem("gate_free")
        coef_done = sem("coef_done")
        acc_read = sem("acc_read")

        block = ctx.enter_context(nc.Block())

        def par_col(name, k=0, rows=P):
            return pa[0:rows, PAR[name] + k:PAR[name] + k + 1]

        def whole(name):
            which, count = jobs.whole[name]
            return (psum_full if which == "psum_full" else half_used), count

        assert RUN % RING == 0 and RING == 4 and PARTS == 4

        def part_a(l):
            return STARTS[f"experts{l}"]

        def part_g(l):
            return part_a(l) + AHEAD

        def part_b(l):
            return part_a(l) + RUN

        def part_c(l):
            return part_b(l) + 2 * (KEYS - RUN)

        def take_rounded(eng, n, half):
            p = parts[:, (2 * n + half) % PARTS, :, :]
            return eng.tensor_tensor(p[:, 1, :], ring[:, n % RING, half * HALF:(half + 1) * HALF],
                                     p[:, 0, :].bitcast(F32), ALU.subtract)

        def coef_tokens(j0, j1, i, b):
            t0 = i * (BODY * BT) + b * BT
            return coef[:, j0:j1, t0:t0 + 2 * BT] if isinstance(i, int) else coef[:, j0:j1, bass.ds(t0, 2 * BT)]

        def bank_pair(j0, j1, b):
            return ps[:, b % GB:b % GB + 2, :].rearrange("p q (t j) -> p j (q t)", t=BT)[:, j0:j1, :]

        def at_half(i, per, n, half):
            return i * (2 * per) + (2 * n + half + 1)

        @block.sync
        def _(sp):
            def load(n, src):
                if n >= RING:
                    sp.wait_ge(lo_done, 2 * (n - RING) + 2)
                sp.dma_start(ring[:, n % RING, :], src).then_inc(full[n % RING], 16)

            def load_part(name, w, first=0):
                for k in range(first, w.shape[0]):
                    load(STARTS[name] + k, w[k])

            for n in range(4):
                sp.dma_start(x[:, 2 * n:2 * n + 2, :], xT[:, 2 * n:2 * n + 2, :]).then_inc(x_in[n], 16)
            load_part("in0", w_ev_in)
            load_part("out0", w_ev_out)
            for l in range(2):
                if l == 1:
                    for k in range(RING):
                        load(STARTS["in1"] + k, w_od_in[k])
                    sp.wait_ge(acc_read, 4)
                    sp.dma_start(bias[:, 0:8, :, :], na_bias).then_inc(bias_in, 16)
                    sp.dma_start(bias[:, 8, :, :], con1).then_inc(bias_in, 16)
                    sp.dma_start(sk[:, :, :], subk[1]).then_inc(bias_in, 16)
                    load_part("in1", w_od_in, RING)
                    load_part("out1", w_od_out)
                load_part(f"q{l}", w_q[l])
                sp.wait_ge(normed, 4 + 4 * l)
                sp.dma_start(out, x[:, :, :]).then_inc(x_saved, 16)

                def experts(first, turns, order):
                    with sp.Fori(0, turns) as i:
                        for k, (table, base, step) in enumerate(order):
                            sp.wait_ge(lo_done, at_half(i, RING, first + k - RING, 1))
                            src = table[l, bass.ds(i * step + base, 1), :, :].rearrange("a p n -> p (a n)")
                            sp.dma_start(ring[:, (first + k) % RING, :], src).then_inc(full[(first + k) % RING], 16)

                experts(part_a(l), RUN // RING, [(u_t, k, RING) for k in range(RING)])
                experts(part_b(l), (KEYS - RUN) // 2, [(u_t, RUN, 2), (v_t, 0, 2), (u_t, RUN + 1, 2), (v_t, 1, 2)])
                sp.wait_ge(x_saved, 16 * (l + 1))
                sp.wait_ge(gate_full, (l + 1) * TURNS * GB)
                sp.dma_start(x[:, :, :], out).then_inc(x_back, 16)
                experts(part_c(l), RUN // RING, [(v_t, KEYS - RUN + k, RING) for k in range(RING)])
            for b in range(4):
                sp.wait_ge(acc_read, 4 + b + 1)
                sp.dma_start(out[:, 2 * b:2 * b + 2, :], x[:, 2 * b:2 * b + 2, :]).then_inc(out_done, 16)
            sp.wait_ge(out_done, 4 * 16)

        @block.gpsimd
        def _(pool):
            pool.dma_start(pa[:, :], par).then_inc(par_in, 16)
            pool.dma_start(cst[:, :], consts).then_inc(cst_in, 16)
            pool.wait_ge(x_in[3], 16)
            pool.dma_start(con0_s[:, :], con0).then_inc(con0_in, 16)
            pool.dma_start(fwo[0:HY_FILTERS, :], fw_out).then_inc(fwo_in, 16)
            pool.dma_start(sk[:, :, :], subk[0]).then_inc(sk_in, 16)

            def low_part(i, n, half):
                pool.wait_ge(hi_done, at_half(i, RING, n, half))
                take_rounded(pool, n, half).then_inc(lo_done, 1)

            def low_parts(first, end):
                turns = (end - first) // RING
                with pool.Fori(0, turns) as i:
                    for k in range(RING):
                        for half in range(2):
                            low_part(i, first + k, half)
                for n in range(first + turns * RING, end):
                    for half in range(2):
                        low_part(0, n, half)

            first = 0
            for l in range(2):
                low_parts(first, part_g(l) + 1)
                first = part_g(l) + 1
                with pool.Fori(0, TURNS // RING) as i:
                    for b in range(BODY):
                        for g in range(PLACES * b, PLACES * (b + 1)):
                            if g in ACT_PLACES:
                                continue
                            pool.wait_ge(onehots, i * (PLACES * BODY) + (l * PLACES * TURNS * GB + g + 1))
                            a = places[g % ABN][:, 0, :, :]
                            gates = gij[:, 0, bass.ds(i * (BODY * BT) + g * ABT, ABT)]
                            pool.tensor_tensor(a, a, gates.unsqueeze(2).broadcast_to([P, ABT, P]),
                                               ALU.mult).then_inc(pool_weighted, 1)
                        if b % 2 == 0:
                            low_part(i, first + b // GB, b // 2 % 2)
                for half in range(2):
                    low_part(0, part_b(l) + 1, half)
                first = part_c(l) + RUN + 2
                if l == 0:
                    pool.wait_ge(lo_done, 2 * first)

        @block.tensor
        def _(pe):
            def begin(name):
                n = jobs.number[name]
                if n >= 8:
                    pe.wait_ge(drained[jobs.who[n - 8]], jobs.rank[n - 8])

            def wait_drained(*name):
                who, count = jobs.drained(name)
                pe.wait_ge(drained[who], count)

            def mm(o, a, b, start, stop, **kw):
                return nc.tensor.matmul(o, a, b, start=start, stop=stop, **kw)

            def product(o, w, b, start, stop, **kw):
                mm(o, w[0], b[0], start, False, **kw)
                mm(o, w[0], b[1], False, False, **kw)
                return mm(o, w[1], b[0], False, stop, **kw)

            def mean_square(name, norms):
                begin(name)
                for c in range(DC):
                    if c % 2 == 0:
                        pe.wait_ge(squared, 4 * norms + c // 2 + 1)
                    last = mm(bank(name)[:, 0:T], ones_d, h[:, c, :], c == 0, c == DC - 1)
                last.then_inc(psum_full, 1)

            def project(name, transposed=True, fresh=0):
                begin(name)
                n = (jobs.whole[name][1] - 2) // 2 - 1
                for m in range(2):
                    for half in range(2):
                        k = 2 * (n + m) + half
                        pe.wait_ge(lo_done, k + 1)
                        if fresh and m == 0:
                            pe.wait_ge(rhs_lo, 2 * (fresh - 1) + half + 1)
                        w = parts[:, k % PARTS, :, :].rearrange("p s (c m) -> p s c m", m=P)
                        for c in range(4):
                            d = 4 * half + c
                            first, end = d == 0, d == DC - 1
                            wc = (w[:, 0, c, :], w[:, 1, c, :])
                            if transposed:
                                last = product(bank(name)[:, m * T:(m + 1) * T], wc,
                                               (rhs[:, 0, d, :], rhs[:, 1, d, :]), first, end)
                            else:
                                for tt in range(TT):
                                    last = product(bank(name)[:, tt * T + m * P:tt * T + (m + 1) * P],
                                                   (rhs[:, 0, d, tt * P:(tt + 1) * P],
                                                    rhs[:, 1, d, tt * P:(tt + 1) * P]), wc,
                                                   first and m == 0 and tt == 0, end, skip_group_check=True)
                        last.then_inc(half_used, 1)

            def one(name, *mms):
                begin(name)
                for o, a, b, s, e in mms:
                    last = mm(o, a, b, s, e)
                last.then_inc(psum_full, 1)

            pe.wait_ge(cst_in, 16)
            mean_square(("ms_mix", 0), 0)
            pe.wait_ge(par_in, 16)
            pe.wait_ge(con0_in, 16)

            def hidden(n):
                if n:
                    pe.wait_ge(hid_done, n)
                name = ("hidden", n)
                w = pa[0:EMB if n == 0 else HY_FILTERS, PAR["fw1"] + 64 * n:PAR["fw1"] + 64 * n + 64]
                one(name, (bank(name)[0:HY_FILTERS, 0:T], w, emb[0:EMB, :] if n == 0 else hid[0:HY_FILTERS, :],
                           True, True))

            def filters(o, tt):
                pe.wait_ge(hid_done, 3)
                pe.wait_ge(fwo_in, 16)
                for d in range(2):
                    name = ("filt", o, tt, d)
                    one(name, (bank(name), hid[0:HY_FILTERS, tt * P:(tt + 1) * P],
                               fwo[0:HY_FILTERS, (o * 2 + d) * GW:(o * 2 + d + 1) * GW], True, True))

            def filter_spectrum(o, kt):
                pe.wait_ge(filt_pm, 2 * (o + 1))
                for ri in range(2):
                    name = ("hf", o, kt, ri)
                    one(name, *((bank(name), dft[:, tt, ri * T + kt * P:ri * T + (kt + 1) * P],
                                 fpm[:, ri, tt, :], tt == 0, tt == TT - 1) for tt in range(TT)))

            def turn_input(o, tt):
                wait_drained("in0", 1) if o == 0 else wait_drained("conv", 0, 1)
                name = ("zt", o, tt)
                begin(name)
                for c in range(GC):
                    last = nc.tensor.transpose(bank(name)[:, c * P:(c + 1) * P], zc[:, c, tt * P:(tt + 1) * P],
                                               ident)
                last.then_inc(psum_full, 1)

            def input_spectrum(o, kt):
                wait_drained("zt", o, 1)
                for ri in range(2):
                    name = ("zf", o, kt, ri)
                    one(name, *((bank(name), dft[:, tt, ri * T + kt * P:ri * T + (kt + 1) * P], zt[:, tt, :],
                                 tt == 0, tt == TT - 1) for tt in range(TT)))

            def convolution(o, n):
                pe.wait_ge(yf_done, 2 * (o + 1))
                name = ("conv", o, n)
                begin(name)
                for b in range(2):
                    c = 2 * n + b
                    for r in range(4):
                        last = mm(bank(name)[:, b * T:(b + 1) * T], yf[:, r // 2, r % 2, c * P:(c + 1) * P],
                                  idft[:, r, :], r == 0, r == 3)
                last.then_inc(psum_full, 1)

            def rotate_qk(n):
                name = ("rot0", n)
                wait_drained("in0", 6 + n)
                one(name, (bank(name), rot_m, qk[:, 2 * n:2 * n + 2, :].rearrange("p a t -> p (a t)"), True, True))

            def retention_scores(hh):
                name = ("ret_s", hh)
                pe.wait_ge(roped, 4)
                o64 = 64 * (hh % 2)
                one(name, *((bank(name)[:, a * T:(a + 1) * T], qk[o64:o64 + 64, 4 + hh // 2, a * P:(a + 1) * P],
                             qk[o64:o64 + 64, hh // 2, :], True, True) for a in range(2)))

            def retention_values(n):
                name = ("ret_y", n)
                begin(name)
                wait_drained("in0", 12 + n // 2)
                for b in range(2):
                    hh = 2 * n + b
                    wait_drained("ret_s", hh)
                    for a in range(2):
                        last = mm(bank(name)[64 * b:64 * b + 64, 0:T], v0[:, a, hh * HD:(hh + 1) * HD],
                                  probs[hh][:, a, :], a == 0, a == 1)
                    last.then_inc(psum_full, 1) if b == 1 else None

            def retention_norm(n):
                name = ("ms_gn", n)
                wait_drained("ret_y", 2 * n + 1)
                one(name, (bank(name), ones_h, ysq[:, 2 * n:2 * n + 2, :].rearrange("p a t -> p (a t)"), True, True))

            for step, *at in even_order():
                if step == "in0":
                    project(("in0", at[0]), transposed=at[0] < 12, fresh=1 if at[0] == 0 else 0)
                elif step == "hidden":
                    hidden(*at)
                elif step == "filt":
                    filters(*at)
                elif step == "hf":
                    filter_spectrum(*at)
                elif step == "zt":
                    turn_input(*at)
                elif step == "zf":
                    input_spectrum(*at)
                elif step == "conv":
                    convolution(*at)
                elif step == "rot":
                    rotate_qk(*at)
                elif step == "scores":
                    retention_scores(*at)
                elif step == "values":
                    retention_values(*at)
                elif step == "gn":
                    retention_norm(*at)
            for n in range(EV_OUT):
                project(("out0", n), fresh=0 if n else 2)

            def head_norm(n):
                name = ("ms_head", n)
                wait_drained("in1", n + 2 * (n // 4))
                one(name, (bank(name), ones_h, hsq[:, 2 * n:2 * n + 2, :].rearrange("p a t -> p (a t)"), True, True))

            def rotate(n):
                name = ("rot1", n)
                pe.wait_ge(head_done, 5 + n)
                one(name, (bank(name), rot_m, hq[:, 8 + 2 * n:10 + 2 * n, :].rearrange("p a t -> p (a t)"),
                           True, True))

            def attention_scores(u):
                if u == 0:
                    pe.wait_ge(head_done, 4)
                elif u == H:
                    pe.wait_ge(roped, 8)
                g, hh = divmod(u, H)
                name = ("att_s", u)
                o64 = 64 * (hh % 2)
                one(name, *((bank(name)[:, a * T:(a + 1) * T], hq[o64:o64 + 64, 8 * g + hh // 2, a * P:(a + 1) * P],
                             hq[o64:o64 + 64, 8 * g + 4 + hh // 2, :], True, True) for a in range(2)))

            def attention_turn(u):
                name = ("att_t", u)
                begin(name)
                pe.wait_ge(p_normed, u + 1)
                for kt in range(2):
                    for a in range(2):
                        last = nc.tensor.transpose(bank(name)[:, kt * T + a * P:kt * T + (a + 1) * P],
                                                   p_att[:, u % 4, a, kt * P:(kt + 1) * P], ident)
                last.then_inc(psum_full, 1)

            def attention_values(n):
                name = ("att_o", n)
                begin(name)
                for b in range(2):
                    u = 2 * n + b
                    g, hh = divmod(u, H)
                    wait_drained("att_t", u)
                    for kt in range(2):
                        last = mm(bank(name)[64 * b:64 * b + 64, 0:T], v1[:, g, kt, hh * HD:(hh + 1) * HD],
                                  pt_att[:, u % 4, kt, :], kt == 0, kt == 1)
                    last.then_inc(psum_full, 1) if b == 1 else None

            for l in range(2):
                if l == 1:
                    mean_square(("ms_mix", 1), 2)
                    for step, k in odd_order():
                        if step == "in1":
                            project(("in1", k), transposed=k not in (4, 5, 10, 11), fresh=0 if k else 4)
                        elif step == "head":
                            head_norm(k)
                        elif step == "rot":
                            rotate(k)
                        elif step == "scores":
                            attention_scores(k)
                        elif step == "turn":
                            attention_turn(k)
                        else:
                            attention_values(k)
                    for n in range(OD_OUT):
                        project(("out1", n), fresh=0 if n else 5)

                mean_square(("ms_ffn", l), 1 + 2 * l)
                for n in range(WQ):
                    project(("q", l, n), fresh=0 if n else 3 + 3 * l)
                wait_drained("q", l, WQ - 1)
                pe.wait_ge(bias_in, 48) if l else pe.wait_ge(sk_in, 16)
                for n in range(8):
                    tt, quad, s = n // 4, n // 2 % 2, n % 2
                    name = ("sc", l, n)
                    one(name, *((bank(name)[:, k * KEYS:(k + 1) * KEYS],
                                 qT[64 * s:64 * s + 64, 4 * quad + k, tt * P:(tt + 1) * P],
                                 sk[64 * s:64 * s + 64, 4 * quad + k, :], True, True) for k in range(4)))

                def halves(i, per, n):
                    for half in range(2):
                        pe.wait_ge(lo_done, at_half(i, per, n, half))
                        w = parts[:, (2 * n + half) % PARTS, :, :].rearrange("p s (c m) -> p s c m", m=P)
                        yield half, [(w[:, 0, c, :], w[:, 1, c, :]) for c in range(4)]

                def up(i, per, n, j, step):
                    pe.wait_ge(gelu_done, i * step + (KEYS * l + j + 1))
                    for half, w in halves(i, per, n):
                        for c in range(4):
                            d = 4 * half + c
                            last = product(ps[:, 4 + j % 2, 0:T], w[c], (rhs[:, 0, d, :], rhs[:, 1, d, :]),
                                           d == 0, d == DC - 1)
                        last.then_inc(half_used, 1)

                def down(i, per, n, v, step, fresh=False):
                    pe.wait_ge(clo_done, i * step + (KEYS * l + v + 1))
                    c2 = (cparts[:, v % 2, 0, :], cparts[:, v % 2, 1, :])
                    for half, w in halves(i, per, n):
                        for c in range(4):
                            d = 4 * half + c
                            last = product(ps[:, d // 2, (d % 2) * T:(d % 2 + 1) * T], w[c], c2,
                                           fresh and d % 2 == 0, False,
                                           skip_group_check=True)
                        last.then_inc(half_used, 1)

                def up_loop(lo, hi):
                    with pe.Fori(lo, hi) as i:
                        for k in range(RING):
                            up(i, RING, part_a(l) + k, k, RING)

                wait_drained("sc", l, 6)
                wait_drained("sc", l, 7)
                up_loop(0, EARLY // RING)
                for k in range(2):
                    up(EARLY // RING, RING, part_a(l) + k, k, RING)
                pe.wait_ge(gates_done, l + 1)
                for n in range(3):
                    name = ("gt", l, n)
                    src = gs if n == 0 else ijs[:, n - 1, :]
                    for tt in range(TT):
                        last = nc.tensor.transpose(ps[:, (6 + n) % 8, tt * P:(tt + 1) * P],
                                                   src[:, tt * P:(tt + 1) * P], ident)
                    last.then_inc(psum_full, 1)
                for k in range(2, RING):
                    up(EARLY // RING, RING, part_a(l) + k, k, RING)
                wait_drained("gt", l, 2)
                with pe.Fori(0, TURNS // RING) as i:
                    for b in range(BODY):
                        k, q = divmod(b, GB)
                        pe.wait_ge(gate_free, i * BODY + (l * TURNS * GB + b + 1))
                        for g in range(PLACES * b, PLACES * (b + 1)):
                            for own, weighted in ((ACT_PLACES, act_weighted), (POOL_PLACES, pool_weighted)):
                                if g in own:
                                    pe.wait_ge(weighted, i * len(own) + (l * len(own) * TURNS // RING +
                                                                         own.index(g) + 1))
                            for t in range(ABT):
                                t0 = (g % PLACES * ABT + t) * P
                                last = mm(ps[:, q, t0:t0 + P], places[g % ABN][:, 0, t, :], places[g % ABN][:, 1, t, :],
                                          True, True)
                        last.then_inc(gate_full, 1)
                        if q == 0:
                            pe.wait_ge(gelu_done, i * RING + (KEYS * l + AHEAD + k + 1))
                        n, half = part_g(l) + k, q // 2
                        if q % 2 == 0:
                            pe.wait_ge(lo_done, at_half(i, RING, n, half))
                        w = parts[:, (2 * n + half) % PARTS, :, :].rearrange("p s (c m) -> p s c m", m=P)
                        for d in (2 * q, 2 * q + 1):
                            last = product(ps[:, 4 + k % 2, 0:T], (w[:, 0, d % 4, :], w[:, 1, d % 4, :]),
                                           (rhs[:, 0, d, :], rhs[:, 1, d, :]), d == 0, d == DC - 1)
                        if q % 2 == 1:
                            last.then_inc(half_used, 1)
                def up_down(i, k):
                    up(i, RING, part_b(l) + 2 * k, RUN + k, 2)
                    if isinstance(i, int) and k == 0:
                        pe.wait_ge(gate_free, (l + 1) * TURNS * GB + GB)
                    down(i, RING, part_b(l) + 2 * k + 1, k, 2, fresh=isinstance(i, int) and k == 0)

                for k in range(2):
                    up_down(0, k)
                with pe.Fori(1, (KEYS - RUN) // 2) as i:
                    for k in range(2):
                        up_down(i, k)
                with pe.Fori(0, RUN // RING) as i:
                    for k in range(RING):
                        down(i, RING, part_c(l) + k, KEYS - RUN + k, RING)

        @block.scalar
        def _(act):
            A = nc.scalar.activation

            def take(name):
                act.wait_ge(*whole(name))

            def wait_drained(*name):
                who, count = jobs.drained(name)
                act.wait_ge(drained[who], count)

            def round_half(i, per, n, half):
                if n >= 2:
                    act.wait_ge(half_used, at_half(i, per, n - 2, half))
                if half == 0:
                    act.wait_ge(full[n % RING], i * (16 * per // RING) + 16 * (n // RING + 1))
                A(parts[:, (2 * n + half) % PARTS, 0, :], ring[:, n % RING, half * HALF:(half + 1) * HALF],
                  ACT.Copy).then_inc(hi_done, 1)

            def stream(n, i=0, per=0):
                for half in range(2):
                    round_half(i, per, n + 2, half)

            def stream_pair(part, k):
                stream(STARTS[part] + 2 * k)
                stream(STARTS[part] + 2 * k + 1)

            def round_rhs(src, half):
                A(rhs[:, 0, 4 * half:4 * half + 4, :], src[:, 4 * half:4 * half + 4, :], ACT.Copy).then_inc(rhs_hi, 1)

            def square(n):
                if n == 3:
                    A(warm[:, :], eps[:, 0:1], ACT.Sqrt)
                A(h[:, 2 * n:2 * n + 2, :], x[:, 2 * n:2 * n + 2, :], ACT.Square).then_inc(squared, 1)

            def norm(name):
                take(name)
                A(rs[:, 0:T], bank(name)[:, 0:T], ACT.Sqrt, bias=eps[:, 0:1]).then_inc(drained["act"], 1)
                for half in range(2):
                    norms[0] += 1
                    act.wait_ge(normed, norms[0])
                    round_rhs(h, half)

            def copy(o, i, scale=1.0):
                A(o, i, ACT.Copy, scale=scale).then_inc(drained["act"], 1)

            norms = [0]
            act.sem_inc(gelu_done, 2)
            act.sem_inc(gate_free, GB)
            act.wait_ge(consts_set, 1)
            for n in range(4):
                act.wait_ge(x_in[n], 16)
                square(n)
            for n in range(2):
                for half in range(2):
                    round_half(0, 0, n, half)
            norm(("ms_mix", 0))
            act.wait_ge(par_in, 16)
            A(lgn[:, :], pa[:, PAR["decay"]:PAR["decay"] + 16], ACT.Exp).then_inc(lg_done, 1)
            for step, *at in even_order():
                n = at[-1]
                if step == "hidden":
                    act.wait_ge(hid_arg, n + 1)
                    A(hid[0:HY_FILTERS, :], harg[0:HY_FILTERS, 0, :], ACT.Sin).then_inc(hid_done, 1)
                elif step == "in0":
                    stream_pair("in0", n)
                    take(("in0", n))
                    b = bank(("in0", n))
                    if n < 6:
                        for m in range(2):
                            t = 2 * n + m
                            last = A(uc[:, t, :], b[:, m * T:(m + 1) * T], ACT.Identity,
                                     bias=par_col("conv_b", t), scale=par_col("conv_w", 12 + t))
                        last.then_inc(conv_mid, 1)
                    elif n < 10:
                        t = 2 * (n - 6)
                        copy(qk[:, t:t + 2, :].rearrange("p a t -> p (a t)"), b,
                             scale=1.0 if n < 8 else HD ** -0.5)
                    elif n < 12:
                        t = 2 * (n - 10)
                        copy(rg[:, t:t + 2, :].rearrange("p a t -> p (a t)"), b)
                    else:
                        c0 = T * (n - 12)
                        copy(v0[:, :, c0:c0 + T], b.rearrange("p (a c) -> p a c", a=2))
                elif step == "hf":
                    o, kt = at
                    for ri in range(2):
                        take(("hf", o, kt, ri))
                        copy(hf[:, o, kt, ri, :], bank(("hf", o, kt, ri)))
                elif step == "zt":
                    take(("zt", *at))
                    copy(zt[:, n, :], bank(("zt", *at)))
                elif step == "decay":
                    act.wait_ge(dec_arg, n + 1)
                    A(decs[n], decs[n], ACT.Exp, scale=-1.0).then_inc(dec_exp, 1)
                elif step == "silu":
                    wait_drained("in0", 11)
                    A(sig[:, :, :], rg[:, :, :], ACT.Exp, scale=-1.0).then_inc(silu_e, 1)
                elif step == "values":
                    take(("ret_y", n))
                    b = bank(("ret_y", n))[:, 0:T]
                    A(yr[:, n, :], b, ACT.Copy)
                    A(ysq[:, n, :], b, ACT.Square).then_inc(drained["act"], 1)
                elif step == "gn":
                    take(("ms_gn", n))
                    A(gn_root(n), bank(("ms_gn", n)), ACT.Sqrt, bias=eps[:, 0:1]).then_inc(drained["act"], 1)
            act.wait_ge(cat_done, 2)
            round_rhs(cat, 0)
            wait_drained("conv", 1, 1)
            round_rhs(cat, 1)
            for n in range(EV_OUT):
                stream_pair("out0", n)
                wait_drained("out0", n)
                square(n)

            for l in range(2):
                if l == 1:
                    for n in range(4):
                        act.wait_ge(acc_read, n + 1)
                        square(n)
                    norm(("ms_mix", 1))
                    for step, n in odd_order():
                        if step == "in1":
                            stream_pair("in1", n)
                            take(("in1", n))
                            g, k = divmod(n, 6)
                            if k < 4:
                                t = 8 * g + 2 * k
                                A(hq[:, t:t + 2, :].rearrange("p a t -> p (a t)"), bank(("in1", n)), ACT.Copy)
                                A(hsq[:, t:t + 2, :].rearrange("p a t -> p (a t)"), bank(("in1", n)),
                                  ACT.Square).then_inc(drained["act"], 1)
                            else:
                                c0 = T * (k - 4)
                                copy(v1[:, g, :, c0:c0 + T], bank(("in1", n)).rearrange("p (a c) -> p a c", a=2))
                        elif step == "head":
                            take(("ms_head", n))
                            q = n % 4 < 2
                            A(hsq[:, 2 * n:2 * n + 2, :].rearrange("p a t -> p (a t)"), bank(("ms_head", n)),
                              ACT.Sqrt, scale=float(HD) if q else 1.0,
                              bias=eps[:, 1:2] if q else eps[:, 0:1]).then_inc(drained["act"], 1)
                        elif step == "scores":
                            act.wait_ge(s_biased, n + 1)
                            for a in range(2):
                                last = A(p_att[:, n % 4, a, :], s_att[:, n % 4, a, :], ACT.Exp,
                                         bias=st_att[:, n % 8, 0, a:a + 1], accum_out=st_att[:, n % 8, 1, a:a + 1])
                            last.then_inc(s_exp, 1)
                        elif step == "turn":
                            take(("att_t", n))
                            if n >= 4:
                                act.wait_ge(*whole(("att_o", (n - 4) // 2)))
                            copy(pt_att[:, n % 4, :, :].rearrange("p a t -> p (a t)"), bank(("att_t", n)))
                        elif step == "values":
                            take(("att_o", n))
                            copy(cat1[:, n, :], bank(("att_o", n))[:, 0:T])
                    for half in range(2):
                        wait_drained("att_o", 4 * half + 3)
                        round_rhs(cat1, half)
                    for n in range(OD_OUT):
                        stream_pair("out1", n)
                        wait_drained("out1", n)
                        square(n)

                norm(("ms_ffn", l))
                for n in range(WQ):
                    stream_pair(f"q{l}", n)
                    take(("q", l, n))
                    copy(qT[:, 2 * n:2 * n + 2, :].rearrange("p a t -> p (a t)"), bank(("q", l, n)))
                for n in range(1, 8, 2):
                    take(("sc", l, n))
                    tt, quad, s = n // 4, n // 2 % 2, n % 2
                    q0 = (tt * 8 + 4 * quad) * KEYS
                    copy(sc[:, s, q0:q0 + 4 * KEYS], bank(("sc", l, n)))

                def load_gelu():
                    A(warm[:, :], eps[:, 0:1], ACT.Gelu_apprx_tanh)

                def gelus(lo, hi):
                    with act.Fori(lo, hi) as i:
                        load_gelu()
                        for k in range(RING):
                            n = part_a(l) + k
                            stream(n, i, RING)
                            act.wait_ge(half_used, at_half(i, RING, n, 1))
                            A(coef[:, bass.ds(RING * i + k, 1), :].rearrange("p a t -> p (a t)"),
                              ps[:, 4 + k % 2, 0:T], ACT.Gelu_apprx_tanh).then_inc(gelu_done, 1)

                gelus(0, EARLY // RING)
                act.wait_ge(gate_arg, l + 1)
                A(ge[:, :], ge[:, :], ACT.Exp).then_inc(gate_exp, 1)
                gelus(EARLY // RING, AHEAD // RING)

                def weight_place(i, g):
                    act.wait_ge(onehots, i * (PLACES * BODY) + (l * PLACES * TURNS * GB + g + 1))
                    for k in range(ABT):
                        t = i * (BODY * BT) + (g * ABT + k)
                        gate = gij[:, 0, t:t + 1] if isinstance(i, int) else gij[:, 0, bass.ds(t, 1)]
                        rows = places[g % ABN][:, 0, k, :]
                        last = A(rows, rows, ACT.Copy, scale=gate)
                    last.then_inc(act_weighted, 1)

                def gates_out(i, b):
                    act.wait_ge(gate_mult, i * (BODY // 2) + ((l * TURNS * GB + b) // 2 + 1))
                    A(coef_tokens(RUN, KEYS, i, b), bank_pair(RUN, KEYS, b), ACT.Copy).then_inc(gate_free, 2)

                def late_gelu(i, k):
                    act.wait_ge(half_used, at_half(i, RING, part_g(l) + k, 1))
                    act.wait_ge(coef_done, i * RING + (l * (KEYS - AHEAD) + k + 1))
                    A(gtmp[:, k % 2, :], ps[:, 4 + k % 2, 0:T], ACT.Gelu_apprx_tanh).then_inc(gelu_done, 1)

                def gates_bank(i, b):
                    peeled = isinstance(i, int)
                    k, q = divmod(b, GB)
                    for g in range(PLACES * b, PLACES * (b + 1)):
                        if g in ACT_PLACES:
                            weight_place(i, g)
                    if b % 2 == 0 and b >= 4:
                        gates_out(i, b - 4)
                    elif b % 2 == 0 and not peeled:
                        gates_out(i - 1, BODY + b - 4)
                    if q == 3:
                        round_half(i, RING, part_g(l) + k + 2, 0)
                    elif q == 1 and b >= GB:
                        round_half(i, RING, part_g(l) + k + 1, 1)
                        late_gelu(i, k - 1)
                    elif q == 1 and not peeled:
                        round_half(i, RING, part_g(l) + 1, 1)
                        late_gelu(i - 1, RING - 1)

                for b in range(BODY):
                    gates_bank(0, b)
                with act.Fori(1, TURNS // RING) as i:
                    load_gelu()
                    for b in range(BODY):
                        gates_bank(i, b)
                gates_out(TURNS // RING - 1, BODY - 4)
                gates_out(TURNS // RING - 1, BODY - 2)
                round_half(TURNS // RING - 1, RING, part_g(l) + RING + 1, 1)
                late_gelu(TURNS // RING - 1, RING - 1)

                def round_coef(i, step, v):
                    src = coef[:, i * step + v, :] if isinstance(i, int) else \
                        coef[:, bass.ds(i * step + v, 1), :].rearrange("p a t -> p (a t)")
                    A(cparts[:, v % 2, 0, :], src, ACT.Copy).then_inc(chi_done, 1)

                round_coef(0, 0, 0)
                with act.Fori(0, (KEYS - RUN) // 2) as i:
                    load_gelu()
                    for k in range(2):
                        n = part_b(l) + 2 * k
                        stream(n, i, RING)
                        act.wait_ge(coef_done, i * 2 + (l * (KEYS - AHEAD) + TURNS + k + 1))
                        A(gtmp[:, k, :], ps[:, 4 + k, 0:T], ACT.Gelu_apprx_tanh).then_inc(gelu_done, 1)
                        round_coef(i, 2, k + 1)
                        stream(n + 1, i, RING)
                act.wait_ge(coef_done, 2 + (l + 1) * (KEYS - AHEAD))

                def last_part(i, end=False):
                    for k in range(RING):
                        n = part_c(l) + k
                        if not (end and k == RING - 1):
                            act.wait_ge(half_used, at_half(i, RING, n - 1, 1))
                            round_coef(i, RING, KEYS - RUN + k + 1)
                        if not (end and k >= RING - 2 and l == 1):
                            stream(n, i, RING)

                turns = RUN // RING
                with act.Fori(0, turns - 1) as i:
                    last_part(i)
                last_part(turns - 1, end=True)

        @block.vector
        def _(dve):
            own = Chain(dve, dve_own)
            V = nc.vector

            def take(name):
                dve.wait_ge(*whole(name))

            def wait_drained(*name):
                who, count = jobs.drained(name)
                dve.wait_ge(drained[who], count)

            def drain(name, ins):
                ins.then_inc(drained["dve"], 1)
                wait_drained(*name)

            rests = [0]

            def rest_of_rhs(src, half):
                rests[0] += 1
                dve.wait_ge(rhs_hi, rests[0])
                c = slice(4 * half, 4 * half + 4)
                V.tensor_tensor(rhs[:, 1, c, :], src[:, c, :], rhs[:, 0, c, :].bitcast(F32),
                                ALU.subtract).then_inc(rhs_lo, 1)

            def norm(gain, l, *name):
                wait_drained(*name)
                own.link(V.reciprocal(rs[:, T:2 * T], rs[:, 0:T]))
                for c in range(DC):
                    last = V.scalar_tensor_tensor(out=h[:, c, :], in0=x[:, c, :], scalar=par_col(gain, l * DC + c),
                                                  in1=rs[:, T:2 * T], op0=ALU.mult, op1=ALU.mult)
                    if c % 4 == 3:
                        last.then_inc(normed, 1)
                for half in range(2):
                    rest_of_rhs(h, half)

            V.memset(eps[:, 0:1], EPS)
            V.memset(eps[:, 1:2], EPS * HD).then_inc(consts_set, 1)
            dve.sem_inc(coef_done, 2)
            dve.wait_ge(par_in, 16)
            norm("mix_gain", 0, "ms_mix", 0)
            TWO_PI_HI, TWO_PI_LO, MAGIC = 6.28125, 0.0019353071795864769, 12582912.0
            F = HY_FILTERS

            def sine_argument(n):
                take(("hidden", n))
                if n:
                    dve.wait_ge(hid_done, n)
                a, r = harg[0:F, 0, :], harg[0:F, 1, :]
                drain(("hidden", n), V.tensor_scalar(a, bank(("hidden", n))[0:F, 0:T], par_col("fb", n, F),
                                                     par_col("freq", 0, F), ALU.add, ALU.mult))
                own.link(V.tensor_scalar(r, a, 0.15915494309189535, MAGIC, ALU.mult, ALU.add))
                own.link(V.tensor_scalar(r, r, -MAGIC, None, ALU.add))
                own.link(V.scalar_tensor_tensor(out=a, in0=r, scalar=-TWO_PI_HI, in1=a, op0=ALU.mult, op1=ALU.add))
                own.link(V.scalar_tensor_tensor(out=a, in0=r, scalar=-TWO_PI_LO, in1=a, op0=ALU.mult, op1=ALU.add))
                V.tensor_scalar(a, a, 3.1415925, -3.1415925, ALU.min, ALU.max).then_inc(hid_arg, 1)

            def outer_taps(it):
                dve.wait_ge(conv_mid, it + 1)
                for m in range(2):
                    t = 2 * it + m
                    b = bank(("in0", it))[:, m * T:(m + 1) * T]
                    own.link(V.scalar_tensor_tensor(out=uc[:, t, 1:T], in0=b[:, 0:T - 1],
                                                    scalar=par_col("conv_w", t), in1=uc[:, t, 1:T],
                                                    op0=ALU.mult, op1=ALU.add))
                    ins = V.scalar_tensor_tensor(out=uc[:, t, 0:T - 1], in0=b[:, 1:T],
                                                 scalar=par_col("conv_w", 24 + t), in1=uc[:, t, 0:T - 1],
                                                 op0=ALU.mult, op1=ALU.add)
                ins.then_inc(drained["dve"], 1)

            def window(o, tt):
                if o == 0:
                    dve.wait_ge(con0_in, 16)
                elif tt == 0:
                    dve.wait_ge(*whole(("hf", 0, 1, 1)))
                take(("filt", o, tt, 1))
                dve.drain()
                f, b = bank(("filt", o, tt, 0)), bank(("filt", o, tt, 1))
                drain(("filt", o, tt, 0), V.tensor_tensor(tmp[:, 0, :], f, win[:, tt, 0, :], ALU.mult))
                drain(("filt", o, tt, 1), V.tensor_tensor(tmp[:, 1, :], b, win[:, tt, 1, :], ALU.mult))
                V.tensor_tensor(fpm[:, 0, tt, :], tmp[:, 0, :], tmp[:, 1, :], ALU.add)
                V.tensor_tensor(fpm[:, 1, tt, :], tmp[:, 0, :], tmp[:, 1, :], ALU.subtract).then_inc(filt_pm, 1)

            def filter_input(o, kt):
                wait_drained("hf", o, kt, 1)
                take(("zf", o, kt, 1))
                dve.drain()
                zr, zi = bank(("zf", o, kt, 0)), bank(("zf", o, kt, 1))
                hr, hi = hf[:, o, kt, 0, :], hf[:, o, kt, 1, :]
                if o == 1 and kt == 0:
                    dve.wait_ge(*whole(("conv", 0, 1)))
                V.tensor_tensor(yf[:, kt, 0, :], zr, hr, ALU.mult)
                own.link(V.tensor_tensor(tmp[:, 0, :], zi, hi, ALU.mult))
                V.tensor_tensor(yf[:, kt, 0, :], yf[:, kt, 0, :], tmp[:, 0, :], ALU.subtract)
                V.tensor_tensor(yf[:, kt, 1, :], zr, hi, ALU.mult)
                own.link(V.tensor_tensor(tmp[:, 1, :], zi, hr, ALU.mult))
                dve.sem_inc(drained["dve"], 2)
                V.tensor_tensor(yf[:, kt, 1, :], yf[:, kt, 1, :], tmp[:, 1, :], ALU.add).then_inc(yf_done, 1)

            def skip_and_gate(o, n):
                take(("conv", o, n))
                dve.drain()
                for b in range(2):
                    c = 2 * n + b
                    z = zc[:, c, :]
                    own.link(V.scalar_tensor_tensor(out=tmp[:, b, 0:T], in0=z, scalar=par_col("skip", 4 * o + c),
                                                    in1=bank(("conv", o, n))[:, b * T:(b + 1) * T],
                                                    op0=ALU.mult, op1=ALU.add))
                    last = V.tensor_tensor(z if o == 0 else cat[:, GC + c, :], tmp[:, b, 0:T], uc[:, 4 + 4 * o + c, :],
                                           ALU.mult)
                last.then_inc(drained["dve"], 1)

            ropes = [0]

            def rope(name, tiles, scratch):
                take(name)
                dve.drain()
                t3 = scratch.rearrange("p (a t) -> p a t", a=2)
                sin2 = sin_t.unsqueeze(1).broadcast_to([P, 2, T])
                cos2 = cos_t.unsqueeze(1).broadcast_to([P, 2, T])
                drain(name, V.tensor_tensor(t3, bank(name).rearrange("p (a t) -> p a t", a=2), sin2, ALU.mult))
                own.link(V.tensor_tensor(tiles, tiles, cos2, ALU.mult))
                V.tensor_tensor(tiles, tiles, t3, ALU.add).then_inc(roped, 1)
                ropes[0] += 1
                dve.wait_ge(roped, ropes[0])

            def decay_arg(hh):
                if hh == 0:
                    wait_drained("filt", 1, 1, 1)
                    dve.wait_ge(lg_done, 1)
                d = decs[hh]
                own.link(V.tensor_scalar(d, dist[:, 0, :, :].rearrange("p a t -> p (a t)"),
                                         lgn[:, hh:hh + 1], None, ALU.mult))
                V.scalar_tensor_tensor(out=d, in0=dist[:, 1, :, :].rearrange("p a t -> p (a t)"),
                                       scalar=lgn[:, 8 + hh:9 + hh], in1=d, op0=ALU.mult,
                                       op1=ALU.add).then_inc(dec_arg, 1)

            def decayed(hh):
                take(("ret_s", hh))
                dve.wait_ge(dec_exp, hh + 1)
                V.tensor_tensor(probs[hh].rearrange("p a t -> p (a t)"), bank(("ret_s", hh)), decs[hh],
                                ALU.mult).then_inc(drained["dve"], 1)

            def gated_norm(n):
                wait_drained("ret_y", 2 * n + 1)
                two = slice(2 * n, 2 * n + 2)
                for c in (2 * n, 2 * n + 1):
                    V.scalar_tensor_tensor(out=yr[:, c, :], in0=yr[:, c, :], scalar=par_col("gn", c), in1=rg[:, c, :],
                                           op0=ALU.mult, op1=ALU.mult)
                dve.wait_ge(silu_e, 1)
                wait_drained("ms_gn", n)
                root = gn_root(n).rearrange("p (a t) -> p a t", a=2)
                own.link(V.scalar_tensor_tensor(out=root, in0=sig[:, two, :], scalar=1.0, in1=root, op0=ALU.add,
                                                op1=ALU.mult))
                own.link(V.reciprocal(root, root))
                V.tensor_tensor(cat[:, two, :], yr[:, two, :], root, ALU.mult).then_inc(cat_done, 1)

            for step, *at in even_order():
                if step == "hidden":
                    sine_argument(*at)
                elif step == "in0":
                    if at[0] < 6:
                        outer_taps(*at)
                elif step == "filt":
                    window(*at)
                elif step == "zf":
                    filter_input(*at)
                elif step == "conv":
                    skip_and_gate(*at)
                elif step == "rot":
                    rope(("rot0", at[0]), qk[:, 2 * at[0]:2 * at[0] + 2, :], tmp[:, 0, :])
                elif step == "decay":
                    decay_arg(*at)
                elif step == "scores":
                    decayed(*at)
                elif step == "gn":
                    gated_norm(*at)
            for half in range(2):
                rest_of_rhs(cat, half)

            def residual(name, n):
                take(name)
                drain(name, V.tensor_tensor(x[:, 2 * n:2 * n + 2, :], x[:, 2 * n:2 * n + 2, :],
                                      bank(name).rearrange("p (a t) -> p a t", a=2), ALU.add))

            for n in range(EV_OUT):
                residual(("out0", n), n)

            for l in range(2):
                if l == 1:
                    norm("mix_gain", 1, "ms_mix", 1)

                    def normalise(u):
                        dve.wait_ge(s_exp, u + 1)
                        own.link(V.reciprocal(st_att[:, u % 8, 2, :], st_att[:, u % 8, 1, :]))
                        for a in range(2):
                            last = V.tensor_scalar(p_att[:, u % 4, a, :], p_att[:, u % 4, a, :],
                                                   st_att[:, u % 8, 2, a:a + 1], None, ALU.mult)
                        last.then_inc(p_normed, 1)

                    for step, n in odd_order():
                        if step == "head":
                            wait_drained("ms_head", n)
                            inv = hsq[:, 2 * n:2 * n + 2, :]
                            own.link(V.reciprocal(inv, inv))
                            g = par_col("na_gain" if n < 4 else "dil_gain", n % 4 // 2)
                            tiles = hq[:, 2 * n:2 * n + 2, :]
                            V.scalar_tensor_tensor(out=tiles, in0=tiles, scalar=g, in1=inv, op0=ALU.mult,
                                                   op1=ALU.mult).then_inc(head_done, 1)
                        elif step == "rot":
                            dve.wait_ge(head_done, 5 + n)
                            rope(("rot1", n), hq[:, 8 + 2 * n:10 + 2 * n, :], turned)
                        elif step == "scores":
                            g, hh = divmod(n, H)
                            if n == 0:
                                dve.wait_ge(bias_in, 48)
                            take(("att_s", n))
                            b = bias[:, hh if g == 0 else 8, :, :]
                            drain(("att_s", n), V.tensor_tensor(
                                s_att[:, n % 4, :, :], bank(("att_s", n)).rearrange("p (a t) -> p a t", a=2), b,
                                ALU.add))
                            V.tensor_reduce(st_att[:, n % 8, 0, :], s_att[:, n % 4, :, :], AX.X, ALU.max,
                                            negate=True).then_inc(s_biased, 1)
                            if n:
                                normalise(n - 1)
                    normalise(UNITS - 1)
                    for half in range(2):
                        rest_of_rhs(cat1, half)
                    for n in range(OD_OUT):
                        residual(("out1", n), n)

                norm("ffn_gain", l, "ms_ffn", l)
                V.memset(coef[:, AHEAD:RUN, :], 1.0)
                for n in range(0, 8, 2):
                    take(("sc", l, n))
                    tt, quad = n // 4, n // 2 % 2
                    q0 = (tt * 8 + 4 * quad) * KEYS
                    drain(("sc", l, n), V.tensor_copy(sc[:, 0, q0:q0 + 4 * KEYS], bank(("sc", l, n))))
                wait_drained("sc", l, 7)

                with dve.Fori(0, 8) as i:
                    own.enter(i, 6)
                    V.tensor_copy(cur.rearrange("p s e c -> p s (e c)"), sc[:, :, bass.ds(i * 2 * KEYS, 2 * KEYS)])
                    dve.drain()

                    def top16(lists):
                        for values, rest, best, index in lists:
                            V.max(best[:, 0:8], values)
                        dve.drain()
                        for values, rest, best, index in lists:
                            V.max_index(index[:, 0:8], best[:, 0:8], values)
                        for values, rest, best, index in lists:
                            V.match_replace(rest, best[:, 0:8], values, -3.0e38)
                        dve.drain()
                        for values, rest, best, index in lists:
                            V.max(best[:, 8:16], rest)
                        dve.drain()
                        for values, rest, best, index in lists:
                            last = V.max_index(index[:, 8:16], best[:, 8:16], rest)
                        return last

                    own.link(top16([(cur[:, s, e, :], cut[:, s, e, :], top_s[:, s, e, :], top_i[:, s, e, :])
                                    for s in range(2) for e in range(2)]))
                    V.tensor_copy(top_f.rearrange("p s e c -> p (s e c)"), top_i.rearrange("p s e c -> p (s e c)"))
                    for e in range(2):
                        V.tensor_tensor(cand[:, e, :].rearrange("p (a b) -> p a b", a=16),
                                        top_s[:, 0, e, :].unsqueeze(2).broadcast_to([P, 16, 16]),
                                        top_s[:, 1, e, :].unsqueeze(1).broadcast_to([P, 16, 16]), ALU.add)
                    dve.drain()
                    own.link(top16([(cand[:, e, :], cand2[:, e, :], g16[:, e, :], pick[:, e, :]) for e in range(2)]))
                    V.tensor_copy(gs[:, bass.ds(i * 32, 32)], g16.rearrange("p e c -> p (e c)"))
                    pick2 = pick.rearrange("p e c -> p (e c)")
                    V.tensor_scalar(pab[:, 0, :], pick2, 4, None, ALU.logical_shift_right)
                    own.link(V.tensor_scalar(pab[:, 1, :], pick2, 15, None, ALU.bitwise_and))
                    own.link(V.tensor_copy(pabf[:, :, :], pab[:, :, :]))
                    for s in range(2):
                        last = V.tensor_tensor(look[:, s, :, :, :].rearrange("p e k a -> p (e k) a"),
                                               iota[:, 0:16].unsqueeze(1).broadcast_to([P, 32, 16]),
                                               pabf[:, s, :].unsqueeze(2).broadcast_to([P, 32, 16]), ALU.is_equal)
                    own.link(last)
                    for s in range(2):
                        last = V.tensor_tensor(look[:, s, :, :, :], look[:, s, :, :, :],
                                               top_f[:, s, :, :].unsqueeze(2).broadcast_to([P, 2, 16, 16]), ALU.mult)
                    own.link(last)
                    V.tensor_reduce(ijs[:, :, bass.ds(i * 32, 32)],
                                    look.rearrange("p s e k a -> p s (e k) a"), AX.X, ALU.add)
                    dve.drain()
                own.leave(8)

                g3 = gs.rearrange("p (q k) -> p q k", k=16)
                e3 = ge.rearrange("p (q k) -> p q k", k=16)
                V.tensor_tensor(e3, g3, g3[:, :, 0:1].broadcast_to([P, 16, 16]), ALU.subtract).then_inc(gate_arg, 1)
                dve.wait_ge(gate_exp, l + 1)
                own.link(V.tensor_reduce(gsum, e3, AX.X, ALU.add))
                own.link(V.reciprocal(gsum, gsum))
                own.link(V.tensor_tensor(g3, e3, gsum.unsqueeze(2).broadcast_to([P, 16, 16]), ALU.mult))
                dve.sem_inc(gates_done, 1)
                for n in range(3):
                    take(("gt", l, n))
                    drain(("gt", l, n), V.tensor_copy(gij[:, n, :], ps[:, (6 + n) % 8, 0:T]))

                own.link(V.tensor_copy(ps[:, 6, 0:P], iota))

                def onehot_rows(i, g):
                    t0 = i * (BODY * BT) + g * ABT
                    pick = gij[:, 1:3, t0:t0 + ABT] if isinstance(i, int) else gij[:, 1:3, bass.ds(t0, ABT)]
                    V.tensor_tensor(places[g % ABN],
                                    ps[:, 6, 0:P].unsqueeze(1).unsqueeze(1).broadcast_to([P, 2, ABT, P]),
                                    pick.unsqueeze(3).broadcast_to([P, 2, ABT, P]), ALU.is_equal).then_inc(onehots, 1)

                def gate_tiles(i, b):
                    c = coef_tokens(0, RUN, i, b)
                    V.tensor_tensor(c, c, bank_pair(0, RUN, b), ALU.mult).then_inc(gate_mult, 1)

                def late_tile(i, k, gated):
                    dve.wait_ge(gelu_done, i * RING + (2 + l * KEYS + AHEAD + k + 1))
                    dve.wait_ge(gate_mult, i * (BODY // 2) + (l * TURNS * GB + gated) // 2)
                    c = coef[:, AHEAD + i * RING + k, :] if isinstance(i, int) else \
                        coef[:, bass.ds(i * RING + (AHEAD + k), 1), :].rearrange("p a t -> p (a t)")
                    V.tensor_tensor(c, c, gtmp[:, k % 2, :], ALU.mult).then_inc(coef_done, 1)
                    dve.wait_ge(coef_done, i * RING + (2 + l * (KEYS - AHEAD) + k + 1))

                def gate_bank(i, b):
                    peeled = isinstance(i, int)
                    if not (peeled and b < 4):
                        dve.wait_ge(gate_full, i * BODY + (l * TURNS * GB + b - 3))
                    for g in range(PLACES * b, PLACES * (b + 1)):
                        onehot_rows(i, g)
                    if b % 2 == 0 and not (peeled and b < 4):
                        dve.wait_ge(gate_full, i * BODY + (l * TURNS * GB + b - 2))
                    if peeled and b == 4:
                        dve.wait_ge(gelu_done, 2 + l * KEYS + AHEAD)
                    if b % 2 == 0 and b >= 4:
                        gate_tiles(i, b - 4)
                    elif b % 2 == 0 and not peeled:
                        gate_tiles(i - 1, BODY + b - 4)
                    if b % GB == GB - 1:
                        if b >= GB:
                            late_tile(i, b // GB - 1, b - 3)
                        elif not peeled:
                            late_tile(i - 1, RING - 1, BODY + b - 3)

                dve.wait_ge(x_saved, 16 * (l + 1))
                for b in range(BODY):
                    gate_bank(0, b)
                with dve.Fori(1, TURNS // RING) as i:
                    for b in range(BODY):
                        gate_bank(i, b)
                dve.wait_ge(gate_full, (l + 1) * TURNS * GB)
                gate_tiles(TURNS // RING - 1, BODY - 4)
                gate_tiles(TURNS // RING - 1, BODY - 2)
                late_tile(TURNS // RING - 1, RING - 1, BODY)

                def rest_of_coef(i, step, v):
                    src = coef[:, i * step + v, :] if isinstance(i, int) else \
                        coef[:, bass.ds(i * step + v, 1), :].rearrange("p a t -> p (a t)")
                    dve.wait_ge(chi_done, i * step + (KEYS * l + v + 1))
                    V.tensor_tensor(cparts[:, v % 2, 1, :], src, cparts[:, v % 2, 0, :].bitcast(F32),
                                    ALU.subtract).then_inc(clo_done, 1)

                def low_parts(i, n):
                    for half in range(2):
                        dve.wait_ge(hi_done, at_half(i, RING, n, half))
                        take_rounded(dve, n, half).then_inc(lo_done, 1)

                dve.wait_ge(lo_done, 2 * (part_b(l) + 2))
                rest_of_coef(0, 0, 0)
                with dve.Fori(0, (KEYS - RUN) // 2) as i:
                    for k in range(2):
                        low_parts(i, part_b(l) + 2 * k + 2)
                        dve.wait_ge(gelu_done, i * 2 + (2 + l * KEYS + RUN + k + 1))
                        c = coef[:, bass.ds(2 * i + (RUN + k), 1), :].rearrange("p a t -> p (a t)")
                        V.tensor_tensor(c, c, gtmp[:, k, :], ALU.mult).then_inc(coef_done, 1)
                        rest_of_coef(i, 2, k + 1)
                        low_parts(i, part_b(l) + 2 * k + 3)
                turns = RUN // RING
                with dve.Fori(0, turns - 1) as i:
                    for k in range(RING):
                        rest_of_coef(i, RING, KEYS - RUN + k + 1)
                        low_parts(i, part_c(l) + k + 2)
                for k in range(RING):
                    if k < RING - 1:
                        rest_of_coef(turns - 1, RING, KEYS - RUN + k + 1)
                    if k < RING - 2 or l == 0:
                        low_parts(turns - 1, part_c(l) + k + 2)
                dve.wait_ge(half_used, 2 * (part_c(l) + RUN))
                dve.wait_ge(x_back, 16 * (l + 1))
                for b in range(4):
                    V.tensor_tensor(x[:, 2 * b:2 * b + 2, :], x[:, 2 * b:2 * b + 2, :],
                                    ps[:, b, :].rearrange("p (a t) -> p a t", a=2), ALU.add).then_inc(acc_read, 1)
                dve.wait_ge(acc_read, 4 * (l + 1))




def _constants():
    import numpy as np

    f = np.float32
    t = np.arange(T)
    inv = (10000.0 ** (-np.arange(0, HD, 2, dtype=f) / HD)).astype(f)
    ang = (t.astype(f)[:, None] * inv[None, :]).astype(f)
    cos = np.tile(np.cos(ang).T, (4, 1))
    sin = np.tile(np.sin(ang).T, (4, 1))
    rot = np.zeros((P, P))
    for b in (0, HD):
        for k in range(HD // 2):
            rot[b + HD // 2 + k, b + k] = -1.0
            rot[b + k, b + HD // 2 + k] = 1.0
    same_head = np.kron(np.eye(2), np.full((HD, HD), 1.0 / HD))
    consts = np.concatenate([np.eye(P), rot, np.full((P, P), 1.0 / D), same_head,
                             np.tile(np.arange(P), (P, 1)), cos, sin], axis=1)
    bands = (EMB - 1) // 2
    t_norm = np.linspace(0.0, 1.0, T, dtype=f)[:, None]
    w = (2.0 * np.pi * np.arange(T, dtype=f)[:, None] / T).astype(f)
    fb = np.linspace(1e-4, bands - 1, bands, dtype=f)[None, :]
    e = np.concatenate([t_norm, np.cos(fb * w), -np.sin(fb * w)], axis=-1)
    emb = np.zeros((P, T))
    emb[:EMB] = e.T
    lo, hi = np.log(1e-2) / 1.5, np.log(1e-2) / 0.3
    deltas = np.abs(np.linspace(lo, hi, GW, dtype=f))
    win = np.exp(-t_norm * deltas[None, :]) + 0.05
    win_b = win.copy()
    win_b[0] = 0.0
    ph = np.pi * np.outer(t, 2 * t + 1) / (2 * T)
    dft = np.concatenate([np.cos(ph), -np.sin(ph)], axis=1)
    idft = np.stack([np.cos(ph).T, -np.sin(ph).T]) / T
    dft_s = dft.reshape(TT, P, 2 * T).transpose(1, 0, 2).reshape(P, -1)
    idft_s = idft.reshape(2, 2, P, T).transpose(2, 1, 0, 3).reshape(P, -1)
    win_s = np.stack([win, win_b]).reshape(2, TT, P, GW).transpose(2, 1, 0, 3).reshape(P, -1)
    m = np.arange(T).reshape(TT, P)
    ahead = np.maximum(t[None, None, :] - m[:, :, None], 0)
    behind = np.maximum(m[:, :, None] - t[None, None, :], 0)
    dist = np.stack([ahead, behind]).transpose(2, 0, 1, 3).reshape(P, -1)
    con0 = np.concatenate([emb, dft_s, idft_s, win_s, dist], axis=1)
    q, k = t[:, None], t[None, :]
    seen = np.zeros((T, T))
    for window, dil in ((128, 1), (512, 4), (2048, 16)):
        seen += (q % dil == k % dil) & (np.abs(q // dil - k // dil) <= window // (2 * dil))
    merged = np.where(seen > 0, np.log(np.maximum(seen, 1)), NEG)
    con1 = merged.reshape(TT, P, T).transpose(1, 0, 2)
    return [np.ascontiguousarray(a, dtype=f) for a in (consts, con0, con1)]


def kernel(**inputs):
    import numpy as np
    import concourse.bacc as bacc
    from concourse.bass_utils import run_bass_kernel_spmd as run

    a = {k: np.asarray(v) for k, v in inputs.items()}

    def chunks(v):
        return np.ascontiguousarray(v.reshape(-1, P).T)

    def tiles(w):
        n = w.shape[1] // P
        return np.ascontiguousarray(w.reshape(DC, P, n, P).transpose(2, 1, 0, 3).reshape(n, P, TILE))

    def rows(v):
        out = np.zeros((P, v.shape[1]), v.dtype)
        out[:v.shape[0]] = v
        return out

    def twice(v):
        return np.concatenate([v.T, v.T], axis=0)

    par = np.concatenate([
        chunks(a["mix_norm_gain"]), chunks(a["ffn_norm_gain"]), chunks(a["hy_conv_w"][0]), chunks(a["hy_conv_b"][0]),
        chunks(a["hy_skip"][0]), chunks(a["ret_gn_gain"][0]), twice(a["na_qk_gain"][0]), twice(a["dil_qk_gain"][0]),
        rows(np.stack([a["hy_fb1"][0], a["hy_fb2"][0], a["hy_fb3"][0], a["hy_freq"][0]], axis=1)),
        np.tile(a["ret_log_decay"][0].reshape(1, 16), (P, 1)),
        rows(a["hy_fw1"][0]), rows(a["hy_fw2"][0]), rows(a["hy_fw3"][0])], axis=1)
    assert par.shape[1] == NPAR
    consts, con0, con1 = _constants()

    rows_, cols = T // 64, 64
    r, c = np.arange(rows_), np.arange(cols)
    c0 = np.clip(c - 8, 0, cols - 16)
    valid = (c[None, :] >= c0[:, None]) & (c[None, :] < c0[:, None] + 16)
    row_off = r[None, :] - r[:, None] + 7
    col_off = np.clip(c[None, :] - c[:, None] + 15, 0, 30)
    b = a["na_rpb"][0][:, row_off[:, None, :, None], col_off[None, :, None, :]]
    b = np.where(valid[None, None, :, None, :], b, np.float32(NEG)).reshape(8, TT, P, T)
    na_bias = np.ascontiguousarray(b.transpose(2, 0, 1, 3))

    w_in = a["ev_w_in"][0]
    w_out = np.roll(a["ev_w_out"][0], GW, axis=0)
    ev = tiles(w_in)[[*range(20), *range(24, 28), *range(20, 24)]]
    subk = np.ascontiguousarray(a["peer_sub_keys"].transpose(0, 2, 4, 1, 3).reshape(2, P, 8, KEYS))
    u_t = a["peer_u"].reshape(2, KEYS, KEYS, DC, P).transpose(0, 2, 4, 3, 1).reshape(2, KEYS, P, TILE)
    v_t = a["peer_v"].reshape(2, KEYS, KEYS, D).transpose(0, 2, 1, 3)
    arrays = {
        "xT": a["x"][0].T.reshape(DC, P, T).transpose(1, 0, 2), "par": par, "consts": consts, "con0": con0,
        "con1": con1, "subk": subk, "w_ev_in": ev, "w_ev_out": tiles(w_out),
        "w_od_in": tiles(a["od_w_in"][0]), "w_od_out": tiles(a["od_w_out"][0]),
        "w_q": np.stack([tiles(a["peer_w_q"][0]), tiles(a["peer_w_q"][1])]), "fw_out": a["hy_fw_out"][0],
        "na_bias": na_bias, "u_t": u_t, "v_t": v_t,
    }
    nc = bacc.Bacc("TRN2", target_bir_lowering=False, num_devices=1)
    args = {}
    for name, v in arrays.items():
        arrays[name] = np.ascontiguousarray(v)
        args[name] = nc.dram_tensor(name, v.shape, F32, kind="ExternalInput").ap()
    out = nc.dram_tensor("out", (P, DC, T), F32, kind="ExternalOutput").ap()
    hybrid_trunk(nc, out=out, **args)
    got = run(nc, [arrays], core_ids=[0]).results[0]["out"]
    return np.ascontiguousarray(got.transpose(1, 0, 2).reshape(D, T).T)[None]
```
